# Optimizing a Trainium2 kernel written in Bass

```python
import jax
import jax.numpy as jnp
from jax import lax
import numpy as np
import jax, jax.numpy as jnp

D_MODEL = 1024
BATCH = 1
SEQ = 512
DEPTH = 1

HEAD_DIM = 64
N_SB_HEADS = 8
N_FOX_HEADS = 8
SB_WIDTH = N_SB_HEADS * HEAD_DIM
FOX_WIDTH = N_FOX_HEADS * HEAD_DIM
MIX_WIDTH = SB_WIDTH + FOX_WIDTH
IN_WIDTH = 3 * SB_WIDTH + 3 * FOX_WIDTH + N_FOX_HEADS
D_FF = 2816
BLOCK_Q = 128
N_MOD = 9
EPS = 1e-6


def rms_norm(x, gain):
    xf = x.astype(jnp.float32)
    y = xf * lax.rsqrt(jnp.mean(xf * xf, axis=-1, keepdims=True) + EPS)
    return (y * gain.astype(jnp.float32)).astype(x.dtype)

def modulate(h, shift, scale):
    return h * (1 + scale[:, None, :]) + shift[:, None, :]

def swiglu(h, w_gate, w_up, w_down):
    return (jax.nn.silu(h @ w_gate) * (h @ w_up)) @ w_down

def split_heads(t, n_heads):
    b, s, _ = t.shape
    return t.reshape(b, s, n_heads, HEAD_DIM).transpose(0, 2, 1, 3)

def stick_breaking_attention(q, k, v):
    seq = q.shape[2]
    scale = HEAD_DIM ** -0.5
    outs = []
    for start in range(0, seq, BLOCK_Q):
        end = start + BLOCK_Q
        z = jnp.einsum('bhqd,bhkd->bhqk', q[:, :, start:end], k[:, :, :end]).astype(jnp.float32) * scale
        mask = jnp.arange(end)[None, :] < jnp.arange(start, end)[:, None]
        log_beta = jax.nn.log_sigmoid(z)
        log_keep = jnp.where(mask, jax.nn.log_sigmoid(-z), 0.0)
        later = lax.cumsum(log_keep, axis=3, reverse=True) - log_keep
        w = jnp.where(mask, jnp.exp(log_beta + later), 0.0)
        outs.append(jnp.einsum('bhqk,bhkd->bhqd', w.astype(v.dtype), v[:, :, :end]))
    return jnp.concatenate(outs, axis=2)

def forgetting_attention(q, k, v, log_f_cum):
    seq = q.shape[2]
    scale = HEAD_DIM ** -0.5
    outs = []
    for start in range(0, seq, BLOCK_Q):
        end = start + BLOCK_Q
        z = jnp.einsum('bhqd,bhkd->bhqk', q[:, :, start:end], k[:, :, :end]).astype(jnp.float32) * scale
        z = z + log_f_cum[:, :, start:end, None] - log_f_cum[:, :, None, :end]
        mask = jnp.arange(end)[None, :] <= jnp.arange(start, end)[:, None]
        p = jax.nn.softmax(jnp.where(mask, z, -jnp.inf), axis=-1)
        outs.append(jnp.einsum('bhqk,bhkd->bhqd', p.astype(v.dtype), v[:, :, :end]))
    return jnp.concatenate(outs, axis=2)

def hybrid_mixer(h, w_in, b_f, g_q, g_k, w_o):
    proj = h @ w_in
    splits = [SB_WIDTH, 2 * SB_WIDTH, 3 * SB_WIDTH,
              3 * SB_WIDTH + FOX_WIDTH, 3 * SB_WIDTH + 2 * FOX_WIDTH, 3 * SB_WIDTH + 3 * FOX_WIDTH]
    sb_q, sb_k, sb_v, fox_q, fox_k, fox_v, fox_f = jnp.split(proj, splits, axis=-1)
    sb_out = stick_breaking_attention(split_heads(sb_q, N_SB_HEADS), split_heads(sb_k, N_SB_HEADS),
                                      split_heads(sb_v, N_SB_HEADS))
    fq = rms_norm(split_heads(fox_q, N_FOX_HEADS), g_q[None, :, None, :])
    fk = rms_norm(split_heads(fox_k, N_FOX_HEADS), g_k[None, :, None, :])
    log_f = jax.nn.log_sigmoid((fox_f + b_f).astype(jnp.float32))
    log_f_cum = jnp.cumsum(log_f, axis=1).transpose(0, 2, 1)
    fox_out = forgetting_attention(fq, fk, split_heads(fox_v, N_FOX_HEADS), log_f_cum)
    heads = jnp.concatenate([sb_out, fox_out], axis=1)
    b, _, s, _ = heads.shape
    return heads.transpose(0, 2, 1, 3).reshape(b, s, MIX_WIDTH) @ w_o

def first_inputs(seed: int = 0) -> dict:
    key = jax.random.key(seed)
    ks = jax.random.split(key, 20)
    nrm = jax.random.normal
    d_s = D_MODEL ** -0.5
    return {
        'x': nrm(ks[0], (BATCH, SEQ, D_MODEL), jnp.float32),
        'c': nrm(ks[1], (BATCH, D_MODEL), jnp.float32),
        'w_mod': nrm(ks[2], (DEPTH, D_MODEL, N_MOD * D_MODEL), jnp.float32) * (0.1 * d_s),
        'b_mod': nrm(ks[3], (DEPTH, N_MOD * D_MODEL), jnp.float32) * 0.01,
        'g_ffn1': 1.0 + 0.02 * nrm(ks[4], (DEPTH, D_MODEL), jnp.float32),
        'w1_gate': nrm(ks[5], (DEPTH, D_MODEL, D_FF), jnp.float32) * d_s,
        'w1_up': nrm(ks[6], (DEPTH, D_MODEL, D_FF), jnp.float32) * d_s,
        'w1_down': nrm(ks[7], (DEPTH, D_FF, D_MODEL), jnp.float32) * D_FF ** -0.5,
        'g_mix': 1.0 + 0.02 * nrm(ks[8], (DEPTH, D_MODEL), jnp.float32),
        'w_in': nrm(ks[9], (DEPTH, D_MODEL, IN_WIDTH), jnp.float32) * d_s,
        'b_f': jax.random.uniform(ks[10], (DEPTH, N_FOX_HEADS), jnp.float32, 1.0, 4.0),
        'g_q': 1.0 + 0.02 * nrm(ks[11], (DEPTH, N_FOX_HEADS, HEAD_DIM), jnp.float32),
        'g_k': 1.0 + 0.02 * nrm(ks[12], (DEPTH, N_FOX_HEADS, HEAD_DIM), jnp.float32),
        'w_o': nrm(ks[13], (DEPTH, MIX_WIDTH, D_MODEL), jnp.float32) * MIX_WIDTH ** -0.5,
        'g_ffn2': 1.0 + 0.02 * nrm(ks[14], (DEPTH, D_MODEL), jnp.float32),
        'w2_gate': nrm(ks[15], (DEPTH, D_MODEL, D_FF), jnp.float32) * d_s,
        'w2_up': nrm(ks[16], (DEPTH, D_MODEL, D_FF), jnp.float32) * d_s,
        'w2_down': nrm(ks[17], (DEPTH, D_FF, D_MODEL), jnp.float32) * D_FF ** -0.5,
    }

def first_block(x, c, w_mod, b_mod, g_ffn1, w1_gate, w1_up, w1_down, g_mix, w_in, b_f, g_q, g_k,
              w_o, g_ffn2, w2_gate, w2_up, w2_down):
    c_act = jax.nn.silu(c)
    for l in range(DEPTH):
        mod = c_act @ w_mod[l] + b_mod[l]
        sh1, sc1, ga1, sh2, sc2, ga2, sh3, sc3, ga3 = jnp.split(mod, N_MOD, axis=-1)
        h = modulate(rms_norm(x, g_ffn1[l]), sh1, sc1)
        x = x + 0.5 * (1 + ga1[:, None, :]) * swiglu(h, w1_gate[l], w1_up[l], w1_down[l])
        h = modulate(rms_norm(x, g_mix[l]), sh2, sc2)
        x = x + (1 + ga2[:, None, :]) * hybrid_mixer(h, w_in[l], b_f[l], g_q[l], g_k[l], w_o[l])
        h = modulate(rms_norm(x, g_ffn2[l]), sh3, sc3)
        x = x + 0.5 * (1 + ga3[:, None, :]) * swiglu(h, w2_gate[l], w2_up[l], w2_down[l])
    return x


CHUNK = 64
N_META = 16
Q_BLOCK = 128
GLA_HEADS = 4
GLA_DK = 64
GLA_DV = 128
GLA_GATE_RANK = 16
GLA_TAU = 16.0
GLA_QK = GLA_HEADS * GLA_DK
GLA_VW = GLA_HEADS * GLA_DV
MLA_HEADS = 4
MLA_Q_RANK = 256
MLA_KV_RANK = 128
MLA_NOPE = 128
MLA_ROPE = 64
MLA_V = 128
MLA_OUT = MLA_HEADS * MLA_V
ROPE_BASE = 10000.0
D_MIX = GLA_VW + MLA_OUT
IN_WIDTHS = (GLA_QK, GLA_QK, GLA_VW, GLA_VW, GLA_GATE_RANK, MLA_Q_RANK, MLA_KV_RANK, MLA_ROPE)
D_IN = sum(IN_WIDTHS)
N_GROUPS = 8
EXPERTS_PER_GROUP = 8
N_EXPERTS = N_GROUPS * EXPERTS_PER_GROUP
TOP_K = 2
D_EXPERT = 512
MOE_BLOCK = 128


def rmsnorm(x, gain):
    x32 = x.astype(jnp.float32)
    y = x32 * lax.rsqrt(jnp.mean(x32 * x32, axis=-1, keepdims=True) + EPS)
    return (y * gain.astype(jnp.float32)).astype(x.dtype)

def split_points():
    pts, acc = [], 0
    for w in IN_WIDTHS[:-1]:
        acc += w
        pts.append(acc)
    return pts

def chunk_ids(length):
    p = jnp.arange(length)
    return jnp.where(p < N_META, 0, 1 + (p - N_META) // CHUNK)

def rope_tables(length):
    pos = jnp.arange(length, dtype=jnp.float32)
    inv = ROPE_BASE ** (-jnp.arange(0, MLA_ROPE, 2, dtype=jnp.float32) / MLA_ROPE)
    ang = pos[:, None] * inv[None, :]
    return jnp.cos(ang), jnp.sin(ang)

def apply_rope(x, cos, sin):
    half = x.shape[-1] // 2
    x1, x2 = x[..., :half].astype(jnp.float32), x[..., half:].astype(jnp.float32)
    return jnp.concatenate([x1 * cos - x2 * sin, x2 * cos + x1 * sin], axis=-1).astype(x.dtype)

def gla_group(q, k, v, r, a_low, w_a2, b_a, out_gain):
    f32 = jnp.float32
    B, L, _ = q.shape
    pad = (-L) % CHUNK
    log_a = jax.nn.log_sigmoid((a_low @ w_a2 + b_a).astype(f32)) / GLA_TAU

    def prep(t, d):
        t = jnp.pad(t.astype(f32), ((0, 0), (pad, 0), (0, 0)))
        n = t.shape[1] // CHUNK
        return t.reshape(B, n, CHUNK, GLA_HEADS, d).transpose(0, 3, 1, 2, 4)

    qc = prep(q, GLA_DK) * (GLA_DK ** -0.5)
    kc = prep(k, GLA_DK)
    vc = prep(v, GLA_DV)
    b = jnp.cumsum(prep(log_a, GLA_DK), axis=3)
    b_last = b[:, :, :, -1:, :]
    q_e = qc * jnp.exp(b)
    causal = jnp.tril(jnp.ones((CHUNK, CHUNK), dtype=bool))
    att = jnp.where(causal, jnp.einsum('bhncd,bhnsd->bhncs', q_e, kc * jnp.exp(-b)), 0.0)
    o = jnp.einsum('bhncs,bhnse->bhnce', att, vc)
    upd = jnp.einsum('bhncd,bhnce->nbhde', kc * jnp.exp(b_last - b), vc)
    decay = jnp.exp(b_last[:, :, :, 0, :]).transpose(2, 0, 1, 3)

    def step(s, inp):
        dec, u = inp
        return dec[..., None] * s + u, s

    s0 = jnp.zeros((B, GLA_HEADS, GLA_DK, GLA_DV), f32)
    _, s_prev = lax.scan(step, s0, (decay, upd))
    o = o + jnp.einsum('bhncd,nbhde->bhnce', q_e, s_prev)
    o = o.transpose(0, 2, 3, 1, 4).reshape(B, -1, GLA_HEADS, GLA_DV)[:, pad:]
    o = o * lax.rsqrt(jnp.mean(o * o, axis=-1, keepdims=True) + EPS)
    o = o.reshape(B, L, GLA_VW) * out_gain.astype(f32)
    return (o * jax.nn.silu(r.astype(f32))).astype(q.dtype)

def mla_group(q_lat, kv_lat, k_rope, q_norm, w_qb, kv_norm, w_kvb):
    B, L, _ = q_lat.shape
    q = (rmsnorm(q_lat, q_norm) @ w_qb).reshape(B, L, MLA_HEADS, MLA_NOPE + MLA_ROPE)
    q_nope, q_rope = q[..., :MLA_NOPE], q[..., MLA_NOPE:]
    kv = (rmsnorm(kv_lat, kv_norm) @ w_kvb).reshape(B, L, MLA_HEADS, MLA_NOPE + MLA_V)
    k_nope, v = kv[..., :MLA_NOPE], kv[..., MLA_NOPE:]
    cos, sin = rope_tables(L)
    q_rope = apply_rope(q_rope, cos[:, None, :], sin[:, None, :])
    k_rope = apply_rope(k_rope, cos, sin)
    key_chunk = chunk_ids(L)
    scale = (MLA_NOPE + MLA_ROPE) ** -0.5

    def attend(args):
        qn, qr, qcid = args
        s = (jnp.einsum('bqhd,bkhd->bhqk', qn, k_nope)
             + jnp.einsum('bqhd,bkd->bhqk', qr, k_rope)).astype(jnp.float32) * scale
        s = jnp.where(key_chunk[None, None, None, :] <= qcid[None, None, :, None], s, -jnp.inf)
        p = jax.nn.softmax(s, axis=-1).astype(v.dtype)
        return jnp.einsum('bhqk,bkhd->bqhd', p, v)

    meta_out = attend((q_nope[:, :N_META], q_rope[:, :N_META], key_chunk[:N_META]))
    nb = (L - N_META) // Q_BLOCK

    def blocks(t):
        return t[:, N_META:].reshape(B, nb, Q_BLOCK, *t.shape[2:]).swapaxes(0, 1)

    blk = lax.map(attend, (blocks(q_nope), blocks(q_rope), key_chunk[N_META:].reshape(nb, Q_BLOCK)))
    blk = blk.swapaxes(0, 1).reshape(B, L - N_META, MLA_HEADS, MLA_V)
    return jnp.concatenate([meta_out, blk], axis=1).reshape(B, L, MLA_OUT)

def hier_moe(u, wg, bg, we, be, w_gate, w_up, w_down):
    f32 = jnp.float32
    B, L, D = u.shape
    t = u.reshape(-1, D)
    n_tok = t.shape[0]
    g_prob = jax.nn.softmax((t @ wg + bg).astype(f32), axis=-1)
    g_p, g_idx = lax.top_k(g_prob, 1)
    e_logits = (t @ we + be).astype(f32).reshape(n_tok, N_GROUPS, EXPERTS_PER_GROUP)
    e_logits = jnp.take_along_axis(e_logits, g_idx[:, :, None], axis=1)[:, 0]
    e_p, e_idx = lax.top_k(jax.nn.softmax(e_logits, axis=-1), TOP_K)
    gates = g_p * e_p / jnp.sum(e_p, axis=-1, keepdims=True)
    expert = g_idx * EXPERTS_PER_GROUP + e_idx
    e_flat = expert.reshape(-1)
    tok_flat = jnp.repeat(jnp.arange(n_tok, dtype=jnp.int32), TOP_K)
    gate_flat = gates.reshape(-1)
    order = jnp.argsort(e_flat)
    e_sorted, tok_sorted, gate_sorted = e_flat[order], tok_flat[order], gate_flat[order]
    counts = jnp.bincount(e_flat, length=N_EXPERTS)
    padded = (counts + MOE_BLOCK - 1) // MOE_BLOCK * MOE_BLOCK
    pad_end = jnp.cumsum(padded)
    pad_start = pad_end - padded
    seg_start = jnp.cumsum(counts) - counts
    n_assign = n_tok * TOP_K
    dest = pad_start[e_sorted] + jnp.arange(n_assign) - seg_start[e_sorted]
    n_blocks = -(-(n_assign + N_EXPERTS * (MOE_BLOCK - 1)) // MOE_BLOCK)
    n_slots = n_blocks * MOE_BLOCK
    slot_tok = jnp.full((n_slots,), n_tok, jnp.int32).at[dest].set(tok_sorted)
    slot_gate = jnp.zeros((n_slots,), f32).at[dest].set(gate_sorted)
    block_expert = jnp.minimum(
        jnp.searchsorted(pad_end, jnp.arange(n_blocks) * MOE_BLOCK, side='right'), N_EXPERTS - 1)
    t_pad = jnp.concatenate([t, jnp.zeros((1, D), t.dtype)], axis=0)
    xs = t_pad[slot_tok].reshape(n_blocks, MOE_BLOCK, D)

    def expert_block(args):
        xb, e = args
        hdn = jax.nn.silu(xb @ w_gate[e]) * (xb @ w_up[e])
        return hdn @ w_down[e]

    ys = lax.map(expert_block, (xs, block_expert)).reshape(n_slots, D)
    out = jnp.zeros((n_tok + 1, D), f32).at[slot_tok].add(ys.astype(f32) * slot_gate[:, None])[:n_tok]
    return out.reshape(B, L, D).astype(u.dtype)

def second_inputs(seed: int = 0) -> dict:
    key = jax.random.key(seed)
    ks = jax.random.split(key, 24)
    f32 = jnp.float32

    def nrm(k, shape, scale):
        return jax.random.normal(k, shape, f32) * scale

    def gain(k, shape):
        return 1.0 + 0.02 * jax.random.normal(k, shape, f32)

    return {
        'x': nrm(ks[0], (BATCH, SEQ, D_MODEL), 1.0),
        'meta_tokens': nrm(ks[1], (N_META, D_MODEL), 1.0),
        'mix_norm': gain(ks[2], (DEPTH, D_MODEL)),
        'w_in': nrm(ks[3], (DEPTH, D_MODEL, D_IN), D_MODEL ** -0.5),
        'gla_w_a2': nrm(ks[4], (DEPTH, GLA_GATE_RANK, GLA_QK), GLA_GATE_RANK ** -0.5),
        'gla_b_a': nrm(ks[5], (DEPTH, GLA_QK), 0.1),
        'gla_out_norm': gain(ks[6], (DEPTH, GLA_VW)),
        'mla_q_norm': gain(ks[7], (DEPTH, MLA_Q_RANK)),
        'mla_w_qb': nrm(ks[8], (DEPTH, MLA_Q_RANK, MLA_HEADS * (MLA_NOPE + MLA_ROPE)), MLA_Q_RANK ** -0.5),
        'mla_kv_norm': gain(ks[9], (DEPTH, MLA_KV_RANK)),
        'mla_w_kvb': nrm(ks[10], (DEPTH, MLA_KV_RANK, MLA_HEADS * (MLA_NOPE + MLA_V)), MLA_KV_RANK ** -0.5),
        'w_out': nrm(ks[11], (DEPTH, D_MIX, D_MODEL), D_MIX ** -0.5),
        'ffn_norm': gain(ks[12], (DEPTH, D_MODEL)),
        'router_group_w': nrm(ks[13], (DEPTH, D_MODEL, N_GROUPS), D_MODEL ** -0.5),
        'router_group_b': nrm(ks[14], (DEPTH, N_GROUPS), 0.01),
        'router_expert_w': nrm(ks[15], (DEPTH, D_MODEL, N_EXPERTS), D_MODEL ** -0.5),
        'router_expert_b': nrm(ks[16], (DEPTH, N_EXPERTS), 0.01),
        'expert_w_gate': nrm(ks[17], (DEPTH, N_EXPERTS, D_MODEL, D_EXPERT), D_MODEL ** -0.5),
        'expert_w_up': nrm(ks[18], (DEPTH, N_EXPERTS, D_MODEL, D_EXPERT), D_MODEL ** -0.5),
        'expert_w_down': nrm(ks[19], (DEPTH, N_EXPERTS, D_EXPERT, D_MODEL), D_EXPERT ** -0.5),
        'final_norm': gain(ks[20], (D_MODEL,)),
    }

def second_block(x, meta_tokens, mix_norm, w_in, gla_w_a2, gla_b_a, gla_out_norm, mla_q_norm, mla_w_qb,
              mla_kv_norm, mla_w_kvb, w_out, ffn_norm, router_group_w, router_group_b, router_expert_w,
              router_expert_b, expert_w_gate, expert_w_up, expert_w_down, final_norm):
    B = x.shape[0]
    meta = jnp.broadcast_to(meta_tokens[None].astype(x.dtype), (B, N_META, x.shape[-1]))
    h = jnp.concatenate([meta, x], axis=1)
    pts = split_points()
    for l in range(DEPTH):
        u = rmsnorm(h, mix_norm[l])
        z = u @ w_in[l]
        q, k, v, r, a_low, q_lat, kv_lat, k_rope = jnp.split(z, pts, axis=-1)
        y_gla = gla_group(q, k, v, r, a_low, gla_w_a2[l], gla_b_a[l], gla_out_norm[l])
        y_mla = mla_group(q_lat, kv_lat, k_rope, mla_q_norm[l], mla_w_qb[l], mla_kv_norm[l], mla_w_kvb[l])
        h = h + jnp.concatenate([y_gla, y_mla], axis=-1) @ w_out[l]
        h = h + hier_moe(rmsnorm(h, ffn_norm[l]), router_group_w[l], router_group_b[l], router_expert_w[l],
                         router_expert_b[l], expert_w_gate[l], expert_w_up[l], expert_w_down[l])
    return rmsnorm(h, final_norm)[:, N_META:]


def setup_inputs(seed=0):
    out = dict(first_inputs(seed))
    for name, value in second_inputs(seed + 1).items():
        if name != "x":
            out[name + "_2"] = value
    return out


def reference(
    x, c, w_mod, b_mod, g_ffn1, w1_gate, w1_up, w1_down, g_mix, w_in, b_f, g_q, g_k, w_o,
    g_ffn2, w2_gate, w2_up, w2_down, meta_tokens_2, mix_norm_2, w_in_2, gla_w_a2_2, gla_b_a_2,
    gla_out_norm_2, mla_q_norm_2, mla_w_qb_2, mla_kv_norm_2, mla_w_kvb_2, w_out_2, ffn_norm_2,
    router_group_w_2, router_group_b_2, router_expert_w_2, router_expert_b_2, expert_w_gate_2,
    expert_w_up_2, expert_w_down_2, final_norm_2,
):
    x = first_block(
        x, c, w_mod, b_mod, g_ffn1, w1_gate, w1_up, w1_down, g_mix, w_in, b_f, g_q, g_k, w_o,
        g_ffn2, w2_gate, w2_up, w2_down,
    )
    return second_block(
        x, meta_tokens_2, mix_norm_2, w_in_2, gla_w_a2_2, gla_b_a_2, gla_out_norm_2,
        mla_q_norm_2, mla_w_qb_2, mla_kv_norm_2, mla_w_kvb_2, w_out_2, ffn_norm_2,
        router_group_w_2, router_group_b_2, router_expert_w_2, router_expert_b_2,
        expert_w_gate_2, expert_w_up_2, expert_w_down_2, final_norm_2,
    )


_drawn_inputs = setup_inputs


def setup_inputs(seed=0):
    import zlib

    import numpy as np

    out = dict(_drawn_inputs(seed))
    spreads = {}
    factors = {'g_ffn1': 4.005,
     'g_mix': 2.908,
     'g_q': 6.484,
     'g_k': 7.056,
     'g_ffn2': 4.01,
     'mix_norm_2': 3.181,
     'gla_b_a_2': 2.67,
     'gla_out_norm_2': 4.666,
     'mla_q_norm_2': 8.0,
     'mla_kv_norm_2': 8.0,
     'ffn_norm_2': 2.772,
     'router_group_b_2': 6.252,
     'router_expert_b_2': 21.369,
     'final_norm_2': 7.98}
    for name, (base, spread) in spreads.items():
        noise = np.random.default_rng([zlib.crc32(name.encode()), seed]).standard_normal(out[name].shape)
        drawn = base * np.exp(spread * noise) if base else spread * noise
        out[name] = jnp.asarray(drawn.astype(out[name].dtype))
    for name, factor in factors.items():
        out[name] = (out[name] * factor).astype(out[name].dtype)
    return out
```

```python
from contextlib import ExitStack

import numpy as np
import concourse.bass as bass
from concourse import mybir

ALU = mybir.AluOpType
ACT = mybir.ActivationFunctionType
F32 = mybir.dt.float32
I32 = mybir.dt.int32
U32 = mybir.dt.uint32
AX_X = mybir.AxisListType.X

P = 128
D = 1024
KC = D // P
SEQ = 512
META = 16
TOK = SEQ + META
FF = 2816
FC = FF // P
EPS = 1e-6
HD = 64
N_SLOT = 6
SLOT = 4096
TILE_AT = [0, 128, 384, 768]
TRI = 1280
OFF_DIAG = [(i, k) for i in range(4) for k in range(i)]
BLOCK_AT = {(i, i): i for i in range(4)}
BLOCK_AT.update({ik: 4 + n for n, ik in enumerate(OFF_DIAG)})

COLS = {}


def _cols():
    at = 0
    for name, n in (("c", 8), ("b_mod", 72), ("g_ffn1", 8), ("g_mix", 8), ("g_ffn2", 8), ("mix_norm_2", 8),
                    ("gla_out_norm_2", 4), ("mla_q_norm_2", 2), ("mla_kv_norm_2", 1), ("gla_b_a_2", 2),
                    ("g_q", 4), ("g_k", 4)):
        COLS[name] = (at, n)
        at += n
    return at


N_COLS = _cols()

GH = 4
CHUNK = 64
N_CHUNK = SEQ // CHUNK
ROPE = 64
NOPE = 128
MLA_SCALE = (NOPE + ROPE) ** -0.5
D_IN2 = 2000
NG, NE = 8, 64
DE = 512
CAP = 64
N_ASG = 2 * SEQ
MAX_BLOCKS = NE + (N_ASG - NE) // CAP
MAX_PAIRS = (MAX_BLOCKS + 1) // 2
TAB = 2 * MAX_PAIRS + 4
FAR = 8192.0
NT = SEQ // P

CONST = {}


def constant_tables():
    p = np.arange(P)[:, None]
    j = np.arange(P)[None, :]
    parts = [("ident", (p == j) * 1.0),
             ("ones", np.ones((P, P))),
             ("head_ones", (p // HD == j // HD) * 1.0),
             ("after", (p > j) * -1e30 * 0 + (j > p) * -1e30),
             ("strict_t", (p < j) * 1.0)]
    resets = []
    for i in range(4):
        k = np.arange(P * (i + 1))[None, :]
        resets.append((k < i * P + p - 1) * 1.0)
    parts.append(("resets", np.concatenate(resets, axis=1)))
    tok = np.arange(TOK)[None, :]
    chunk_start = (tok == 0) | ((tok >= META) & ((tok - META) % CHUNK == 0))
    parts.append(("chunk_resets", np.broadcast_to(1.0 - chunk_start, (P, TOK))))
    parts.append(("chunk_causal", ((p <= j) & (p // CHUNK == j // CHUNK)) * 1.0))
    freq = (np.float32(10000.0) ** (-np.arange(0, ROPE, 2, dtype=np.float32) / np.float32(ROPE))).astype(np.float32)
    angle = (np.arange(TOK, dtype=np.float32)[:, None] * freq[None, :]).astype(np.float32).T
    rows = np.zeros((P, TOK), np.float32)
    rows[0:ROPE] = np.concatenate([np.cos(angle), np.cos(angle)], axis=0)
    parts.append(("rope_cos", rows))
    rows = np.zeros((P, TOK), np.float32)
    rows[0:ROPE] = np.concatenate([-np.sin(angle), np.sin(angle)], axis=0)
    parts.append(("rope_sin", rows))
    parts.append(("iota8", np.broadcast_to(np.arange(8.0), (P, 8))))
    parts.append(("block_first", np.broadcast_to(np.arange(0.0, CAP * (TAB + 1), CAP), (P, TAB + 1))))
    parts.append(("block_no", p * 1.0))
    parts.append(("iota_cap", np.broadcast_to(np.arange(float(CAP)), (P, CAP))))
    asg = 2 * (np.arange(NT)[None, :, None] * P + np.arange(P)[:, None, None]) + np.arange(2)[None, None, :] + 1
    parts.append(("asg1", asg.reshape(P, 2 * NT) * 1.0))
    parts.append(("tok1", ((asg - 1) // 2 + 1).reshape(P, 2 * NT) * 1.0))
    at = 0
    for name, t in parts:
        CONST[name] = (at, t.shape[1])
        at += t.shape[1]
    return np.ascontiguousarray(np.concatenate([t for _, t in parts], axis=1).astype(np.float32))


CONST_ARRAY = constant_tables()


class Uses:

    def __init__(self):
        self.filled = [0] * N_SLOT
        self.freed = [1] * N_SLOT

    def take(self, s, dmas, times=1):
        before = (self.filled[s], self.freed[s])
        self.filled[s] += 16 * dmas * times
        self.freed[s] += times
        return before


def build(nc, a, out):
    ctx = ExitStack()
    with ctx:
        def sb(name, shape, dt=F32):
            return ctx.enter_context(nc.sbuf_tensor(name, shape, dt))

        def sem(name):
            return ctx.enter_context(nc.semaphore(name))

        ring = [sb(f"slot{s}", [P, SLOT]) for s in range(N_SLOT)]
        cst = sb("cst", [P, CONST_ARRAY.shape[1]])
        cols = sb("cols", [P, N_COLS])
        xT = sb("xT", [P, KC, TOK])
        hT = sb("hT", [P, KC, TOK])
        big = sb("big", [P, FC * SEQ])
        aT = big[:, :].rearrange("p (f t) -> p f t", f=FC)
        modT = sb("modT", [P, 72])
        small = sb("small", [P, 64])
        tmp = sb("tmp", [P, 2, TOK])
        rstd = sb("rstd", [P, TOK])
        eb = sb("eb", [P, 2, SEQ])
        ps = ctx.enter_context(nc.psum_tensor("ps", [P, 8, 512], F32))

        def const(name):
            at, n = CONST[name]
            return cst[:, at:at + n]

        def col(name, j=None):
            at, n = COLS[name]
            return cols[:, at:at + n] if j is None else cols[:, at + j:at + j + 1]

        ident, ones = const("ident"), const("ones")
        c_act = small[:, 0:8]
        c_exp = small[:, 8:16]
        scale = [small[:, 16 + 8 * r:24 + 8 * r] for r in range(3)]
        gate = [small[:, 40 + 8 * r:48 + 8 * r] for r in range(3)]
        eps_col = sb("eps_col", [P, 1])

        def part(at, n):
            return big[:, at:at + n]
        qT = part(0, 512)
        kT = part(512, 512)
        vt = part(1024, 512).rearrange("p (t n) -> p t n", t=4)
        buf1 = part(1536, TRI)
        buf2 = part(1536 + TRI, TRI)
        PT = part(1536 + 2 * TRI, TRI).rearrange("p (b q) -> p b q", q=P)
        oT = part(5376, 4096).rearrange("p (c t) -> p c t", c=8)
        FL = big[:, 9472:9984]
        FR = big[:, 9984:10496]
        Fc = big[0:8, 10496:11008]
        fA = tmp[0:8, 0, 0:512]
        fB = tmp[0:8, 1, 0:512]
        fox_s = sb("fox_s", [P, 16])
        gqs = sb("gqs", [P, 4])
        wf = sb("wf", [P, KC, 8])
        bf = sb("bf", [8, 1])

        s_in = sem("inputs_in")
        s_x = sem("x_in")
        filled = [sem(f"filled{s}") for s in range(N_SLOT)]
        freed = [sem(f"freed{s}") for s in range(N_SLOT)]
        s_phase = sem("phase_done")
        s_vec = sem("vector_step")
        s_act = sem("scalar_step")
        s_tr = sem("turned")
        s_trc = sem("turned_copied")
        s_cexp = sem("c_exp_ready")
        s_cact = sem("c_act_ready")
        s_mod = sem("mod_done")
        s_sq = sem("squares_ready")
        s_ss = sem("square_sum_done")
        s_std = sem("std_ready")
        s_rs = sem("rstd_ready")
        s_nx = sem("normed_ready")
        s_gu = sem("gate_up_done")
        s_ge = sem("gate_exp_ready")
        s_hid = sem("hidden_ready")
        s_dn = sem("down_done")
        s_qkv = sem("qkv_done")
        s_qc = sem("q_copied")
        s_kvc = sem("kv_copied")
        s_qsq = sem("qk_squares_ready")
        s_qss = sem("qk_square_sum_done")
        s_qstd = sem("qk_std_ready")
        s_z = sem("scores_done")
        s_sp = sem("softplus_ready")
        s_zz = sem("log_weights_ready")
        s_mx = sem("max_ready")
        s_e = sem("exp_ready")
        s_p = sem("probs_ready")
        s_pt = sem("probs_turned")
        s_ptc = sem("probs_turned_copied")
        s_pv = sem("heads_done")
        s_o = sem("heads_copied")
        s_fl = sem("forget_ready")
        s_fm = sem("forget_head_ready")
        s_fp = sem("forget_proj_done")
        s_f1 = sem("forget_exp_ready")
        s_wo = sem("mix_done")
        s_out = sem("out_written")

        flat = ps[:, :, :].rearrange("p b n -> p (b n)")
        gq = part(0, 1024).rearrange("p (c t) -> p c t", c=2)
        gk = part(1024, 1056).rearrange("p (c t) -> p c t", c=2)
        gv = part(2080, 2560).rearrange("p (t n) -> p t n", t=5)
        gr = part(4640, 2048).rearrange("p (c t) -> p c t", c=4)
        aL = part(6688, TOK)
        ql = part(7216, 1024).rearrange("p (c t) -> p c t", c=2)
        kv = part(8240, TOK)
        kr = part(8768, TOK)
        kdtok = part(9296, 1280).rearrange("p (t n) -> p t n", t=5)
        swap = part(10576, TOK)
        Sc = ring[0][:, 0:1056].rearrange("p (c t) -> p c t", c=2)
        km = ring[0][:, 1056:2112].rearrange("p (c t) -> p c t", c=2)
        kd = ring[0][:, 2112:3168].rearrange("p (c t) -> p c t", c=2)
        states = ring[1][:, 0:2 * (N_CHUNK + 1) * P].rearrange("p (c n e) -> p c n e", c=2, n=N_CHUNK + 1)
        o2 = hT[:, :, :].rearrange("p k t -> p (k t)")[:, 0:8 * SEQ].rearrange("p (c t) -> p c t", c=8)
        attS = eb[:, 0, :].rearrange("p (b c) -> p b c", b=4)
        osq = eb[:, 1, :]
        sil = tmp[:, 0, 0:SEQ]
        orst = tmp[:, 1, 0:SEQ]
        qn = ring[0][:, 0:2048].rearrange("p (h t) -> p h t", h=GH)
        qr = ring[0][0:ROPE, 2048:4096].rearrange("p (h t) -> p h t", h=GH)
        kn = ring[1][:, 0:GH * TOK].rearrange("p (h t) -> p h t", h=GH)
        mv = ring[3][:, 0:2560].rearrange("p (t n) -> p t n", t=5)
        PB = [tmp[:, j, :] for j in range(2)]
        mPT = big[:, 0:640].rearrange("p (b q) -> p b q", b=5)
        glst = sb("glst", [P, 64])
        w_a2 = ring[2][0:16, 0:256]
        w_qb = ring[2][:, 256:1792].rearrange("p (k n) -> p k n", k=2)
        w_kvb = ring[2][:, 1792:2816]
        h2 = part(0, 4096).rearrange("p (t d) -> p t d", t=NT)
        u2 = part(4096, 4096).rearrange("p (t d) -> p t d", t=NT)
        uT = xT[:, :, :].rearrange("p k t -> p (k t)")[:, 0:KC * SEQ].rearrange("p (k t) -> p k t", k=KC)
        gain_row = part(8192, D)
        wr = ring[3][:, 2560:2560 + KC * 72].rearrange("p (k n) -> p k n", k=KC)
        bias_row = ring[3][:, 3200:3272]
        gates = sb("gates", [P, NT, 2])
        rb = hT[:, :, :].rearrange("p k t -> p (k t)")
        tok_ix = sb("tok_ix", [CAP, TAB], I32)
        asg_ix = sb("asg_ix", [CAP, TAB], I32)
        expert_ix = sb("expert_ix", [1, P], I32)
        pairs_ix = sb("pairs_ix", [1, 4], I32)
        mo = xT[:, :, :].rearrange("p k t -> p (k t)")
        xs = [mo[0:CAP, 1024 * j:1024 * (j + 1)] for j in range(2)]
        xsT = [mo[:, 2048 + 512 * j:2560 + 512 * j].rearrange("p (k s) -> p k s", k=KC) for j in range(2)]
        sg = [mo[0:CAP, 3072 + 512 * j:3584 + 512 * j] for j in range(2)]
        mo2 = hT[:, :, :].rearrange("p k t -> p (k t)")
        hid = [mo2[:, 256 * j:256 * (j + 1)].rearrange("p (c s) -> p c s", c=4) for j in range(2)]
        ys = [mo2[0:CAP, 512 + 1024 * j:1536 + 1024 * j] for j in range(2)]
        hrow = [mo2[0:CAP, 2560 + 512 * j:3072 + 512 * j] for j in range(2)]
        tcol = [sb(f"tcol{j}", [CAP, 1], I32) for j in range(2)]
        acol = [sb(f"acol{j}", [CAP, 1], I32) for j in range(2)]
        y2 = [ring[j][:, 0:2 * D].rearrange("p (k d) -> p k d", k=2) for j in range(2)]
        u_dram = nc.dram_tensor("normed_tokens", (SEQ, D), F32, kind="Internal").ap()
        y_dram = nc.dram_tensor("expert_rows", (N_ASG, D), F32, kind="Internal").ap()

        s_rn = sem("mean_square_ready")
        s_rnq = sem("row_root_ready")
        s_vec2 = sem("vector_last_step")
        at = [0]

        def scratch(*shape):
            n = 1
            for m in shape:
                n *= m
            ap = rb[:, at[0]:at[0] + n]
            at[0] += n
            if len(shape) == 1:
                return ap
            names = "abcd"[:len(shape)]
            return ap.rearrange("p (" + " ".join(names) + ") -> p " + " ".join(names),
                                **{c: m for c, m in zip(names[1:], shape[1:])})
        lg = scratch(NT, 72)
        t8, ghot, hot1, hot2, el = (scratch(NT, 8) for _ in range(5))
        t1, gtop, top1, top2, gsum = (scratch(NT) for _ in range(5))
        rx = scratch(NT * NG + NT)
        pick = scratch(NT, NG, 8)
        Mk = [scratch(NT, NE) for _ in range(2)]
        Mh = scratch(NT, NE)
        slot = scratch(NT, NE)
        cnt, nblk, blk_end = (scratch(NE) for _ in range(3))
        pos = scratch(NT, 2)
        t2 = scratch(2 * NT)
        expert_col = scratch(1)
        ge = scratch(2 * NT, TAB + 1)
        at[0] = 0
        rb = tmp[:, :, :].rearrange("p b n -> p (b n)")
        block_hot = scratch(2 * NT, TAB)
        at[0] = 0
        rb = eb[:, :, :].rearrange("p b n -> p (b n)")
        slot_hot = [scratch(2 * NT, CAP)]
        at[0] = 0
        rb = part(9216, 2048)
        slot_hot.append(scratch(2 * NT, CAP))
        sq_row = part(9216 + 512, D)
        s_p2 = sem("proj2_done")
        s_p2c = [sem(f"proj2_copied{j}") for j in range(2)]
        s_la = sem("decay_proj_done")
        s_lq = sem("latent_squares_ready")
        s_lss = sem("latent_square_sum_done")
        s_lstd = sem("latent_std_ready")
        s_dt = sem("decay_logit_ready")
        s_dsp = sem("decay_softplus_ready")
        s_S = sem("decay_sum_ready")
        s_dx = sem("decay_exp_ready")
        s_kd = sem("decayed_keys_ready")
        s_kt = sem("decayed_keys_turned")
        s_ktc = sem("decayed_keys_turned_copied")
        s_U = sem("chunk_update_done")
        s_st = sem("state_ready")
        s_at2 = sem("gla_scores_done")
        s_atm = sem("gla_scores_masked")
        s_go = sem("gla_out_done")
        s_gsq = sem("gla_out_squares")
        s_gss = sem("gla_out_square_sum")
        s_gstd = sem("gla_out_std")
        s_gf = sem("gla_head_ready")
        s_mz = sem("mla_scores_done")
        s_mb = sem("mla_max_ready")
        s_me = sem("mla_exp_ready")
        s_mp = sem("mla_probs_ready")
        s_mt = sem("mla_probs_turned")
        s_mtc = sem("mla_probs_turned_copied")
        s_mpv = sem("mla_head_done")
        s_mo = sem("mla_head_copied")
        s_xr = sem("residual_turned")
        s_xrc = sem("residual_copied")
        s_h2 = sem("mixed_ready")
        s_un = sem("normed_row_ready")
        s_ut = sem("normed_turned")
        s_utc = sem("normed_turned_copied")
        s_lg = sem("logits_done")
        s_rx = sem("router_exp")
        s_M = sem("router_onehot_ready")
        s_rk = sem("ranks_done")
        s_pos = sem("slots_ready")
        s_tb = sem("tables_done")
        s_be = sem("block_expert_ready")
        s_bet = sem("block_expert_turned")
        s_row = sem("gain_in")
        s_ud = sem("normed_written")
        s_gat = [sem(f"gathered{j}") for j in range(2)]
        s_scat = [sem(f"scattered{j}") for j in range(2)]
        s_xt = sem("expert_in_turned")
        s_xtc = sem("expert_in_ready")
        s_mg = sem("expert_gate_done")
        s_mu = sem("expert_up_done")
        s_my = sem("expert_down_done")
        s_eg = sem("expert_exp_ready")
        s_hd = sem("expert_hidden_ready")
        s_ha = sem("expert_hidden_rows_ready")
        s_ta = sem("expert_hidden_turned")
        s_yc = sem("expert_rows_ready")
        s_ysf = sem("row_buffer_free")
        s_pix = sem("index_column_ready")
        s_y2 = [sem(f"rows_back{j}") for j in range(2)]
        s_y2f = sem("rows_used")
        s_fin = sem("final_rows_ready")

        w_in2 = a["w_in_2"][0].rearrange("(k p) n -> p k n", p=P)
        w_out2 = a["w_out_2"][0].rearrange("(f p) n -> p f n", p=P)
        ITEMS2 = [(0, 512), (512, 512), (1024, 512), (1536, 464)]

        def w2(n):
            return ring[2 + n][:, 0:KC * ITEMS2[n][1]].rearrange("p (k n) -> p k n", k=KC)
        UNITS = [(0, 0, P, False, gq[:, 0]), (0, P, P, False, gq[:, 1]), (0, 2 * P, P, True, gk[:, 0]), (0, 3 * P, P, True, gk[:, 1]),
                 (1, 0, META, None, gv[0:META, 0]), (1, 0, P, None, gv[:, 1]), (1, 0, P, None, gv[:, 2]),
                 (1, 0, P, None, gv[:, 3]), (1, 0, P, None, gv[:, 4]),
                 (2, 0, P, False, gr[:, 0]), (2, P, P, False, gr[:, 1]), (2, 2 * P, P, False, gr[:, 2]), (2, 3 * P, P, False, gr[:, 3]),
                 (3, 0, 16, True, aL[0:16, :]), (3, 16, P, False, ql[:, 0]), (3, 16 + P, P, False, ql[:, 1]),
                 (3, 16 + 2 * P, P, True, kv), (3, 16 + 3 * P, ROPE, True, kr[0:ROPE, :])]
        TILE0 = [0] + [META + P * t for t in range(NT)]
        TILEN = [META] + [P] * NT

        def halves(ap):
            return ap.rearrange("p (b n) -> p b n", b=2)

        def unit_psum(n):
            b = 2 * (n % 4)
            _, _, m, wide, _ = UNITS[n]
            return ps[0:m, b:b + 2, 0:TOK // 2] if wide else ps[0:m, b, :]

        def unit_dst(n):
            return halves(UNITS[n][4]) if UNITS[n][3] else UNITS[n][4]

        spare = sb("spare", [1, 4])

        def mla_z(un):
            t = un % NT
            at = 1024 * (un % 2) + 512
            return flat[:, at - META:at + P * (t + 1)]

        PH = {}

        def phase_end(eng, n):
            eng.drain().then_inc(s_phase, 1)
            eng.wait_ge(s_phase, 4 * n)

        HALVES = {0: [(META, SEQ)], 1: [(META, SEQ)], 2: [(META, SEQ)], 3: [(0, TOK // 2), (TOK // 2, TOK // 2)]}

        w_mod = a["w_mod"][0].rearrange("(k p) n -> p k n", p=P)
        ffn_w = [(a["w1_gate"][0], a["w1_up"][0], a["w1_down"][0]), (a["w2_gate"][0], a["w2_up"][0], a["w2_down"][0])]
        w_in = a["w_in"][0].rearrange("(k p) n -> p k n", p=P)
        w_o = a["w_o"][0].rearrange("(k p) n -> p k n", p=P)
        DOWN_ITEMS = [(f0, min(8, FC - f0)) for f0 in range(0, FC, 8)]
        N_GU = FC // 2

        def gu_view(s):
            return ring[s][:, :].rearrange("p (g k n) -> p g k n", g=2, k=KC)

        def down_slot(ps_, n):
            return (2 + 3 * ps_ + n) % N_SLOT

        block = ctx.enter_context(nc.Block())

        @block.sync
        def _(sp):
            u = Uses()
            sp.dma_start(cst[:, :], a["const"]).then_inc(s_in, 16)
            sp.dma_start(cols[:, :], a["cols"]).then_inc(s_in, 16)
            sp.dma_start(bf[:, :], a["b_f"].rearrange("a h -> h a")).then_inc(s_in, 16)
            sp.dma_start(wf[:, :, :], w_in[:, :, 3072:3080]).then_inc(s_in, 16)
            sp.dma_start(ring[5][:, :].rearrange("p (t d) -> p t d", t=4),
                         a["x"][0].rearrange("(t p) d -> p t d", p=P)).then_inc(s_x, 16)
            sp.dma_start(ring[4][0:META, 0:D], a["meta_tokens_2"]).then_inc(s_x, 16)

            def refill(s, k):
                if isinstance(k, int) and k == 0:
                    return
                sp.wait_ge(freed[s], k)

            first = [u.take(s, 1, 3)[1] for s in range(N_SLOT)]
            with sp.Fori(0, 3) as i:
                for s in range(N_SLOT):
                    sp.wait_ge(freed[s], first[s] + i)
                    sp.dma_start(ring[s][:, :].rearrange("p (k n) -> p k n", k=KC),
                                 w_mod[:, :, bass.ds((i * N_SLOT + s) * 512, 512)]).then_inc(filled[s], 16)

            def ffn(r):
                wg, wu, wd = ffn_w[r]
                wg, wu = (w.rearrange("(k p) n -> p k n", p=P) for w in (wg, wu))
                wd = wd.rearrange("(f p) n -> p f n", p=P)

                def gate_up(s, k, item):
                    sp.wait_ge(freed[s], k)
                    for g, w in enumerate((wg, wu)):
                        sp.dma_start(gu_view(s)[:, g], w[:, :, bass.ds(item * 256, 256)]).then_inc(filled[s], 16)
                base = [u.take(s, 2, N_GU // 2)[1] for s in range(2)]
                with sp.Fori(0, N_GU // 2) as i:
                    for s in range(2):
                        gate_up(s, base[s] + i, i * 2 + s)
                gate_up(0, u.take(0, 2)[1], N_GU - 1)
                for half in range(2):
                    for n, (f0, nf) in enumerate(DOWN_ITEMS):
                        s = down_slot(half, n)
                        sp.wait_ge(freed[s], u.take(s, 1)[1])
                        sp.dma_start(ring[s][:, 0:nf * 512].rearrange("p (f n) -> p f n", f=nf),
                                     wd[:, f0:f0 + nf, half * 512:half * 512 + 512]).then_inc(filled[s], 16)

            def pairs(s, at):
                k = u.take(s, 3, 4)[1]
                view = ring[s][:, 0:KC * 384].rearrange("p (k w n) -> p k w n", k=KC, w=3)
                with sp.Fori(0, 4) as i:
                    sp.wait_ge(freed[s], i + k)
                    for w in range(3):
                        sp.dma_start(view[:, :, w], w_in[:, :, bass.ds(at + w * 512 + i * P, P)]).then_inc(filled[s], 16)

            ffn(0)
            pairs(2, 0)
            pairs(3, 1536)
            for n, s in enumerate((4, 5)):
                sp.wait_ge(freed[s], u.take(s, 1)[1])
                sp.dma_start(ring[s][:, :].rearrange("p (f n) -> p f n", f=4), w_o[:, 4 * n:4 * n + 4, :])\
                    .then_inc(filled[s], 16)
            ffn(1)
            for n, (c0, w) in enumerate(ITEMS2):
                sp.wait_ge(freed[2 + n], u.take(2 + n, 1)[1])
                sp.dma_start(w2(n), w_in2[:, :, c0:c0 + w]).then_inc(filled[2 + n], 16)
            sp.wait_ge(freed[2], u.take(2, 3)[1])
            sp.dma_start(w_a2, a["gla_w_a2_2"][0]).then_inc(filled[2], 16)
            sp.dma_start(w_qb, a["mla_w_qb_2"][0].rearrange("(k p) n -> p k n", p=P)).then_inc(filled[2], 16)
            sp.dma_start(w_kvb, a["mla_w_kvb_2"][0]).then_inc(filled[2], 16)
            for n, s in enumerate((4, 5)):
                sp.wait_ge(freed[s], u.take(s, 1)[1])
                sp.dma_start(ring[s][:, :].rearrange("p (f n) -> p f n", f=4), w_out2[:, 4 * n:4 * n + 4, :])\
                    .then_inc(filled[s], 16)
            sp.wait_ge(freed[3], u.take(3, 3)[1])
            sp.dma_start(wr[:, :, 0:NG], a["router_group_w_2"][0].rearrange("(k p) n -> p k n", p=P)).then_inc(filled[3], 16)
            sp.dma_start(wr[:, :, NG:], a["router_expert_w_2"][0].rearrange("(k p) n -> p k n", p=P)).then_inc(filled[3], 16)
            sp.dma_start(bias_row, a["router_bias"].to_broadcast([P, NG + NE])).then_inc(filled[3], 16)
            sp.wait_ge(s_mo, GH * NT)
            sp.dma_start(gain_row, a["ffn_norm_2"].to_broadcast([P, D])).then_inc(s_row, 16)
            for t in range(NT):
                sp.wait_ge(s_un, t + 1)
                sp.dma_start(u_dram[t * P:(t + 1) * P, :], u2[:, t, :]).then_inc(s_ud, 16)
            sp.wait_ge(s_ud, 16 * NT)
            k01 = [u.take(s, 0)[1] for s in (0, 1)]
            first = [u.take(s, 1)[1] for s in range(N_SLOT)]
            for s in range(N_SLOT):
                sp.wait_ge(freed[s], first[s])
            sp.wait_ge(s_bet, 2)
            n_pairs = sp.value_load(pairs_ix[0:1, 0:1], min_val=2, max_val=MAX_PAIRS)
            experts = [[a[f"expert_w_{n}_2"][0].rearrange("e (p k) n -> e p (k n)", p=P) for n in ("gate", "up")],
                       a["expert_w_down_2"][0].rearrange("e (f p) n -> e p f n", p=P)]
            with sp.Fori(0, n_pairs) as i:
                for j in range(2):
                    e = sp.value_load(expert_ix[0:1, bass.ds(i * 2 + j, 1)], min_val=0, max_val=NE - 1)
                    for n, done in enumerate((s_mg, s_mu)):
                        sp.wait_ge(done, i * 2 + (j + 1))
                        sp.dma_start(ring[3 * j + n][:, :], experts[0][n][bass.ds(e, 1)].rearrange("e p n -> (e p) n"))\
                            .then_inc(filled[3 * j + n], 16)
                    sp.wait_ge(s_my, i * 2 + (j + 1))
                    sp.dma_start(ring[3 * j + 2][:, :].rearrange("p (f n) -> p f n", f=4),
                                 experts[1][bass.ds(e, 1)].rearrange("e p f n -> (e p) f n")).then_inc(filled[3 * j + 2], 16)
            sp.wait_ge(s_phase, 4 * 21)
            sp.dma_start(gain_row, a["final_norm_2"].to_broadcast([P, D])).then_inc(s_row, 16)
            rows = y_dram.rearrange("(t p k) d -> t p k d", p=P, k=2)
            for t in range(NT):
                if t >= 2:
                    sp.wait_ge(s_y2f, t - 1)
                sp.dma_start(y2[t % 2], rows[t]).then_inc(s_y2[t % 2], 16)
            for t in range(NT):
                sp.wait_ge(s_fin, t + 1)
                sp.dma_start(out[0, t * P:(t + 1) * P, :], h2[:, t, :]).then_inc(s_out, 16)
            sp.wait_ge(s_out, 16 * NT)

        @block.tensor
        def _(pe):
            u = Uses()
            mm = nc.tensor.matmul
            for s in range(4):
                pe.drain().then_inc(freed[s], 1)
            pe.wait_ge(s_in, 64)
            pe.wait_ge(s_x, 32)
            xin = ring[5][:, :].rearrange("p (t d) -> p t d", t=4)
            for k in range(KC):
                for t in range(4):
                    last = nc.tensor.transpose(ps[:, k, t * P:(t + 1) * P], xin[:, t, k * P:(k + 1) * P], ident)
                last.then_inc(s_tr, 1)
            pe.wait_ge(s_trc, 1)
            for k in range(KC):
                last = nc.tensor.transpose(ps[:, 0, k * META:(k + 1) * META], ring[4][0:META, k * P:(k + 1) * P],
                                           ident[0:META, 0:META])
            last.then_inc(s_tr, 1)
            for s in (4, 5):
                pe.drain().then_inc(freed[s], 1)
            phase_end(pe, 1)

            pe.wait_ge(s_cact, 1)
            first = [u.take(s, 1, 3) for s in range(N_SLOT)]
            with pe.Fori(0, 3) as i:
                for s in range(N_SLOT):
                    pe.wait_ge(filled[s], first[s][0] + 16 + i * 16)
                    w = ring[s][:, :].rearrange("p (k n) -> p k n", k=KC)
                    for j in range(4):
                        for k in range(KC):
                            last = mm(ps[:, 1, bass.ds(i * 24 + s * 4 + j, 1)], w[:, k, j * P:(j + 1) * P],
                                      c_act[:, k:k + 1], start=(k == 0), stop=(k == KC - 1))
                    last.then_inc(freed[s], 1)
            pe.drain().then_inc(s_mod, 1)

            def norm(r):
                for n in range(KC):
                    pe.wait_ge(s_sq, KC * r + n + 1)
                    for b, (t0, w) in enumerate(HALVES[r]):
                        last = mm(ps[:, b, 0:w], ones, tmp[:, n % 2, t0:t0 + w], start=(n == 0), stop=(n == KC - 1))
                    last.then_inc(s_ss, 1)

            def ffn(r):
                def gate_up(s, have, n0):
                    pe.wait_ge(filled[s], have)
                    w = gu_view(s)
                    for j in range(2):
                        if not (isinstance(n0, int) and n0 == 0):
                            pe.wait_ge(s_hid, n0 + j - 1)
                        for g in range(2):
                            for k in range(KC):
                                last = mm(ps[:, 2 * j + g, :], w[:, g, k, j * P:(j + 1) * P], hT[:, k, META:TOK],
                                          start=(k == 0), stop=(k == KC - 1))
                        last.then_inc(s_gu, 1)
                    pe.drain().then_inc(freed[s], 1)
                base = [u.take(s, 2, N_GU // 2)[0] for s in range(2)]
                with pe.Fori(0, N_GU // 2) as i:
                    for s in range(2):
                        gate_up(s, base[s] + 32 + i * 32, (FC + 2) * r + 2 + i * 4 + 2 * s)
                gate_up(0, u.take(0, 2)[0] + 32, (FC + 2) * r + 2 + FC - 2)
                pe.wait_ge(s_hid, (FC + 2) * r + 2 + FC)
                for half in range(2):
                    bank = 4 if half == 0 else 0
                    for n, (f0, nf) in enumerate(DOWN_ITEMS):
                        s = down_slot(half, n)
                        pe.wait_ge(filled[s], u.take(s, 1)[0] + 16)
                        w = ring[s][:, 0:nf * 512].rearrange("p (f n) -> p f n", f=nf)
                        for f in range(nf):
                            for d in range(4):
                                last = mm(ps[:, bank + d, :], w[:, f, d * P:(d + 1) * P], aT[:, f0 + f, :],
                                          start=(f0 + f == 0), stop=(f0 + f == FC - 1))
                        pe.drain().then_inc(freed[s], 1)
                    pe.drain().then_inc(s_dn, 1)

            def pairs(s, fox):
                have = u.take(s, 3, 4)[0]
                w = ring[s][:, 0:KC * 384].rearrange("p (k w n) -> p k w n", k=KC, w=3)
                with pe.Fori(0, 4) as i:
                    h0 = i * 2 + (8 if fox else 0)
                    pr = i + (4 if fox else 0)
                    pe.wait_ge(filled[s], have + 48 + i * 48)
                    for m in range(2):
                        if m == 1:
                            pe.wait_ge(s_o, h0 + 1)
                        for k in range(KC):
                            last = mm(ps[:, 7 - m, :], w[:, k, m, :], hT[:, k, META:TOK], start=(k == 0), stop=(k == KC - 1))
                        last.then_inc(s_qkv, 1)
                    if fox:
                        for m in range(2):
                            pe.wait_ge(s_qsq, 2 * i + m + 1)
                            mm(ps[:, 3 + m, :], const("head_ones"), buf1[:, m * 512:(m + 1) * 512], start=True, stop=True)\
                                .then_inc(s_qss, 1)
                    pe.wait_ge(s_qc, pr + 1)
                    for t in range(4):
                        for k in range(KC):
                            last = mm(ps[:, 7, t * P:(t + 1) * P], hT[:, k, META + t * P:META + (t + 1) * P], w[:, k, 2, :],
                                      start=(k == 0), stop=(k == KC - 1))
                    last.then_inc(s_qkv, 1)
                    pe.drain().then_inc(freed[s], 1)
                    pe.wait_ge(s_kvc, pr * 2 + 2)
                    for hh in range(2):
                        h = h0 + hh
                        lo = hh * HD
                        if fox:
                            pe.wait_ge(s_fm, 2 * i + hh + 1)
                        for t in range(4):
                            n = P * (t + 1)
                            z = ps[:, [0, 0, 1, 2][t], (P if t == 1 else 0):(P if t == 1 else 0) + n]
                            last = mm(z, qT[lo:lo + HD, t * P:(t + 1) * P], kT[lo:lo + HD, 0:n], start=True, stop=not fox)
                            if fox:
                                mm(z, FL[lo:lo + HD, t * P:(t + 1) * P], FR[lo:lo + HD, 0:n], start=False, stop=True)
                                last = mm(z[:, t * P:n], ident, const("after"), start=False, stop=True, skip_group_check=True)
                        last.then_inc(s_z, 1)
                        pe.wait_ge(s_p, h + 1)
                        for (q, k), b in BLOCK_AT.items():
                            at = TILE_AT[q] + k * P
                            dst = ps[:, 3, b * P:(b + 1) * P] if b < 4 else \
                                ps[:, 4 + (b - 4) // 3, (b - 4) % 3 * P:(b - 4) % 3 * P + P]
                            last = nc.tensor.transpose(dst, buf2[:, at:at + P], ident)
                        last.then_inc(s_pt, 1)
                        pe.wait_ge(s_ptc, 2 * h + 2)
                        pe.wait_ge(s_o, h + 1)
                        for q in range(4):
                            for k in range(q + 1):
                                last = mm(ps[0:HD, 6, q * P:(q + 1) * P], vt[:, k, lo:lo + HD], PT[:, BLOCK_AT[q, k], :],
                                          start=(k == 0), stop=(k == q))
                        last.then_inc(s_pv, 1)

            norm(0)
            phase_end(pe, 2)
            ffn(0)
            phase_end(pe, 3)
            norm(1)
            phase_end(pe, 4)
            for k in range(KC):
                last = mm(ps[0:8, 7, :], wf[:, k, :], hT[:, k, META:TOK], start=(k == 0), stop=(k == KC - 1))
            last.then_inc(s_fp, 1)
            phase_end(pe, 5)
            pairs(2, False)
            pairs(3, True)
            phase_end(pe, 6)
            wo = [ring[s][:, :].rearrange("p (f n) -> p f n", f=4) for s in (4, 5)]
            for n, s in enumerate((4, 5)):
                pe.wait_ge(filled[s], u.take(s, 1)[0] + 16)
            for d in range(KC):
                for f in range(8):
                    last = mm(ps[:, d, :], wo[f // 4][:, f % 4, d * P:(d + 1) * P], oT[:, f, :], start=(f == 0), stop=(f == 7))
                last.then_inc(s_wo, 1)
            for s in (4, 5):
                pe.drain().then_inc(freed[s], 1)
            phase_end(pe, 7)
            norm(2)
            phase_end(pe, 8)
            ffn(1)
            phase_end(pe, 9)
            norm(3)
            phase_end(pe, 10)
            item = -1
            for n, (it, c0, m, wide, _) in enumerate(UNITS):
                if it != item:
                    if item >= 0:
                        pe.drain().then_inc(freed[2 + item], 1)
                    item = it
                    pe.wait_ge(filled[2 + it], u.take(2 + it, 1)[0] + 16)
                if n >= 4:
                    pe.wait_ge(s_p2c[n % 2], (n - 4) // 2 + 1)
                b = 2 * (n % 4)
                for k in range(KC):
                    flags = dict(start=(k == 0), stop=(k == KC - 1))
                    if wide is None:
                        t = n - 4
                        last = mm(ps[0:m, b, :], hT[:, k, TILE0[t]:TILE0[t] + m], w2(it)[:, k, :], **flags)
                    elif wide:
                        for g in range(2):
                            last = mm(ps[0:m, b + g, 0:264], w2(it)[:, k, c0:c0 + m], hT[:, k, g * 264:(g + 1) * 264], **flags)
                    else:
                        last = mm(ps[0:m, b, :], w2(it)[:, k, c0:c0 + m], hT[:, k, META:TOK], **flags)
                last.then_inc(s_p2, 1)
            pe.drain().then_inc(freed[5], 1)
            phase_end(pe, 11)

            pe.wait_ge(filled[2], u.take(2, 3)[0] + 48)
            for p in range(2):
                for g in range(2):
                    last = mm(ps[:, 2 * p + g, 0:264], w_a2[:, p * P:(p + 1) * P], aL[0:16, g * 264:(g + 1) * 264],
                              start=True, stop=True)
            last.then_inc(s_la, 1)
            pe.wait_ge(s_lq, 1)
            for k in range(2):
                last = mm(ps[:, 4, :], ones, eb[:, k, :], start=(k == 0), stop=(k == 1))
            for g in range(2):
                last = mm(ps[:, 6 + g, 0:264], ones, tmp[:, 0, g * 264:(g + 1) * 264], start=True, stop=True)
            last.then_inc(s_lss, 1)
            pe.wait_ge(s_kd, 1)
            for t in range(5):
                for p in range(2):
                    last = nc.tensor.transpose(ps[0:TILEN[t], t // 2, (t % 2) * 256 + p * P:(t % 2) * 256 + (p + 1) * P],
                                               kd[:, p, TILE0[t]:TILE0[t] + TILEN[t]], ident)
            last.then_inc(s_kt, 1)
            pe.wait_ge(s_ktc, 1)
            for n in range(N_CHUNK):
                t, lo, rows = (0, 0, META) if n == 0 else (1 + (n - 1) // 2, (n - 1) % 2 * CHUNK, CHUNK)
                if n >= 4:
                    pe.wait_ge(s_st, n - 3)
                for p in range(2):
                    last = mm(ps[:, 4 + n % 4, p * 256:(p + 1) * 256], kdtok[lo:lo + rows, t, p * P:(p + 1) * P],
                              gv[lo:lo + rows, t, p * 256:(p + 1) * 256], start=True, stop=True)
                last.then_inc(s_U, 1)
            phase_end(pe, 12)
            for h in range(GH):
                p, lo = h // 2, h % 2 * HD
                for b in range(NT):
                    last = mm(ps[:, 0, b * P:(b + 1) * P], km[lo:lo + HD, p, META + b * P:META + (b + 1) * P],
                              gq[lo:lo + HD, p, b * P:(b + 1) * P], start=True, stop=True)
                last.then_inc(s_at2, 1)
                pe.wait_ge(s_atm, h + 1)
                if h >= 1:
                    pe.wait_ge(s_gf, h)
                for b in range(NT):
                    mm(ps[:, 1, b * P:(b + 1) * P], gv[:, 1 + b, h * P:(h + 1) * P], attS[:, b, :], start=(b == 0), stop=True,
                       skip_group_check=True)
                for n in range(N_CHUNK):
                    last = mm(ps[:, 1, n * CHUNK:(n + 1) * CHUNK], states[lo:lo + HD, p, n + 1, :],
                              gq[lo:lo + HD, p, n * CHUNK:(n + 1) * CHUNK], start=False, stop=True, skip_group_check=True)
                last.then_inc(s_go, 1)
                pe.wait_ge(s_gsq, h + 1)
                mm(ps[:, 2, :], ones, osq, start=True, stop=True).then_inc(s_gss, 1)
            phase_end(pe, 13)

            NU = 0
            for h in range(GH):
                for kind in range(3):
                    b = 2 * (NU % 3)
                    if NU >= 3:
                        pe.wait_ge(s_mb, NU - 2)
                    for k in range(2 if kind < 2 else 1):
                        if kind == 0:
                            last = mm(ps[:, b, :], w_qb[:, k, h * 192:h * 192 + P], ql[:, k, :], start=(k == 0), stop=(k == 1))
                        elif kind == 1:
                            last = mm(ps[0:ROPE, b, :], w_qb[:, k, h * 192 + P:h * 192 + 192], ql[:, k, :], start=(k == 0), stop=(k == 1))
                        else:
                            for g in range(2):
                                last = mm(ps[:, b + g, 0:264], w_kvb[:, h * 256:h * 256 + P], kv[:, g * 264:(g + 1) * 264],
                                          start=True, stop=True)
                    last.then_inc(s_mz, 1)
                    NU += 1
            for t in range(5):
                if t >= 2:
                    pe.wait_ge(s_mtc, t - 1)
                mm(ps[0:TILEN[t], 6 + t % 2, :], kv[:, TILE0[t]:TILE0[t] + TILEN[t]],
                   w_kvb.rearrange("p (h n) -> p h n", h=GH)[:, :, P:2 * P], start=True, stop=True).then_inc(s_mt, 1)
            phase_end(pe, 14)

            def scores(un):
                h, t = un // NT, un % NT
                b = 2 * (un % 2)
                q0 = t * P
                for first, (lhs, rhs) in enumerate(((qn[:, h, q0:q0 + P], kn[:, h, :]), (qr[:, h, q0:q0 + P], kr[0:ROPE, :]))):
                    mm(ps[:, b, 512 - META:512], lhs, rhs[:, 0:META], start=(first == 0), stop=(first == 1))
                    last = mm(ps[:, b + 1, 0:P * (t + 1)], lhs, rhs[:, META:META + P * (t + 1)], start=(first == 0), stop=(first == 1))
                last.then_inc(s_mz, 1)
            scores(0)
            for un in range(GH * NT):
                h, t = un // NT, un % NT
                if un + 1 < GH * NT:
                    if un >= 1:
                        pe.wait_ge(s_me, un)
                    scores(un + 1)
                pe.wait_ge(s_mp, un + 1)
                src = PB[un % 2]
                nc.tensor.transpose(ps[0:META, 5, 0:P], src[:, 0:META], ident)
                for b in range(t + 1):
                    last = nc.tensor.transpose(ps[:, 4, b * P:(b + 1) * P], src[:, META + b * P:META + (b + 1) * P], ident)
                last.then_inc(s_mt, 1)
                pe.wait_ge(s_mtc, 5 + un + 1)
                if un >= 2:
                    pe.wait_ge(s_mo, un - 1)
                dst = ps[:, 6 + un % 2, 0:P]
                mm(dst, mv[0:META, 0, h * P:(h + 1) * P], mPT[0:META, 0, :], start=True, stop=False)
                for b in range(t + 1):
                    last = mm(dst, mv[:, 1 + b, h * P:(h + 1) * P], mPT[:, 1 + b, :], start=False, stop=(b == t))
                last.then_inc(s_mpv, 1)
            phase_end(pe, 15)
            u.take(0, 0), u.take(1, 0)
            pe.drain().then_inc(freed[2], 1)
            for n, s in enumerate((4, 5)):
                pe.wait_ge(filled[s], u.take(s, 1)[0] + 16)
            wo = [ring[s][:, :].rearrange("p (f n) -> p f n", f=4) for s in (4, 5)]
            for t in range(NT):
                b = 4 * (t % 2)
                if t >= 2:
                    pe.wait_ge(s_h2, t - 1)
                for k in range(KC):
                    last = nc.tensor.transpose(ps[:, b + k // 4, (k % 4) * P:(k % 4 + 1) * P],
                                               xT[:, k, META + t * P:META + (t + 1) * P], ident)
                last.then_inc(s_xr, 1)
                for g in range(2):
                    for f in range(8):
                        last = mm(ps[:, b + 2 + g, :], o2[:, f, t * P:(t + 1) * P], wo[f // 4][:, f % 4, g * 512:(g + 1) * 512],
                                  start=(f == 0), stop=(f == 7))
                last.then_inc(s_xr, 1)
            for s in (4, 5):
                pe.drain().then_inc(freed[s], 1)
            phase_end(pe, 16)
            for k in range(KC):
                if k == 0:
                    pe.wait_ge(s_un, NT)
                for t in range(NT):
                    last = nc.tensor.transpose(ps[:, k, t * P:(t + 1) * P], u2[:, t, k * P:(k + 1) * P], ident)
                last.then_inc(s_ut, 1)
            pe.wait_ge(s_utc, KC)
            pe.wait_ge(filled[3], u.take(3, 3)[0] + 48)
            for t in range(NT):
                for k in range(KC):
                    last = mm(ps[:, 0, t * 72:(t + 1) * 72], uT[:, k, t * P:(t + 1) * P], wr[:, k, :],
                              start=(k == 0), stop=(k == KC - 1))
            last.then_inc(s_lg, 1)
            for s in (0, 1, 3):
                pe.drain().then_inc(freed[s], 1)
            pe.wait_ge(s_M, 1)
            for t in range(NT + 1):
                for q in range(min(t + 1, NT)):
                    last = mm(ps[:, 1, t * NE:(t + 1) * NE], const("strict_t") if q == t else ones, Mh[:, q, :],
                              start=(q == 0), stop=(q == min(t, NT - 1)))
            last.then_inc(s_rk, 1)
            pe.wait_ge(s_pos, 1)
            for w in range(2):
                for n in range(2 * NT):
                    last = mm(ps[0:CAP, 2 + w, 0:TAB], slot_hot[w][:, n, :], block_hot[:, n, :], start=(n == 0), stop=(n == 2 * NT - 1))
            last.then_inc(s_tb, 1)
            pe.wait_ge(s_be, 1)
            nc.tensor.transpose(ps[0:1, 4, 0:P], expert_col, ident).then_inc(s_tb, 1)
            phase_end(pe, 17)
            phase_end(pe, 18)

            pe.drain().then_inc(s_mg, 2)
            pe.drain().then_inc(s_mu, 2)
            pe.drain().then_inc(s_my, 2)
            n_more = pe.value_load(pairs_ix[0:1, 1:2], min_val=1, max_val=MAX_PAIRS - 1)
            first = [u.take(s, 1)[0] for s in range(N_SLOT)]

            def turn_rows(j):
                for k in range(KC):
                    last = nc.tensor.transpose(ps[:, 4 + j, k * CAP:(k + 1) * CAP],
                                               xs[j].rearrange("p (m k) -> p k m", k=KC)[:, k, :], ident[0:CAP, 0:CAP])
                last.then_inc(s_xt, 1)

            def gate_up(j, n, i16, rows, hidden=None):
                pe.wait_ge(s_xtc, n)
                for g in range(2):
                    pe.wait_ge(filled[3 * j + g], i16 + (first[3 * j + g] + 16))
                w = [ring[3 * j + g][:, :].rearrange("p (k n) -> p k n", k=KC) for g in range(2)]
                for k in range(KC):
                    if k == KC - 1:
                        if rows is not None:
                            pe.wait_ge(s_gat[1 - j], rows)
                        if hidden is not None:
                            pe.wait_ge(s_ha, hidden)
                    for g in range(2):
                        last = mm(ps[g * CAP:(g + 1) * CAP, j, :], xsT[j][:, k, :], w[g][:, k, :], start=(k == 0), stop=(k == KC - 1))
                        if k == KC - 1:
                            last.then_inc((s_mg, s_mu)[g], 1)

            def turn_hidden(j, n):
                if n is not None:
                    pe.wait_ge(s_ha, n)
                for c in range(4):
                    last = nc.tensor.transpose(ps[:, 6 + j, c * CAP:(c + 1) * CAP], hrow[j][:, c * P:(c + 1) * P],
                                               ident[0:CAP, 0:CAP])
                last.then_inc(s_ta, 1)

            def down(j, n, i16):
                pe.wait_ge(filled[3 * j + 2], i16 + (first[3 * j + 2] + 16))
                pe.wait_ge(s_hd, n)
                w = ring[3 * j + 2][:, :].rearrange("p (f n) -> p f n", f=4)
                for c in range(4):
                    for g in range(2):
                        last = mm(ps[g * CAP:(g + 1) * CAP, 2 + j, :], hid[j][:, c, :], w[:, c, g * 512:(g + 1) * 512],
                                  start=(c == 0), stop=(c == 3))
                last.then_inc(s_my, 1)

            pe.wait_ge(s_gat[0], 16)
            turn_rows(0)
            gate_up(0, 1, 0, 16)
            turn_rows(1)
            with pe.Fori(0, n_more) as i:
                gate_up(1, i * 2 + 2, i * 16, i * 16 + 32, i * 2 + 1)
                turn_hidden(0, None)
                turn_rows(0)
                down(0, i * 2 + 1, i * 16)
                gate_up(0, i * 2 + 3, i * 16 + 16, i * 16 + 32, i * 2 + 2)
                turn_hidden(1, None)
                turn_rows(1)
                down(1, i * 2 + 2, i * 16)
            before = pe.snap(n_more * 2)
            before16 = pe.snap(n_more * 16)
            gate_up(1, before + 2, before16, None, before + 1)
            turn_hidden(0, None)
            down(0, before + 1, before16)
            pe.wait_ge(s_ha, before + 2)
            mm(ps[:, 7, 0:P], ident, ident, start=True, stop=True)
            turn_hidden(1, None)
            down(1, before + 2, before16)
            phase_end(pe, 19)
            phase_end(pe, 20)
            phase_end(pe, 21)
            phase_end(pe, 22)

        @block.scalar
        def _(act):
            av = nc.scalar.activation
            act.wait_ge(s_in, 64)
            av(c_exp, col("c"), ACT.Exp, scale=-1.0).then_inc(s_cexp, 1)
            phase_end(act, 1)

            steps = [0]

            def norm(r):
                t0, t1 = HALVES[r][0][0], TOK
                for k in range(KC):
                    if k >= 2:
                        act.wait_ge(s_ss, KC * r + k - 1)
                    av(tmp[:, k % 2, t0:t1], xT[:, k, t0:t1], ACT.Square).then_inc(s_sq, 1)
                act.wait_ge(s_ss, KC * (r + 1))
                for b, (h0, w) in enumerate(HALVES[r]):
                    last = av(rstd[:, h0:h0 + w], ps[:, b, 0:w], ACT.Sqrt, scale=1.0 / D, bias=eps_col[:, 0:1])
                last.then_inc(s_std, 1)
                for k in range(KC):
                    act.wait_ge(s_nx, KC * r + k + 1)
                    if r < 3:
                        av(hT[:, k, t0:t1], hT[:, k, t0:t1], ACT.Identity, scale=scale[r][:, k:k + 1],
                           bias=modT[:, 24 * r + k:24 * r + k + 1])
                    else:
                        av(hT[:, k, t0:t1], hT[:, k, t0:t1], ACT.Copy, scale=col("mix_norm_2", k))

            def ffn(r):
                def chunk(j, n):
                    act.wait_ge(s_gu, n + 1)
                    act.wait_ge(s_hid, n + 2 * r + 1)
                    av(eb[:, j, :], ps[:, 2 * j, :], ACT.Exp, scale=-1.0).then_inc(s_ge, 1)
                with act.Fori(0, FC // 2) as i:
                    for j in range(2):
                        chunk(j, FC * r + i * 2 + j)

            norm(0)
            phase_end(act, 2)
            ffn(0)
            phase_end(act, 3)
            norm(1)
            phase_end(act, 4)
            act.wait_ge(s_f1, 1)
            av(fB, fA, ACT.Abs).then_inc(s_act, 1)
            act.wait_ge(s_act, 1)
            av(fB, fB, ACT.Exp, scale=-1.0).then_inc(s_act, 1)
            act.wait_ge(s_act, 2)
            av(fB, fB, ACT.Ln, bias=1.0).then_inc(s_f1, 1)
            phase_end(act, 5)

            SBA = 3
            with act.Fori(0, 4) as i:
                act.wait_ge(s_qkv, i * 3 + 1)
                av(qT, ps[:, 7, :], ACT.Copy, scale=HD ** -0.5).then_inc(s_qc, 1)
                for hh in range(2):
                    h = i * 2 + hh
                    act.wait_ge(s_z, h + 1)
                    av(buf1[:, 0:768].rearrange("p (b n) -> p b n", b=2), ps[:, 0:2, 0:384], ACT.Abs)
                    av(buf1[:, 768:TRI], ps[:, 2, :], ACT.Abs).then_inc(s_act, 1)
                    act.wait_ge(s_act, i * 4 + 3 + 2 * hh)
                    av(buf1, buf1, ACT.Exp, scale=-1.0).then_inc(s_act, 1)
                    act.wait_ge(s_act, i * 4 + 4 + 2 * hh)
                    av(buf1, buf1, ACT.Ln, bias=1.0).then_inc(s_sp, 1)
                    act.wait_ge(s_zz, h + 1)
                    av(buf2, buf1, ACT.Exp).then_inc(s_p, 1)
                    act.wait_ge(s_pt, h + 1)
                    av(PT[:, 4:10, :].rearrange("p (b m) q -> p b (m q)", b=2), ps[:, 4:6, 0:384], ACT.Copy).then_inc(s_ptc, 1)
            with act.Fori(0, 4) as i:
                for m in range(2):
                    act.wait_ge(s_qkv, 12 + i * 3 + m + 1)
                    av(buf1[:, m * 512:(m + 1) * 512], ps[:, 7 - m, :], ACT.Square).then_inc(s_qsq, 1)
                for m in range(2):
                    act.wait_ge(s_qss, 2 * i + m + 1)
                    av(buf1[:, m * 512:(m + 1) * 512], ps[:, 3 + m, :], ACT.Sqrt, scale=1.0 / HD, bias=eps_col[:, 0:1])\
                        .then_inc(s_qstd, 1)
                for hh in range(2):
                    h = i * 2 + hh + 8
                    act.wait_ge(s_mx, i * 2 + hh + 1)
                    for t in range(4):
                        n = P * (t + 1)
                        z = ps[:, [0, 0, 1, 2][t], (P if t == 1 else 0):(P if t == 1 else 0) + n]
                        last = av(buf2[:, TILE_AT[t]:TILE_AT[t] + n], z, ACT.Exp, bias=fox_s[:, t:t + 1],
                                  accum_out=fox_s[:, 4 + t:5 + t])
                    last.then_inc(s_e, 1)
                    act.wait_ge(s_pt, h + 1)
                    av(PT[:, 4:10, :].rearrange("p (b m) q -> p b (m q)", b=2), ps[:, 4:6, 0:384], ACT.Copy).then_inc(s_ptc, 1)
            phase_end(act, 6)
            phase_end(act, 7)
            norm(2)
            phase_end(act, 8)
            ffn(1)
            phase_end(act, 9)
            norm(3)
            phase_end(act, 10)
            for n in range(1, len(UNITS), 2):
                act.wait_ge(s_p2, n + 1)
                av(unit_dst(n), unit_psum(n), ACT.Copy, scale=HD ** -0.5 if n == 1 else 1.0).then_inc(s_p2c[1], 1)
            phase_end(act, 11)
            av(eb[:, :, :], ql, ACT.Square)
            av(tmp[:, 0, :], kv, ACT.Square).then_inc(s_lq, 1)
            act.wait_ge(s_dt, 1)
            steps = [2 + 4 * 4]

            def link(ins):
                ins.then_inc(s_act, 1)
                steps[0] += 1
                act.wait_ge(s_act, steps[0])
            link(av(km, Sc, ACT.Abs))
            link(av(km, km, ACT.Exp, scale=-1.0))
            av(km, km, ACT.Ln, bias=1.0).then_inc(s_dsp, 1)
            act.wait_ge(s_lss, 1)
            av(eb[:, 0, :], ps[:, 4, :], ACT.Sqrt, scale=1.0 / 256, bias=eps_col[:, 0:1])
            av(halves(tmp[:, 0, :]), ps[:, 6:8, 0:264], ACT.Sqrt, scale=1.0 / P, bias=eps_col[:, 0:1]).then_inc(s_lstd, 1)
            act.wait_ge(s_S, 1)
            av(km, Sc, ACT.Exp, scale=1.0 / 16).then_inc(s_dx, 1)
            av(glst[:, 0:18].rearrange("p (c n) -> p c n", c=2), Sc[:, :, META - 1::CHUNK], ACT.Exp, scale=-1.0 / 16).then_inc(s_dx, 1)
            act.wait_ge(s_S, 2)
            av(eb[:, :, :], Sc[:, :, META:TOK], ACT.Exp, scale=-1.0 / 16).then_inc(s_dx, 1)
            act.wait_ge(s_S, 3)
            av(kd, kd, ACT.Exp, scale=1.0 / 16).then_inc(s_dx, 1)
            act.wait_ge(s_kt, 1)
            av(kdtok[:, 1:3, :], flat[:, 256:768].rearrange("p (t n) -> p t n", t=2), ACT.Copy)
            av(kdtok[:, 3:5, :], flat[:, 768:1280].rearrange("p (t n) -> p t n", t=2), ACT.Copy)
            av(kdtok[0:META, 0, :], ps[0:META, 0, 0:256], ACT.Copy).then_inc(s_ktc, 1)
            phase_end(act, 12)
            for h in range(GH):
                if h >= 1:
                    act.wait_ge(s_gf, h)
                av(sil, gr[:, h, :], ACT.Exp, scale=-1.0).then_inc(s_gstd, 1)
                act.wait_ge(s_go, h + 1)
                av(osq, ps[:, 1, :], ACT.Square).then_inc(s_gsq, 1)
                act.wait_ge(s_gss, h + 1)
                av(orst, ps[:, 2, :], ACT.Sqrt, scale=1.0 / P, bias=eps_col[:, 0:1]).then_inc(s_gstd, 1)
            phase_end(act, 13)
            for t in range(5):
                act.wait_ge(s_mt, t + 1)
                av(mv[0:TILEN[t], t, :], ps[0:TILEN[t], 6 + t % 2, :], ACT.Copy).then_inc(s_mtc, 1)
            phase_end(act, 14)
            for un in range(GH * NT):
                t = un % NT
                n = META + P * (t + 1)
                act.wait_ge(s_mb, 12 + un + 1)
                av(PB[un % 2][:, 0:n], mla_z(un), ACT.Exp, bias=glst[:, 20 + un % 2:21 + un % 2],
                   accum_out=glst[:, 22 + un % 2:23 + un % 2]).then_inc(s_me, 1)
                act.wait_ge(s_mt, 5 + un + 1)
                av(mPT[0:META, 0, :], ps[0:META, 5, 0:P], ACT.Copy)
                av(mPT[:, 1:2 + t, :].rearrange("p b q -> p (b q)"), ps[:, 4, 0:P * (t + 1)], ACT.Copy).then_inc(s_mtc, 1)
            phase_end(act, 15)
            for t in range(NT):
                b = 4 * (t % 2)
                act.wait_ge(s_xr, 2 * t + 1)
                av(h2[:, t, :].rearrange("p (b n) -> p b n", b=2), ps[:, b:b + 2, :], ACT.Copy).then_inc(s_xrc, 1)
                act.wait_ge(s_rn, t + 1)
                av(glst[:, 31:32], glst[:, 29:30], ACT.Sqrt).then_inc(s_rnq, 1)
            phase_end(act, 16)
            act.wait_ge(s_rx, 1)
            av(rx[:, 0:NT * NG], rx[:, 0:NT * NG], ACT.Exp)
            av(rx[:, NT * NG:NT * NG + NT], rx[:, NT * NG:NT * NG + NT], ACT.Exp).then_inc(s_rx, 1)
            phase_end(act, 17)
            act.drain().then_inc(s_ysf, 2)
            n_more = act.value_load(pairs_ix[0:1, 1:2], min_val=1, max_val=MAX_PAIRS - 1)
            phase_end(act, 18)

            def rows_in(j, n):
                act.wait_ge(s_xt, n)
                av(xsT[j].rearrange("p k s -> p (k s)"), ps[:, 4 + j, :], ACT.Copy).then_inc(s_xtc, 1)

            def gate_exp(j, n):
                act.wait_ge(s_mg, n + 2)
                av(sg[j], ps[0:CAP, j, :], ACT.Exp, scale=-1.0).then_inc(s_eg, 1)

            def rows_out(j, n):
                act.wait_ge(s_my, n + 2)
                act.wait_ge(s_ysf, n)
                for g in range(2):
                    last = av(ys[j][:, g * 512:(g + 1) * 512], ps[g * CAP:(g + 1) * CAP, 2 + j, :], ACT.Copy)
                last.then_inc(s_yc, 1)
            rows_in(0, 1)
            gate_exp(0, 1)
            rows_in(1, 2)
            with act.Fori(0, n_more) as i:
                gate_exp(1, i * 2 + 2)
                rows_in(0, i * 2 + 3)
                rows_out(0, i * 2 + 1)
                gate_exp(0, i * 2 + 3)
                rows_in(1, i * 2 + 4)
                rows_out(1, i * 2 + 2)
            before = act.snap(n_more * 2)
            gate_exp(1, before + 2)
            rows_out(0, before + 1)
            rows_out(1, before + 2)
            phase_end(act, 19)
            phase_end(act, 20)
            phase_end(act, 21)
            for t in range(NT):
                act.wait_ge(s_rn, NT + t + 1)
                av(glst[:, 31:32], glst[:, 29:30], ACT.Sqrt).then_inc(s_rnq, 1)
            phase_end(act, 22)

        @block.vector
        def _(dve):
            v = nc.vector
            steps = [0]
            vec_sem = [s_vec]
            rn = [0]

            def link(ins):
                ins.then_inc(vec_sem[0], 1)
                steps[0] += 1
                dve.wait_ge(vec_sem[0], steps[0])

            def row_norm(t):
                link(v.tensor_tensor_reduce(out=sq_row, in0=h2[:, t, :], in1=h2[:, t, :], scale=1.0, scalar=0.0, op0=ALU.mult,
                                            op1=ALU.add, accum_out=glst[:, 28:29]))
                v.tensor_scalar(glst[:, 29:30], glst[:, 28:29], 1.0 / D, EPS, ALU.mult, ALU.add).then_inc(s_rn, 1)
                rn[0] += 1
                dve.wait_ge(s_rnq, rn[0])
                link(v.reciprocal(glst[:, 30:31], glst[:, 31:32]))

            v.memset(eps_col[:, :], EPS).then_inc(s_o, 1)
            for k in range(KC):
                dve.wait_ge(s_tr, k + 1)
                v.tensor_copy(xT[:, k, META:TOK], ps[:, k, :]).then_inc(s_trc, 1)
            dve.wait_ge(s_tr, KC + 1)
            v.tensor_copy(xT[:, :, 0:META], ps[:, 0, 0:KC * META].rearrange("p (k t) -> p k t", k=KC))
            dve.wait_ge(s_cexp, 1)
            link(v.tensor_scalar(c_act, c_exp, 1.0, None, ALU.add))
            link(v.reciprocal(c_exp, c_act))
            v.tensor_tensor(c_act, c_exp, col("c"), ALU.mult).then_inc(s_cact, 1)
            phase_end(dve, 1)

            dve.wait_ge(s_mod, 1)
            link(v.tensor_tensor(modT[:, :], ps[:, 1, 0:72], col("b_mod"), ALU.add))
            for r, g in enumerate(("g_ffn1", "g_mix", "g_ffn2")):
                v.scalar_tensor_tensor(out=scale[r], in0=modT[:, 24 * r + 8:24 * r + 16], scalar=1.0, in1=col(g),
                                       op0=ALU.add, op1=ALU.mult)
                half = 1.0 if r == 1 else 0.5
                v.tensor_scalar(gate[r], modT[:, 24 * r + 16:24 * r + 24], 1.0, half, ALU.add, ALU.mult)
            v.tensor_scalar(gqs[:, :], col("g_q"), HD ** -0.5, None, ALU.mult)

            def norm(r):
                t0, t1 = HALVES[r][0][0], TOK
                dve.wait_ge(s_std, r + 1)
                link(v.reciprocal(rstd[:, t0:t1], rstd[:, t0:t1]))
                for k in range(KC):
                    v.tensor_tensor(hT[:, k, t0:t1], xT[:, k, t0:t1], rstd[:, t0:t1], ALU.mult).then_inc(s_nx, 1)

            def ffn(r):
                v.tensor_copy(fox_s[:, 12:13], eps_col[:, 0:1]).then_inc(s_hid, 1)
                v.tensor_copy(fox_s[:, 13:14], eps_col[:, 0:1]).then_inc(s_hid, 1)
                at = steps[0]
                with dve.Fori(0, FC // 2) as i:
                    for j in range(2):
                        k = at + i * 6 + 3 * j
                        dve.wait_ge(s_ge, FC * r + i * 2 + j + 1)
                        v.tensor_scalar(eb[:, j, :], eb[:, j, :], 1.0, None, ALU.add).then_inc(s_vec, 1)
                        dve.wait_ge(s_vec, k + 1)
                        v.reciprocal(eb[:, j, :], eb[:, j, :]).then_inc(s_vec, 1)
                        dve.wait_ge(s_vec, k + 2)
                        v.tensor_tensor(eb[:, j, :], ps[:, 2 * j, :], eb[:, j, :], ALU.mult).then_inc(s_vec, 1)
                        dve.wait_ge(s_vec, k + 3)
                        v.tensor_tensor(aT[:, bass.ds(i * 2 + j, 1), :], ps[:, 2 * j + 1:2 * j + 2, :],
                                        eb[:, j:j + 1, :], ALU.mult).then_inc(s_hid, 1)
                steps[0] += 3 * FC
                for half in range(2):
                    dve.wait_ge(s_dn, 2 * r + half + 1)
                    for d in range(4):
                        k = 4 * half + d
                        v.scalar_tensor_tensor(out=xT[:, k, META:TOK], in0=ps[:, (4 if half == 0 else 0) + d, :],
                                               scalar=gate[2 * r][:, k:k + 1], in1=xT[:, k, META:TOK],
                                               op0=ALU.mult, op1=ALU.add)

            norm(0)
            phase_end(dve, 2)
            ffn(0)
            phase_end(dve, 3)
            norm(1)
            phase_end(dve, 4)
            dve.wait_ge(s_fp, 1)
            v.tensor_scalar(fA, ps[0:8, 7, :], bf[:, 0:1], -1.0, ALU.add, ALU.mult).then_inc(s_f1, 1)
            v.memset(FL, 0.0)
            v.memset(FR, 0.0).then_inc(s_fl, 1)
            dve.wait_ge(s_f1, 2)
            link(v.scalar_tensor_tensor(out=fA, in0=fA, scalar=0.0, in1=fB, op0=ALU.max, op1=ALU.add))
            link(v.memset(fB, 1.0))
            link(v.tensor_tensor_scan(Fc, fB, fA, 0.0, ALU.mult, ALU.add))
            for lo in (0, HD):
                v.memset(FL[lo + 32:lo + 40, :], 1.0)
                v.memset(FR[lo:lo + 8, :], 1.0)
            phase_end(dve, 5)

            at = steps[0]
            with dve.Fori(0, 4) as i:
                dve.wait_ge(s_qkv, i * 3 + 2)
                v.tensor_copy(kT, ps[:, 6, :]).then_inc(s_kvc, 1)
                dve.wait_ge(s_qkv, i * 3 + 3)
                v.tensor_copy(vt.rearrange("p t n -> p (t n)"), ps[:, 7, :]).then_inc(s_kvc, 1)
                for hh in range(2):
                    h = i * 2 + hh
                    k = at + i * 4 + 2 * hh
                    dve.wait_ge(s_sp, h + 1)
                    v.scalar_tensor_tensor(out=buf1[:, 0:768].rearrange("p (b n) -> p b n", b=2), in0=ps[:, 0:2, 0:384],
                                           scalar=0.0, in1=buf1[:, 0:768].rearrange("p (b n) -> p b n", b=2),
                                           op0=ALU.max, op1=ALU.add)
                    v.scalar_tensor_tensor(out=buf1[:, 768:TRI], in0=ps[:, 2, :], scalar=0.0, in1=buf1[:, 768:TRI],
                                           op0=ALU.max, op1=ALU.add).then_inc(s_vec, 1)
                    dve.wait_ge(s_vec, k + 1)
                    v.tensor_tensor_scan(buf2[:, ::-1], const("resets")[:, ::-1], buf1[:, ::-1], 0.0, ALU.mult, ALU.add)\
                        .then_inc(s_vec, 1)
                    dve.wait_ge(s_vec, k + 2)
                    v.tensor_tensor(buf1[:, 0:768].rearrange("p (b n) -> p b n", b=2), ps[:, 0:2, 0:384],
                                    buf2[:, 0:768].rearrange("p (b n) -> p b n", b=2), ALU.subtract)
                    v.tensor_tensor(buf1[:, 768:TRI], ps[:, 2, :], buf2[:, 768:TRI], ALU.subtract).then_inc(s_zz, 1)
                    dve.wait_ge(s_pt, h + 1)
                    v.tensor_tensor(PT[:, 0:4, :], ps[:, 3, :].rearrange("p (b q) -> p b q", b=4),
                                    const("strict_t").unsqueeze(1).to_broadcast([P, 4, P]), ALU.mult).then_inc(s_ptc, 1)
                    dve.wait_ge(s_pv, h + 1)
                    v.tensor_copy(oT[hh * HD:(hh + 1) * HD, bass.ds(i, 1), :], ps[0:HD, 6:7, :]).then_inc(s_o, 1)
            at += 16
            with dve.Fori(0, 4) as i:
                for m, (dst, g) in enumerate(((qT, gqs[:, :]), (kT, col("g_k")))):
                    dve.wait_ge(s_qstd, 2 * i + m + 1)
                    v.reciprocal(buf1[:, m * 512:(m + 1) * 512], buf1[:, m * 512:(m + 1) * 512]).then_inc(s_vec, 1)
                    dve.wait_ge(s_vec, at + i * 4 + m + 1)
                    v.scalar_tensor_tensor(out=dst, in0=ps[:, 7 - m, :], scalar=g[:, bass.ds(i, 1)],
                                           in1=buf1[:, m * 512:(m + 1) * 512], op0=ALU.mult, op1=ALU.mult).then_inc((s_qc, s_kvc)[m], 1)
                dve.wait_ge(s_qkv, 12 + i * 3 + 3)
                v.tensor_copy(vt.rearrange("p t n -> p (t n)"), ps[:, 7, :]).then_inc(s_kvc, 1)
                for hh in range(2):
                    h = i * 2 + hh
                    dve.wait_ge(s_z, h + 8)
                    lo = hh * HD
                    v.tensor_scalar(FL[lo:lo + 8, :], Fc, ident[0:8, bass.ds(h, 1)], -1.0, ALU.mult, ALU.mult)
                    v.tensor_scalar(FR[lo + 32:lo + 40, :], Fc, ident[0:8, bass.ds(h, 1)], None, ALU.mult).then_inc(s_fm, 1)
                    dve.wait_ge(s_z, h + 9)
                    for t in range(4):
                        n = P * (t + 1)
                        z = ps[:, [0, 0, 1, 2][t], (P if t == 1 else 0):(P if t == 1 else 0) + n]
                        last = v.tensor_reduce(fox_s[:, t:t + 1], z, AX_X, ALU.max, negate=True)
                    last.then_inc(s_mx, 1)
                    dve.wait_ge(s_e, h + 1)
                    v.reciprocal(fox_s[:, 8:12], fox_s[:, 4:8]).then_inc(s_vec, 1)
                    dve.wait_ge(s_vec, at + i * 4 + 3 + hh)
                    for t in range(4):
                        n = P * (t + 1)
                        b = buf2[:, TILE_AT[t]:TILE_AT[t] + n]
                        last = v.tensor_scalar(b, b, fox_s[:, 8 + t:9 + t], None, ALU.mult)
                    last.then_inc(s_p, 1)
                    dve.wait_ge(s_pt, h + 9)
                    v.tensor_copy(PT[:, 0:4, :].rearrange("p b q -> p (b q)"), ps[:, 3, :]).then_inc(s_ptc, 1)
                    dve.wait_ge(s_pv, h + 9)
                    v.tensor_copy(oT[hh * HD:(hh + 1) * HD, bass.ds(i + 4, 1), :], ps[0:HD, 6:7, :]).then_inc(s_o, 1)
            steps[0] += 32
            phase_end(dve, 6)
            for k in range(KC):
                dve.wait_ge(s_wo, k + 1)
                v.scalar_tensor_tensor(out=xT[:, k, META:TOK], in0=ps[:, k, :], scalar=gate[1][:, k:k + 1],
                                       in1=xT[:, k, META:TOK], op0=ALU.mult, op1=ALU.add)
            phase_end(dve, 7)
            norm(2)
            phase_end(dve, 8)
            ffn(1)
            phase_end(dve, 9)
            norm(3)
            phase_end(dve, 10)
            for n in range(0, len(UNITS), 2):
                dve.wait_ge(s_p2, n + 1)
                if n == 0:
                    v.tensor_scalar(unit_dst(n), unit_psum(n), HD ** -0.5, None, ALU.mult).then_inc(s_p2c[0], 1)
                else:
                    v.tensor_copy(unit_dst(n), unit_psum(n)).then_inc(s_p2c[0], 1)
            phase_end(dve, 11)
            dve.wait_ge(s_la, 1)
            for p in range(2):
                last = v.tensor_scalar(halves(Sc[:, p, :]), ps[:, 2 * p:2 * p + 2, 0:264], col("gla_b_a_2", p), -1.0,
                                       ALU.add, ALU.mult)
            last.then_inc(s_dt, 1)
            v.tensor_copy(swap[0:32, :], kr[32:64, :])
            link(v.tensor_copy(swap[32:64, :], kr[0:32, :]))
            v.tensor_tensor(kr[0:ROPE, :], kr[0:ROPE, :], const("rope_cos")[0:ROPE, :], ALU.mult)
            link(v.tensor_tensor(swap[0:ROPE, :], swap[0:ROPE, :], const("rope_sin")[0:ROPE, :], ALU.mult))
            v.tensor_tensor(kr[0:ROPE, :], kr[0:ROPE, :], swap[0:ROPE, :], ALU.add)
            dve.wait_ge(s_dsp, 1)
            link(v.scalar_tensor_tensor(out=kd, in0=Sc, scalar=0.0, in1=km, op0=ALU.max, op1=ALU.add))
            for p in range(2):
                last = v.tensor_tensor_scan(Sc[:, p, :], const("chunk_resets"), kd[:, p, :], 0.0, ALU.mult, ALU.add)
            last.then_inc(s_S, 1)
            dve.wait_ge(s_lstd, 1)
            v.reciprocal(eb[:, 0, :], eb[:, 0, :])
            link(v.reciprocal(tmp[:, 0, :], tmp[:, 0, :]))
            for k in range(2):
                v.scalar_tensor_tensor(out=ql[:, k, :], in0=ql[:, k, :], scalar=col("mla_q_norm_2", k), in1=eb[:, 0, :],
                                       op0=ALU.mult, op1=ALU.mult)
            v.scalar_tensor_tensor(out=kv, in0=kv, scalar=col("mla_kv_norm_2", 0), in1=tmp[:, 0, :],
                                   op0=ALU.mult, op1=ALU.mult).then_inc(s_S, 1)
            dve.wait_ge(s_S, 2)
            for p in range(2):
                v.tensor_scalar(kd[:, p, 0:META], Sc[:, p, 0:META], Sc[:, p, META - 1:META], None, ALU.subtract)
                ends = Sc[:, p, META - 1 + CHUNK::CHUNK].unsqueeze(2).to_broadcast([P, N_CHUNK, CHUNK])
                last = v.tensor_tensor(kd[:, p, META:].rearrange("p (n t) -> p n t", t=CHUNK),
                                       Sc[:, p, META:].rearrange("p (n t) -> p n t", t=CHUNK), ends, ALU.subtract)
            last.then_inc(s_S, 1)
            dve.wait_ge(s_dx, 1)
            v.tensor_tensor(km, km, gk, ALU.mult)
            dve.wait_ge(s_dx, 3)
            v.tensor_tensor(gq, gq, eb[:, :, :], ALU.mult)
            dve.wait_ge(s_dx, 4)
            v.tensor_tensor(kd, kd, gk, ALU.mult).then_inc(s_kd, 1)
            link(v.memset(states[:, :, 0, :], 0.0))
            for n in range(N_CHUNK):
                dve.wait_ge(s_U, n + 1)
                for p in range(2):
                    for g in range(2):
                        lo = g * HD
                        last = v.scalar_tensor_tensor(out=states[lo:lo + HD, p, n + 1, :], in0=states[lo:lo + HD, p, n, :],
                                                      scalar=glst[lo:lo + HD, 9 * p + n:9 * p + n + 1],
                                                      in1=ps[lo:lo + HD, 4 + n % 4, p * 256 + g * P:p * 256 + (g + 1) * P],
                                                      op0=ALU.mult, op1=ALU.add)
                last.then_inc(s_st, 1)
                dve.wait_ge(s_st, n + 1)
            phase_end(dve, 12)
            for h in range(GH):
                dve.wait_ge(s_at2, h + 1)
                v.tensor_tensor(attS, ps[:, 0, :].rearrange("p (b c) -> p b c", b=4),
                                const("chunk_causal").unsqueeze(1).to_broadcast([P, 4, P]), ALU.mult).then_inc(s_atm, 1)
                dve.wait_ge(s_gstd, 2 * h + 1)
                link(v.tensor_scalar(sil, sil, 1.0, None, ALU.add))
                link(v.reciprocal(sil, sil))
                link(v.tensor_tensor(sil, sil, gr[:, h, :], ALU.mult))
                dve.wait_ge(s_gstd, 2 * h + 2)
                link(v.reciprocal(orst, orst))
                link(v.tensor_tensor(sil, sil, orst, ALU.mult))
                v.scalar_tensor_tensor(out=o2[:, h, :], in0=ps[:, 1, :], scalar=col("gla_out_norm_2", h), in1=sil,
                                       op0=ALU.mult, op1=ALU.mult).then_inc(s_gf, 1)
            phase_end(dve, 13)
            NU = 0
            for h in range(GH):
                for kind in range(3):
                    b = 2 * (NU % 3)
                    dve.wait_ge(s_mz, NU + 1)
                    if kind == 0:
                        v.tensor_scalar(qn[:, h, :], ps[:, b, :], MLA_SCALE, None, ALU.mult).then_inc(s_mb, 1)
                    elif kind == 1:
                        cos, sin = (const(n)[0:ROPE, META:TOK] for n in ("rope_cos", "rope_sin"))
                        v.tensor_scalar(swap[0:32, 0:SEQ], ps[32:64, b, :], MLA_SCALE, None, ALU.mult)
                        v.tensor_scalar(swap[32:64, 0:SEQ], ps[0:32, b, :], MLA_SCALE, None, ALU.mult)
                        link(v.scalar_tensor_tensor(out=qr[:, h, :], in0=ps[0:ROPE, b, :], scalar=MLA_SCALE, in1=cos,
                                                    op0=ALU.mult, op1=ALU.mult))
                        link(v.tensor_tensor(swap[0:ROPE, 0:SEQ], swap[0:ROPE, 0:SEQ], sin, ALU.mult))
                        v.tensor_tensor(qr[:, h, :], qr[:, h, :], swap[0:ROPE, 0:SEQ], ALU.add).then_inc(s_mb, 1)
                        dve.wait_ge(s_mb, NU + 1)
                    else:
                        v.tensor_copy(halves(kn[:, h, :]), ps[:, b:b + 2, 0:264]).then_inc(s_mb, 1)
                    NU += 1
            phase_end(dve, 14)

            def mla_max(un):
                t = un % NT
                dve.wait_ge(s_mz, NU + un + 1)
                z = ps[0:CHUNK, 2 * (un % 2) + 1, P * t + CHUNK:P * (t + 1)]
                link(v.tensor_scalar(z, z, -1e30, None, ALU.add))
                v.tensor_reduce(glst[:, 20 + un % 2:21 + un % 2], mla_z(un), AX_X, ALU.max, negate=True).then_inc(s_mb, 1)
            mla_max(0)
            for un in range(GH * NT):
                h, t = un // NT, un % NT
                if un + 1 < GH * NT:
                    mla_max(un + 1)
                dve.wait_ge(s_me, un + 1)
                link(v.reciprocal(glst[:, 24:25], glst[:, 22 + un % 2:23 + un % 2]))
                n = META + P * (t + 1)
                v.tensor_scalar(PB[un % 2][:, 0:n], PB[un % 2][:, 0:n], glst[:, 24:25], None, ALU.mult).then_inc(s_mp, 1)
                dve.wait_ge(s_mpv, un + 1)
                v.tensor_copy(o2[:, 4 + h, t * P:(t + 1) * P], ps[:, 6 + un % 2, 0:P]).then_inc(s_mo, 1)
            phase_end(dve, 15)
            for t in range(NT):
                b = 4 * (t % 2)
                dve.wait_ge(s_xrc, t + 1)
                dve.wait_ge(s_xr, 2 * t + 2)
                v.tensor_tensor(h2[:, t, :].rearrange("p (b n) -> p b n", b=2), ps[:, b + 2:b + 4, :],
                                h2[:, t, :].rearrange("p (b n) -> p b n", b=2), ALU.add).then_inc(s_h2, 1)
                dve.wait_ge(s_h2, t + 1)
                row_norm(t)
                if t == 0:
                    dve.wait_ge(s_row, 16)
                v.scalar_tensor_tensor(out=u2[:, t, :], in0=h2[:, t, :], scalar=glst[:, 30:31], in1=gain_row,
                                       op0=ALU.mult, op1=ALU.mult).then_inc(s_un, 1)
                dve.wait_ge(s_un, t + 1)
            phase_end(dve, 16)
            for k in range(KC):
                dve.wait_ge(s_ut, k + 1)
                v.tensor_copy(uT[:, k, :], ps[:, k, :]).then_inc(s_utc, 1)

            dve.wait_ge(s_lg, 1)
            link(v.tensor_tensor(lg, ps[:, 0, 0:NT * 72].rearrange("p (t n) -> p t n", t=NT),
                                 bias_row.unsqueeze(1).to_broadcast([P, NT, 72]), ALU.add))
            glog, elog = lg[:, :, 0:NG], lg[:, :, NG:72]
            iota8 = const("iota8").unsqueeze(1).to_broadcast([P, NT, 8])

            def wide(ap):
                return ap.unsqueeze(2).to_broadcast([P, NT, 8])

            def best(src, top, hot):
                link(v.tensor_reduce(top, src, AX_X, ALU.max))
                link(v.tensor_tensor(t8, src, wide(top), ALU.is_equal))
                link(v.tensor_scalar(t8, t8, -16.0, 16.0, ALU.mult, ALU.add))
                link(v.tensor_tensor(t8, t8, iota8, ALU.add))
                link(v.tensor_reduce(t1, t8, AX_X, ALU.min))
                link(v.tensor_tensor(hot, iota8, wide(t1), ALU.is_equal))
            best(glog, gtop, ghot)
            link(v.tensor_tensor(rx[:, 0:NT * NG].rearrange("p (t n) -> p t n", t=NT), glog, wide(gtop), ALU.subtract))
            link(v.tensor_tensor(pick, elog.rearrange("p t (g e) -> p t g e", g=NG),
                                 ghot.unsqueeze(3).to_broadcast([P, NT, NG, 8]), ALU.mult))
            link(v.tensor_reduce(el, pick.rearrange("p t g e -> p t e g"), AX_X, ALU.add))
            best(el, top1, hot1)
            link(v.scalar_tensor_tensor(out=el, in0=hot1, scalar=-1e30, in1=el, op0=ALU.mult, op1=ALU.add))
            best(el, top2, hot2)
            v.tensor_tensor(rx[:, NT * NG:NT * NG + NT], top2, top1, ALU.subtract).then_inc(s_rx, 1)
            for k, hot in enumerate((hot1, hot2)):
                link(v.tensor_tensor(Mk[k].rearrange("p t (g e) -> p t g e", g=NG), ghot.unsqueeze(3).to_broadcast([P, NT, NG, 8]),
                                     hot.unsqueeze(2).to_broadcast([P, NT, NG, 8]), ALU.mult))
            v.tensor_tensor(Mh, Mk[0], Mk[1], ALU.add).then_inc(s_M, 1)
            dve.wait_ge(s_rx, 2)
            link(v.tensor_reduce(gsum, rx[:, 0:NT * NG].rearrange("p (t n) -> p t n", t=NT), AX_X, ALU.add))
            e2 = rx[:, NT * NG:NT * NG + NT]
            link(v.scalar_tensor_tensor(out=gsum, in0=e2, scalar=1.0, in1=gsum, op0=ALU.add, op1=ALU.mult))
            link(v.reciprocal(gates[:, :, 0], gsum))
            v.tensor_tensor(gates[:, :, 1], gates[:, :, 0], e2, ALU.mult)
            dve.wait_ge(s_rk, 1)
            link(v.tensor_copy(cnt, ps[:, 1, NT * NE:(NT + 1) * NE]))
            link(v.tensor_scalar(nblk, cnt, 0.0, None, ALU.is_gt))
            for m in range(1, SEQ // CAP):
                link(v.scalar_tensor_tensor(out=nblk, in0=cnt, scalar=float(CAP * m), in1=nblk, op0=ALU.is_gt, op1=ALU.add))
            link(v.tensor_tensor_scan(blk_end, ones[:, 0:NE], nblk, 0.0, ALU.mult, ALU.add))
            link(v.tensor_tensor(nblk, blk_end, nblk, ALU.subtract))
            link(v.scalar_tensor_tensor(out=slot, in0=nblk.unsqueeze(1).to_broadcast([P, NT, NE]), scalar=float(CAP),
                                        in1=ps[:, 1, 0:NT * NE].rearrange("p (t e) -> p t e", t=NT), op0=ALU.mult, op1=ALU.add))
            for k in range(2):
                link(v.tensor_tensor(Mk[k], Mk[k], slot, ALU.mult))
                link(v.tensor_reduce(pos[:, :, k], Mk[k], AX_X, ALU.add))
            pos8 = pos.rearrange("p t k -> p (t k)")
            link(v.tensor_tensor(ge, pos8.unsqueeze(2).to_broadcast([P, 2 * NT, TAB + 1]),
                                 const("block_first").unsqueeze(1).to_broadcast([P, 2 * NT, TAB + 1]), ALU.is_ge))
            v.tensor_tensor(block_hot, ge[:, :, 0:TAB], ge[:, :, 1:TAB + 1], ALU.subtract)
            link(v.tensor_reduce(t2, ge, AX_X, ALU.add))
            link(v.tensor_scalar(t2, t2, -1.0, -float(CAP), ALU.add, ALU.mult))
            link(v.tensor_tensor(t2, pos8, t2, ALU.add))
            link(v.tensor_tensor(slot_hot[0], t2.unsqueeze(2).to_broadcast([P, 2 * NT, CAP]),
                                 const("iota_cap").unsqueeze(1).to_broadcast([P, 2 * NT, CAP]), ALU.is_equal))
            link(v.tensor_tensor(slot_hot[1], slot_hot[0], const("asg1").unsqueeze(2).to_broadcast([P, 2 * NT, CAP]), ALU.mult))
            v.tensor_tensor(slot_hot[0], slot_hot[0], const("tok1").unsqueeze(2).to_broadcast([P, 2 * NT, CAP]),
                            ALU.mult).then_inc(s_pos, 1)
            link(v.tensor_scalar(nblk, blk_end, const("block_no"), None, ALU.is_le))
            link(v.tensor_reduce(expert_col, nblk, AX_X, ALU.add))
            v.tensor_scalar(expert_col, expert_col, float(NE - 1), None, ALU.min).then_inc(s_be, 1)
            link(v.tensor_scalar(ge[0:1, 0, 0:TAB // 2], const("block_first")[0:1, 0:TAB // 2], 2.0 / CAP, 1.0, ALU.mult, ALU.add))
            link(v.tensor_scalar(ge[0:1, 0, 0:TAB // 2], ge[0:1, 0, 0:TAB // 2], blk_end[0:1, NE - 1:NE], None, ALU.is_le))
            link(v.tensor_reduce(t2[0:1, 0:1], ge[0:1, 0, 0:TAB // 2], AX_X, ALU.add))
            v.tensor_copy(pairs_ix[0:1, 0:1], t2[0:1, 0:1])
            v.tensor_scalar(pairs_ix[0:1, 1:2], t2[0:1, 0:1], -1.0, None, ALU.add).then_inc(s_bet, 1)
            dve.wait_ge(s_tb, 2)
            v.tensor_copy(expert_ix[:, :], ps[0:1, 4, 0:P]).then_inc(s_bet, 1)
            for w, dst in enumerate((tok_ix, asg_ix)):
                tab = slot[0:CAP, :, :].rearrange("p t e -> p (t e)")[:, 0:TAB]
                link(v.tensor_scalar(tab, ps[0:CAP, 2 + w, 0:TAB], 0.0, FAR, ALU.is_equal, ALU.mult))
                link(v.scalar_tensor_tensor(out=dst[:, :], in0=ps[0:CAP, 2 + w, 0:TAB], scalar=-1.0, in1=tab,
                                            op0=ALU.add, op1=ALU.add))
            phase_end(dve, 17)
            v.memset(xs[0], 0.0)
            v.memset(xs[1], 0.0)
            n_more = dve.value_load(pairs_ix[0:1, 1:2], min_val=1, max_val=MAX_PAIRS - 1)
            phase_end(dve, 18)
            at = steps[0]

            def hidden(j, n, done):
                dve.wait_ge(s_eg, n)
                v.tensor_scalar(sg[j], sg[j], 1.0, None, ALU.add).then_inc(s_vec, 1)
                dve.wait_ge(s_vec, done + 1)
                v.reciprocal(sg[j], sg[j]).then_inc(s_vec, 1)
                dve.wait_ge(s_vec, done + 2)
                v.tensor_tensor(sg[j], ps[0:CAP, j, :], sg[j], ALU.mult).then_inc(s_vec, 1)
                dve.wait_ge(s_vec, done + 3)
                dve.wait_ge(s_mu, n + 2)
                v.tensor_tensor(hrow[j], ps[CAP:2 * CAP, j, :], sg[j], ALU.mult).then_inc(s_ha, 1)

            def hidden_in(j, n):
                dve.wait_ge(s_ta, n)
                v.tensor_copy(hid[j].rearrange("p c s -> p (c s)"), ps[:, 6 + j, 0:4 * CAP]).then_inc(s_hd, 1)
            hidden(0, 1, at)
            with dve.Fori(0, n_more) as i:
                hidden_in(0, i * 2 + 1)
                hidden(1, i * 2 + 2, i * 6 + (at + 3))
                hidden_in(1, i * 2 + 2)
                hidden(0, i * 2 + 3, i * 6 + (at + 6))
            before = dve.snap(n_more * 2)
            hidden_in(0, before + 1)
            hidden(1, before + 2, dve.snap(n_more * 6 + (at + 3)))
            hidden_in(1, before + 2)
            phase_end(dve, 19)
            phase_end(dve, 20)
            phase_end(dve, 21)
            steps[0] = 0
            vec_sem[0] = s_vec2
            for t in range(NT):
                dve.wait_ge(s_y2[t % 2], 16 * (t // 2 + 1))
                link(v.scalar_tensor_tensor(out=h2[:, t, :], in0=y2[t % 2][:, 0, :], scalar=gates[:, t, 0:1], in1=h2[:, t, :],
                                            op0=ALU.mult, op1=ALU.add))
                v.scalar_tensor_tensor(out=h2[:, t, :], in0=y2[t % 2][:, 1, :], scalar=gates[:, t, 1:2], in1=h2[:, t, :],
                                       op0=ALU.mult, op1=ALU.add).then_inc(s_y2f, 1)
                dve.wait_ge(s_y2f, t + 1)
                row_norm(t)
                if t == 0:
                    dve.wait_ge(s_row, 32)
                v.scalar_tensor_tensor(out=h2[:, t, :], in0=h2[:, t, :], scalar=glst[:, 30:31], in1=gain_row,
                                       op0=ALU.mult, op1=ALU.mult).then_inc(s_fin, 1)
                dve.wait_ge(s_fin, t + 1)
            phase_end(dve, 22)

        @block.gpsimd
        def _(pool):
            for n in range(1, 19):
                phase_end(pool, n)
            n_more = pool.value_load(pairs_ix[0:1, 1:2], min_val=2, max_val=MAX_PAIRS - 1)

            def settle(cell=0):
                return pool.tensor_tensor(spare[:, cell:cell + 1], spare[:, 2:3], spare[:, 2:3], ALU.add)

            def gather(j, b, copies):
                pool.tensor_copy(tcol[j][:, :], tok_ix[:, bass.ds(b, 1)]).then_inc(s_pix, 1)
                pool.wait_ge(s_pix, copies)
                settle()
                pool.indirect_dma_start(xs[j], None, u_dram, bass.IndirectOffsetOnAxis(tcol[j][:, :], 0),
                                        bounds_check=SEQ - 1, oob_is_err=False).then_inc(s_gat[j], 16)
            pool.memset(spare[:, :], 0.0).then_inc(s_pix, 1)
            pool.wait_ge(s_pix, 1)
            pool.wait_ge(s_ud, 16 * NT)
            gather(0, 0, 2)
            gather(1, 1, 3)
            def scatter(j, b, copies, n, earlier):
                if earlier is not None:
                    pool.wait_ge(s_scat[j], earlier)
                    settle(1).then_inc(s_ysf, 1)
                pool.tensor_copy(acol[j][:, :], asg_ix[:, bass.ds(b, 1)]).then_inc(s_pix, 1)
                pool.wait_ge(s_pix, copies)
                pool.wait_ge(s_yc, n)
                settle()
                pool.indirect_dma_start(y_dram, bass.IndirectOffsetOnAxis(acol[j][:, :], 0), ys[j], None,
                                        bounds_check=N_ASG - 1, oob_is_err=False).then_inc(s_scat[j], 16)

            for j in range(2):
                pool.wait_ge(s_xt, j + 1)
                gather(j, j + 2, j + 4)
            for j in range(2):
                pool.wait_ge(s_xt, j + 3)
                gather(j, j + 4, 2 * j + 6)
                scatter(j, j, 2 * j + 7, j + 1, None)
            with pool.Fori(1, n_more) as i:
                for j in range(2):
                    pool.wait_ge(s_xt, i * 2 + (j + 3))
                    gather(j, i * 2 + (j + 4), i * 4 + (2 * j + 6))
                    scatter(j, i * 2 + j, i * 4 + (2 * j + 7), i * 2 + (j + 1), i * 16)
            before = pool.snap(n_more * 2)
            for j in range(2):
                scatter(j, before + j, pool.snap(n_more * 4 + (j + 6)), pool.snap(n_more * 2 + (j + 1)), pool.snap(n_more * 16))
            for j in range(2):
                pool.wait_ge(s_gat[j], pool.snap(n_more * 16 + 32))
                pool.wait_ge(s_scat[j], pool.snap(n_more * 16 + 16))
            settle(3)
            for n in range(19, 23):
                phase_end(pool, n)


_INS = ["x", "w_mod", "w1_gate", "w1_up", "w1_down", "w_in", "b_f", "w_o", "w2_gate", "w2_up", "w2_down", "meta_tokens_2",
        "w_in_2", "gla_w_a2_2", "mla_w_qb_2", "mla_w_kvb_2", "w_out_2", "ffn_norm_2", "router_group_w_2", "router_expert_w_2",
        "expert_w_gate_2", "expert_w_up_2", "expert_w_down_2"]


def kernel(**inputs):
    import concourse.bacc as _bacc
    from concourse.bass_utils import run_bass_kernel_spmd as _run

    nc = _bacc.Bacc("TRN2", target_bir_lowering=False, num_devices=1)
    arrays = {name: np.ascontiguousarray(inputs[name]) for name in _INS}
    arrays["cols"] = np.ascontiguousarray(np.concatenate(
        [np.asarray(inputs[name]).reshape(-1, P) for name in COLS], axis=0).T)
    arrays["router_bias"] = np.concatenate([inputs["router_group_b_2"], inputs["router_expert_b_2"]], axis=1)
    arrays["final_norm_2"] = np.ascontiguousarray(inputs["final_norm_2"]).reshape(1, D)
    arrays["const"] = CONST_ARRAY
    args = {name: nc.dram_tensor(f"in_{name}", x.shape, mybir.dt.from_np(x.dtype), kind="ExternalInput").ap()
            for name, x in arrays.items()}
    out = nc.dram_tensor("out_0", (1, SEQ, D), F32, kind="ExternalOutput").ap()
    build(nc, args, out)
    r = _run(nc, [{f"in_{name}": x for name, x in arrays.items()}], core_ids=[0])
    return r.results[0]["out_0"]
```

```python
from contextlib import ExitStack

import numpy as np
import concourse.bass as bass
from concourse import mybir

ALU = mybir.AluOpType
ACT = mybir.ActivationFunctionType
F32 = mybir.dt.float32
I32 = mybir.dt.int32
U32 = mybir.dt.uint32
AX_X = mybir.AxisListType.X

P = 128
D = 1024
KC = D // P
SEQ = 512
META = 16
TOK = SEQ + META
FF = 2816
FC = FF // P
EPS = 1e-6
HD = 64
N_SLOT = 6
SLOT = 4096
TILE_AT = [0, 128, 384, 768]
TRI = 1280
OFF_DIAG = [(i, k) for i in range(4) for k in range(i)]
BLOCK_AT = {(i, i): i for i in range(4)}
BLOCK_AT.update({ik: 4 + n for n, ik in enumerate(OFF_DIAG)})

COLS = {}


def _cols():
    at = 0
    for name, n in (("c", 8), ("b_mod", 72), ("g_ffn1", 8), ("g_mix", 8), ("g_ffn2", 8), ("mix_norm_2", 8),
                    ("gla_out_norm_2", 4), ("mla_q_norm_2", 2), ("mla_kv_norm_2", 1), ("gla_b_a_2", 2),
                    ("g_q", 4), ("g_k", 4)):
        COLS[name] = (at, n)
        at += n
    return at


N_COLS = _cols()

LAST_LEFT = 10
GH = 4
CHUNK = 64
N_CHUNK = SEQ // CHUNK
ROPE = 64
NOPE = 128
MLA_SCALE = (NOPE + ROPE) ** -0.5
D_IN2 = 2000
NG, NE = 8, 64
DE = 512
CAP = 64
N_ASG = 2 * SEQ
MAX_BLOCKS = NE + (N_ASG - NE) // CAP
MAX_PAIRS = (MAX_BLOCKS + 1) // 2
TAB = 2 * MAX_PAIRS + 4
FAR = 8192.0
NT = SEQ // P

CONST = {}


def constant_tables():
    p = np.arange(P)[:, None]
    j = np.arange(P)[None, :]
    parts = [("ident", (p == j) * 1.0),
             ("ones", np.ones((P, P))),
             ("head_ones", (p // HD == j // HD) * 1.0),
             ("after", (p > j) * -1e30 * 0 + (j > p) * -1e30),
             ("strict_t", (p < j) * 1.0)]
    resets = []
    for i in range(4):
        k = np.arange(P * (i + 1))[None, :]
        resets.append((k < i * P + p - 1) * 1.0)
    parts.append(("resets", np.concatenate(resets, axis=1)))
    tok = np.arange(TOK)[None, :]
    chunk_start = (tok == 0) | ((tok >= META) & ((tok - META) % CHUNK == 0))
    parts.append(("chunk_resets", np.broadcast_to(1.0 - chunk_start, (P, TOK))))
    parts.append(("chunk_causal", ((p <= j) & (p // CHUNK == j // CHUNK)) * 1.0))
    freq = (np.float32(10000.0) ** (-np.arange(0, ROPE, 2, dtype=np.float32) / np.float32(ROPE))).astype(np.float32)
    angle = (np.arange(TOK, dtype=np.float32)[:, None] * freq[None, :]).astype(np.float32).T
    rows = np.zeros((P, TOK), np.float32)
    rows[0:ROPE] = np.concatenate([np.cos(angle), np.cos(angle)], axis=0)
    parts.append(("rope_cos", rows))
    rows = np.zeros((P, TOK), np.float32)
    rows[0:ROPE] = np.concatenate([-np.sin(angle), np.sin(angle)], axis=0)
    parts.append(("rope_sin", rows))
    parts.append(("iota8", np.broadcast_to(np.arange(8.0), (P, 8))))
    parts.append(("block_first", np.broadcast_to(np.arange(0.0, CAP * (TAB + 1), CAP), (P, TAB + 1))))
    parts.append(("block_no", p * 1.0))
    parts.append(("iota_cap", np.broadcast_to(np.arange(float(CAP)), (P, CAP))))
    asg = 2 * (np.arange(NT)[None, :, None] * P + np.arange(P)[:, None, None]) + np.arange(2)[None, None, :] + 1
    parts.append(("asg1", asg.reshape(P, 2 * NT) * 1.0))
    parts.append(("tok1", ((asg - 1) // 2 + 1).reshape(P, 2 * NT) * 1.0))
    at = 0
    for name, t in parts:
        CONST[name] = (at, t.shape[1])
        at += t.shape[1]
    return np.ascontiguousarray(np.concatenate([t for _, t in parts], axis=1).astype(np.float32))


CONST_ARRAY = constant_tables()


class Uses:

    def __init__(self):
        self.filled = [0] * N_SLOT
        self.freed = [1] * N_SLOT

    def take(self, s, dmas, times=1):
        before = (self.filled[s], self.freed[s])
        self.filled[s] += 16 * dmas * times
        self.freed[s] += times
        return before


def build(nc, a, out):
    ctx = ExitStack()
    with ctx:
        def sb(name, shape, dt=F32):
            return ctx.enter_context(nc.sbuf_tensor(name, shape, dt))

        def sem(name):
            return ctx.enter_context(nc.semaphore(name))

        ring = [sb(f"slot{s}", [P, SLOT]) for s in range(N_SLOT)]
        cst = sb("cst", [P, CONST_ARRAY.shape[1]])
        cols = sb("cols", [P, N_COLS])
        xT = sb("xT", [P, KC, TOK])
        hT = sb("hT", [P, KC, TOK])
        big = sb("big", [P, FC * SEQ])
        aT = big[:, :].rearrange("p (f t) -> p f t", f=FC)
        modT = sb("modT", [P, 72])
        small = sb("small", [P, 64])
        tmp = sb("tmp", [P, 2, TOK])
        rstd = sb("rstd", [P, TOK])
        eb = sb("eb", [P, 2, SEQ])
        ps = ctx.enter_context(nc.psum_tensor("ps", [P, 8, 512], F32))

        def const(name):
            at, n = CONST[name]
            return cst[:, at:at + n]

        def col(name, j=None):
            at, n = COLS[name]
            return cols[:, at:at + n] if j is None else cols[:, at + j:at + j + 1]

        ident, ones = const("ident"), const("ones")
        c_act = small[:, 0:8]
        c_exp = small[:, 8:16]
        scale = [small[:, 16 + 8 * r:24 + 8 * r] for r in range(3)]
        gate = [small[:, 40 + 8 * r:48 + 8 * r] for r in range(3)]
        eps_col = sb("eps_col", [P, 1])

        def part(at, n):
            return big[:, at:at + n]
        qT = part(0, 512)
        kT = part(512, 512)
        vt = part(1024, 512).rearrange("p (t n) -> p t n", t=4)
        buf1 = part(1536, TRI)
        buf2 = part(1536 + TRI, TRI)
        PT = part(1536 + 2 * TRI, TRI).rearrange("p (b q) -> p b q", q=P)
        oT = part(5376, 4096).rearrange("p (c t) -> p c t", c=8)
        FL = big[:, 9472:9984]
        FR = big[:, 9984:10496]
        Fc = big[0:8, 10496:11008]
        fA = tmp[0:8, 0, 0:512]
        fB = tmp[0:8, 1, 0:512]
        fox_s = sb("fox_s", [P, 16])
        gqs = sb("gqs", [P, 4])
        wf = sb("wf", [P, KC, 8])
        bf = sb("bf", [8, 1])

        s_in = sem("inputs_in")
        s_x = sem("x_in")
        filled = [sem(f"filled{s}") for s in range(N_SLOT)]
        freed = [sem(f"freed{s}") for s in range(N_SLOT)]
        s_phase = [sem(f"phase_done{n}") for n in range(LAST_LEFT + 2)]
        s_vec = sem("vector_step")
        s_act = sem("scalar_step")
        s_tr = sem("turned")
        s_trc = sem("turned_copied")
        s_cexp = sem("c_exp_ready")
        s_cact = sem("c_act_ready")
        s_mod = sem("mod_done")
        s_mrow = sem("mod_row_ready")
        s_mstep = sem("mod_item_step")
        s_macc = sem("mod_item_ready")
        s_msum = sem("mod_item_summed")
        s_mcp = sem("mod_copied")
        s_d0 = sem("first_half_added")
        s_sq = sem("squares_ready")
        s_ss = sem("square_sum_done")
        s_std = sem("std_ready")
        s_rs = sem("rstd_ready")
        s_nx = sem("normed_ready")
        s_scale = sem("norm_scale_ready")
        s_hn = sem("normed_scaled_ready")
        s_xu = sem("residual_updated")
        s_gu = sem("gate_up_done")
        s_ge = sem("gate_exp_ready")
        s_hid = sem("hidden_ready")
        s_dn = sem("down_done")
        s_qkv = sem("qkv_done")
        s_qc = sem("q_copied")
        s_kvc = sem("kv_copied")
        s_qsq = sem("qk_squares_ready")
        s_qss = sem("qk_square_sum_done")
        s_qr = sem("qk_rstd_ready")
        s_qn = sem("qk_normed")
        s_qstd = sem("qk_std_ready")
        s_z = sem("scores_done")
        s_sp = sem("softplus_ready")
        s_zz = sem("log_weights_ready")
        s_mx = sem("max_ready")
        s_e = sem("exp_ready")
        s_p = sem("probs_ready")
        s_pt = sem("probs_turned")
        s_ptc = sem("probs_turned_copied")
        s_pv = sem("heads_done")
        s_o = sem("heads_copied")
        s_fl = sem("forget_ready")
        s_fm = sem("forget_head_ready")
        s_fp = sem("forget_proj_done")
        s_f1 = sem("forget_exp_ready")
        s_wo = sem("mix_done")
        s_out = sem("out_written")

        flat = ps[:, :, :].rearrange("p b n -> p (b n)")
        gq = part(0, 1024).rearrange("p (c t) -> p c t", c=2)
        gk = part(1024, 1056).rearrange("p (c t) -> p c t", c=2)
        gv = part(2080, 2560).rearrange("p (t n) -> p t n", t=5)
        gr = part(4640, 2048).rearrange("p (c t) -> p c t", c=4)
        aL = part(6688, TOK)
        ql = part(7216, 1024).rearrange("p (c t) -> p c t", c=2)
        kv = part(8240, TOK)
        kr = part(8768, TOK)
        kdtok = part(9296, 1280).rearrange("p (t n) -> p t n", t=5)
        swap = part(10576, TOK)
        Sc = ring[0][:, 0:1056].rearrange("p (c t) -> p c t", c=2)
        km = ring[0][:, 1056:2112].rearrange("p (c t) -> p c t", c=2)
        kd = ring[0][:, 2112:3168].rearrange("p (c t) -> p c t", c=2)
        gexp = ring[0][:, 0:2048].rearrange("p (h t) -> p h t", h=4)
        states = ring[1][:, 0:2 * (N_CHUNK + 1) * P].rearrange("p (c n e) -> p c n e", c=2, n=N_CHUNK + 1)
        o2 = hT[:, :, :].rearrange("p k t -> p (k t)")[:, 0:8 * SEQ].rearrange("p (c t) -> p c t", c=8)
        attS = eb[:, 0, :].rearrange("p (b c) -> p b c", b=4)
        osq = eb[:, 1, :]
        sil = tmp[:, 0, 0:SEQ]
        orst = tmp[:, 1, 0:SEQ]
        qn = ring[0][:, 0:2048].rearrange("p (h t) -> p h t", h=GH)
        qr = ring[0][0:ROPE, 2048:4096].rearrange("p (h t) -> p h t", h=GH)
        kn = ring[1][:, 0:GH * TOK].rearrange("p (h t) -> p h t", h=GH)
        mv = ring[3][:, 0:2560].rearrange("p (t n) -> p t n", t=5)
        PB = [tmp[:, j, :] for j in range(2)]
        mPT = big[:, 0:640].rearrange("p (b q) -> p b q", b=5)
        glst = sb("glst", [P, 64])
        w_a2 = ring[2][0:16, 0:256]
        w_qb = ring[2][:, 256:1792].rearrange("p (k n) -> p k n", k=2)
        w_kvb = ring[2][:, 1792:2816]
        h2 = part(0, 4096).rearrange("p (t d) -> p t d", t=NT)
        u2 = part(4096, 4096).rearrange("p (t d) -> p t d", t=NT)
        uT = xT[:, :, :].rearrange("p k t -> p (k t)")[:, 0:KC * SEQ].rearrange("p (k t) -> p k t", k=KC)
        gain_row = part(8192, D)
        wr = ring[3][:, 2560:2560 + KC * 72].rearrange("p (k n) -> p k n", k=KC)
        bias_row = ring[3][:, 3200:3272]
        gates = sb("gates", [P, NT, 2])
        rb = hT[:, :, :].rearrange("p k t -> p (k t)")
        tok_ix = sb("tok_ix", [CAP, TAB], I32)
        asg_ix = sb("asg_ix", [CAP, TAB], I32)
        expert_ix = sb("expert_ix", [1, P], I32)
        pairs_ix = sb("pairs_ix", [1, 4], I32)
        mo = xT[:, :, :].rearrange("p k t -> p (k t)")
        xs = [mo[0:CAP, 1024 * j:1024 * (j + 1)] for j in range(2)]
        xsT = [mo[:, 2048 + 512 * j:2560 + 512 * j].rearrange("p (k s) -> p k s", k=KC) for j in range(2)]
        sg = [mo[0:CAP, 3072 + 512 * j:3584 + 512 * j] for j in range(2)]
        mo2 = hT[:, :, :].rearrange("p k t -> p (k t)")
        hid = [mo2[:, 256 * j:256 * (j + 1)].rearrange("p (c s) -> p c s", c=4) for j in range(2)]
        ys = [mo2[0:CAP, 512 + 1024 * j:1536 + 1024 * j] for j in range(2)]
        hrow = [mo2[0:CAP, 2560 + 512 * j:3072 + 512 * j] for j in range(2)]
        tcol = [sb(f"tcol{j}", [CAP, 1], I32) for j in range(2)]
        acol = [sb(f"acol{j}", [CAP, 1], I32) for j in range(2)]
        y2 = [ring[j][:, 0:2 * D].rearrange("p (k d) -> p k d", k=2) for j in range(NT)]
        u_dram = nc.dram_tensor("normed_tokens", (SEQ, D), F32, kind="Internal").ap()
        y_dram = nc.dram_tensor("expert_rows", (N_ASG, D), F32, kind="Internal").ap()

        s_rn = sem("mean_square_ready")
        s_rnq = sem("row_root_ready")
        s_vec2 = sem("vector_last_step")
        at = [0]

        def scratch(*shape):
            n = 1
            for m in shape:
                n *= m
            ap = rb[:, at[0]:at[0] + n]
            at[0] += n
            if len(shape) == 1:
                return ap
            names = "abcd"[:len(shape)]
            return ap.rearrange("p (" + " ".join(names) + ") -> p " + " ".join(names),
                                **{c: m for c, m in zip(names[1:], shape[1:])})
        lg = scratch(NT, 72)
        t8, ghot, hot1, hot2, el = (scratch(NT, 8) for _ in range(5))
        t1, gtop, top1, top2, gsum = (scratch(NT) for _ in range(5))
        rx = scratch(NT * NG + NT)
        pick = scratch(NT, NG, 8)
        Mk = [scratch(NT, NE) for _ in range(2)]
        Mh = scratch(NT, NE)
        slot = scratch(NT, NE)
        cnt, nblk, blk_end = (scratch(NE) for _ in range(3))
        pos = scratch(NT, 2)
        t2 = scratch(2 * NT)
        expert_col = scratch(1)
        ge = scratch(2 * NT, TAB + 1)
        at[0] = 0
        rb = tmp[:, :, :].rearrange("p b n -> p (b n)")
        block_hot = scratch(2 * NT, TAB)
        at[0] = 0
        rb = eb[:, :, :].rearrange("p b n -> p (b n)")
        slot_hot = [scratch(2 * NT, CAP)]
        at[0] = 0
        rb = part(9216, 2048)
        slot_hot.append(scratch(2 * NT, CAP))
        sq_row = part(9216 + 512, D)
        s_p2 = sem("proj2_done")
        s_p2c = [sem(f"proj2_copied{j}") for j in range(2)]
        s_la = sem("decay_proj_done")
        s_lq = sem("latent_squares_ready")
        s_lss = sem("latent_square_sum_done")
        s_lstd = sem("latent_std_ready")
        s_dt = sem("decay_logit_ready")
        s_dsp = sem("decay_softplus_ready")
        s_S = sem("decay_sum_ready")
        s_dx = sem("decay_exp_ready")
        s_kd = sem("decayed_keys_ready")
        s_kt = sem("decayed_keys_turned")
        s_ktc = sem("decayed_keys_turned_copied")
        s_U = sem("chunk_update_done")
        s_st = sem("state_ready")
        s_at2 = sem("gla_scores_done")
        s_atm = sem("gla_scores_masked")
        s_go = sem("gla_out_done")
        s_gsq = sem("gla_out_squares")
        s_gss = sem("gla_out_square_sum")
        s_gstd = sem("gla_out_std")
        s_gf = sem("gla_head_ready")
        s_gex = sem("gla_gate_exp_ready")
        s_mz = sem("mla_scores_done")
        s_mb = sem("mla_max_ready")
        s_me = sem("mla_exp_ready")
        s_mp = sem("mla_probs_ready")
        s_mt = sem("mla_probs_turned")
        s_mtc = sem("mla_probs_turned_copied")
        s_mpv = sem("mla_head_done")
        s_mo = sem("mla_head_copied")
        s_xr = sem("residual_turned")
        s_xrc = sem("residual_copied")
        s_h2 = sem("mixed_ready")
        s_un = sem("normed_row_ready")
        s_ut = sem("normed_turned")
        s_utc = sem("normed_turned_copied")
        s_lg = sem("logits_done")
        s_rx = sem("router_exp")
        s_M = sem("router_onehot_ready")
        s_rk = sem("ranks_done")
        s_pos = sem("slots_ready")
        s_tb = sem("tables_done")
        s_be = sem("block_expert_ready")
        s_bet = sem("block_expert_turned")
        s_row = sem("gain_in")
        s_ud = sem("normed_written")
        s_gat = [sem(f"gathered{j}") for j in range(2)]
        s_scat = [sem(f"scattered{j}") for j in range(2)]
        s_xt = sem("expert_in_turned")
        s_xtc = sem("expert_in_ready")
        s_mg = sem("expert_gate_done")
        s_mu = sem("expert_up_done")
        s_my = sem("expert_down_done")
        s_eg = sem("expert_exp_ready")
        s_hd = sem("expert_hidden_ready")
        s_ha = sem("expert_hidden_rows_ready")
        s_ta = sem("expert_hidden_turned")
        s_yc = sem("expert_rows_ready")
        s_ysf = sem("row_buffer_free")
        s_pix = sem("index_column_ready")
        s_y2 = [sem(f"rows_back{j}") for j in range(NT)]
        s_y2f = sem("rows_used")
        s_fsq = sem("final_square_sum")
        s_fst = sem("final_std")
        s_fin = sem("final_rows_ready")

        w_in2 = a["w_in_2"][0].rearrange("(k p) n -> p k n", p=P)
        w_out2 = a["w_out_2"][0].rearrange("(f p) n -> p f n", p=P)
        ITEMS2 = [(0, 512), (512, 512), (1024, 512), (1536, 464)]

        def w2(n):
            return ring[2 + n][:, 0:KC * ITEMS2[n][1]].rearrange("p (k n) -> p k n", k=KC)
        UNITS = [(0, 0, P, False, gq[:, 0]), (0, P, P, False, gq[:, 1]), (0, 2 * P, P, True, gk[:, 0]), (0, 3 * P, P, True, gk[:, 1]),
                 (1, 0, META, None, gv[0:META, 0]), (1, 0, P, None, gv[:, 1]), (1, 0, P, None, gv[:, 2]),
                 (1, 0, P, None, gv[:, 3]), (1, 0, P, None, gv[:, 4]),
                 (2, 0, P, False, gr[:, 0]), (2, P, P, False, gr[:, 1]), (2, 2 * P, P, False, gr[:, 2]), (2, 3 * P, P, False, gr[:, 3]),
                 (3, 0, 16, True, aL[0:16, :]), (3, 16, P, False, ql[:, 0]), (3, 16 + P, P, False, ql[:, 1]),
                 (3, 16 + 2 * P, P, True, kv), (3, 16 + 3 * P, ROPE, True, kr[0:ROPE, :])]
        GATE_PAIRS = {11: 0, 13: 2}
        TILE0 = [0] + [META + P * t for t in range(NT)]
        TILEN = [META] + [P] * NT

        def halves(ap):
            return ap.rearrange("p (b n) -> p b n", b=2)

        def unit_psum(n):
            b = 2 * (n % 4)
            _, _, m, wide, _ = UNITS[n]
            return ps[0:m, b:b + 2, 0:TOK // 2] if wide else ps[0:m, b, :]

        def unit_dst(n):
            return halves(UNITS[n][4]) if UNITS[n][3] else UNITS[n][4]

        spare = sb("spare", [1, 4])

        def mla_z(un):
            t = un % NT
            at = 1024 * (un % 2) + 512
            return flat[:, at - META:at + P * (t + 1)]

        PH = {}

        def phase_end(eng, n):
            eng.drain().then_inc(s_phase[min(n, LAST_LEFT + 1)], 1)
            eng.wait_ge(s_phase[min(n, LAST_LEFT + 1)], 4 * max(1, n - LAST_LEFT))

        def phase_left(eng, n):
            eng.drain().then_inc(s_phase[n], 1)

        HALVES = {0: [(META, SEQ)], 1: [(META, SEQ)], 2: [(META, SEQ)], 3: [(0, TOK // 2), (TOK // 2, TOK // 2)]}

        w_mod = a["w_mod"][0].rearrange("(k p) n -> p k n", p=P)
        ffn_w = [(a["w1_gate"][0], a["w1_up"][0], a["w1_down"][0]), (a["w2_gate"][0], a["w2_up"][0], a["w2_down"][0])]
        w_in = a["w_in"][0].rearrange("(k p) n -> p k n", p=P)
        w_o = a["w_o"][0].rearrange("(k p) n -> p k n", p=P)
        DOWN_ITEMS = [(f0, min(8, FC - f0)) for f0 in range(0, FC, 8)]
        N_GU = FC // 2

        def gu_view(s):
            return ring[s][:, :].rearrange("p (g k n) -> p g k n", g=2, k=KC)

        def down_slot(ps_, n):
            return 3 + n

        MOD_FIRST = 4
        MOD_LAST = (0, 1, 2)
        assert MOD_FIRST + N_GU + len(MOD_LAST) == 18
        mod_row = big[0:1, 0:MOD_FIRST * 512]
        acc = rstd[:, 0:512]
        acc_last = [tmp[:, 0, 0:512], tmp[:, 1, 0:512], rstd[:, 0:512]]

        block = ctx.enter_context(nc.Block())

        @block.sync
        def _(sp):
            u = Uses()
            sp.dma_start(cst[:, :], a["const"]).then_inc(s_in, 16)
            sp.dma_start(cols[:, :], a["cols"]).then_inc(s_in, 16)
            sp.dma_start(bf[:, :], a["b_f"].rearrange("a h -> h a")).then_inc(s_in, 16)
            sp.dma_start(wf[:, :, :], w_in[:, :, 3072:3080]).then_inc(s_in, 16)
            sp.dma_start(ring[5][:, :].rearrange("p (t d) -> p t d", t=4),
                         a["x"][0].rearrange("(t p) d -> p t d", p=P)).then_inc(s_x, 16)
            sp.dma_start(ring[4][0:META, 0:D], a["meta_tokens_2"]).then_inc(s_x, 16)

            def refill(s, k):
                if isinstance(k, int) and k == 0:
                    return
                sp.wait_ge(freed[s], k)

            def mod_item(s, k, item):
                sp.wait_ge(freed[s], k)
                sp.dma_start(ring[s][:, :].rearrange("p (k n) -> p k n", k=KC),
                             w_mod[:, :, bass.ds(item * 512, 512)]).then_inc(filled[s], 16)
            for s in range(MOD_FIRST):
                mod_item(s, u.take(s, 1)[1], s)

            def ffn(r):
                wg, wu, wd = ffn_w[r]
                wg, wu = (w.rearrange("(k p) n -> p k n", p=P) for w in (wg, wu))
                wd = wd.rearrange("(f p) n -> p f n", p=P)

                def gate_up(s, k, item):
                    sp.wait_ge(freed[s], k)
                    for g, w in enumerate((wg, wu)):
                        sp.dma_start(gu_view(s)[:, g], w[:, :, bass.ds(item * 256, 256)]).then_inc(filled[s], 16)
                base = [u.take(s, 2, N_GU // 2)[1] for s in range(2)]
                base2 = u.take(2, 1, N_GU)[1] if r == 0 else 0
                with sp.Fori(0, N_GU // 2) as i:
                    for s in range(2):
                        gate_up(s, base[s] + i, i * 2 + s)
                        if r == 0:
                            mod_item(2, i * 2 + (base2 + s), i * 2 + (MOD_FIRST + s))
                gate_up(0, u.take(0, 2)[1], N_GU - 1)
                if r == 0:
                    mod_item(2, base2 + N_GU - 1, MOD_FIRST + N_GU - 1)
                for half in range(2):
                    for n, (f0, nf) in enumerate(DOWN_ITEMS):
                        s = down_slot(half, n)
                        sp.wait_ge(freed[s], u.take(s, 1)[1])
                        sp.dma_start(ring[s][:, 0:nf * 512].rearrange("p (f n) -> p f n", f=nf),
                                     wd[:, f0:f0 + nf, half * 512:half * 512 + 512]).then_inc(filled[s], 16)
                    if r == 0 and half == 0:
                        for s in MOD_LAST:
                            mod_item(s, u.take(s, 1)[1], MOD_FIRST + N_GU + MOD_LAST.index(s))

            def pairs(s, at):
                k = u.take(s, 3, 4)[1]
                view = ring[s][:, 0:KC * 384].rearrange("p (k w n) -> p k w n", k=KC, w=3)
                with sp.Fori(0, 4) as i:
                    sp.wait_ge(freed[s], i + k)
                    for w in range(3):
                        sp.dma_start(view[:, :, w], w_in[:, :, bass.ds(at + w * 512 + i * P, P)]).then_inc(filled[s], 16)

            ffn(0)
            pairs(2, 0)
            pairs(3, 1536)
            for n, s in enumerate((4, 5)):
                sp.wait_ge(freed[s], u.take(s, 1)[1])
                sp.dma_start(ring[s][:, :].rearrange("p (f n) -> p f n", f=4), w_o[:, 4 * n:4 * n + 4, :])\
                    .then_inc(filled[s], 16)
            ffn(1)
            for n, (c0, w) in enumerate(ITEMS2):
                sp.wait_ge(freed[2 + n], u.take(2 + n, 1)[1])
                sp.dma_start(w2(n), w_in2[:, :, c0:c0 + w]).then_inc(filled[2 + n], 16)
            sp.wait_ge(freed[2], u.take(2, 3)[1])
            sp.dma_start(w_a2, a["gla_w_a2_2"][0]).then_inc(filled[2], 16)
            sp.dma_start(w_qb, a["mla_w_qb_2"][0].rearrange("(k p) n -> p k n", p=P)).then_inc(filled[2], 16)
            sp.dma_start(w_kvb, a["mla_w_kvb_2"][0]).then_inc(filled[2], 16)
            for n, s in enumerate((4, 5)):
                sp.wait_ge(freed[s], u.take(s, 1)[1])
                sp.dma_start(ring[s][:, :].rearrange("p (f n) -> p f n", f=4), w_out2[:, 4 * n:4 * n + 4, :])\
                    .then_inc(filled[s], 16)
            sp.wait_ge(freed[3], u.take(3, 3)[1])
            sp.dma_start(wr[:, :, 0:NG], a["router_group_w_2"][0].rearrange("(k p) n -> p k n", p=P)).then_inc(filled[3], 16)
            sp.dma_start(wr[:, :, NG:], a["router_expert_w_2"][0].rearrange("(k p) n -> p k n", p=P)).then_inc(filled[3], 16)
            sp.dma_start(bias_row, a["router_bias"].to_broadcast([P, NG + NE])).then_inc(filled[3], 16)
            sp.wait_ge(s_mo, GH * NT)
            sp.dma_start(gain_row, a["ffn_norm_2"].to_broadcast([P, D])).then_inc(s_row, 16)
            for t in range(NT):
                sp.wait_ge(s_un, t + 1)
                sp.dma_start(u_dram[t * P:(t + 1) * P, :], u2[:, t, :]).then_inc(s_ud, 16)
            sp.wait_ge(s_ud, 16 * NT)
            k01 = [u.take(s, 0)[1] for s in (0, 1)]
            first = [u.take(s, 1)[1] for s in range(N_SLOT)]
            for s in range(N_SLOT):
                sp.wait_ge(freed[s], first[s])
            sp.wait_ge(s_bet, 2)
            n_pairs = sp.value_load(pairs_ix[0:1, 0:1], min_val=2, max_val=MAX_PAIRS)
            experts = [[a[f"expert_w_{n}_2"][0].rearrange("e (p k) n -> e p (k n)", p=P) for n in ("gate", "up")],
                       a["expert_w_down_2"][0].rearrange("e (f p) n -> e p f n", p=P)]
            with sp.Fori(0, n_pairs) as i:
                for j in range(2):
                    e = sp.value_load(expert_ix[0:1, bass.ds(i * 2 + j, 1)], min_val=0, max_val=NE - 1)
                    for n, done in enumerate((s_mg, s_mu)):
                        sp.wait_ge(done, i * 2 + (j + 1))
                        sp.dma_start(ring[3 * j + n][:, :], experts[0][n][bass.ds(e, 1)].rearrange("e p n -> (e p) n"))\
                            .then_inc(filled[3 * j + n], 16)
                    sp.wait_ge(s_my, i * 2 + (j + 1))
                    sp.dma_start(ring[3 * j + 2][:, :].rearrange("p (f n) -> p f n", f=4),
                                 experts[1][bass.ds(e, 1)].rearrange("e p f n -> (e p) f n")).then_inc(filled[3 * j + 2], 16)
            sp.wait_ge(s_phase[LAST_LEFT + 1], 4 * (21 - LAST_LEFT))
            rows = y_dram.rearrange("(t p k) d -> t p k d", p=P, k=2)
            for t in range(NT):
                sp.dma_start(y2[t], rows[t]).then_inc(s_y2[t], 16)
                if t == 0:
                    sp.dma_start(gain_row, a["final_norm_2"].to_broadcast([P, D])).then_inc(s_row, 16)
            for t in range(NT):
                sp.wait_ge(s_fin, t + 1)
                sp.dma_start(out[0, t * P:(t + 1) * P, :], h2[:, t, :]).then_inc(s_out, 16)
            sp.wait_ge(s_out, 16 * NT)

        @block.tensor
        def _(pe):
            u = Uses()
            mm = nc.tensor.matmul
            for s in range(4):
                pe.drain().then_inc(freed[s], 1)
            pe.wait_ge(s_in, 64)
            pe.wait_ge(s_x, 32)
            xin = ring[5][:, :].rearrange("p (t d) -> p t d", t=4)
            for k in range(KC):
                for t in range(4):
                    last = nc.tensor.transpose(ps[:, k, t * P:(t + 1) * P], xin[:, t, k * P:(k + 1) * P], ident)
                last.then_inc(s_tr, 1)
            pe.wait_ge(s_trc, 1)
            for k in range(KC):
                last = nc.tensor.transpose(ps[:, 0, k * META:(k + 1) * META], ring[4][0:META, k * P:(k + 1) * P],
                                           ident[0:META, 0:META])
            last.then_inc(s_tr, 1)
            for s in (4, 5):
                pe.drain().then_inc(freed[s], 1)
            phase_end(pe, 1)

            def norm_sum(r, n):
                pe.wait_ge(s_sq, KC * r + n + 1)
                for b, (t0, w) in enumerate(HALVES[r]):
                    last = mm(ps[:, b, 0:w], ones, tmp[:, n % 2, t0:t0 + w], start=(n == 0), stop=(n == KC - 1))
                last.then_inc(s_ss, 1)

            pe.wait_ge(s_cact, 1)
            for s in range(MOD_FIRST):
                pe.wait_ge(filled[s], u.take(s, 1)[0] + 16)
                w = ring[s][:, :].rearrange("p (k n) -> p k n", k=KC)
                for k in range(KC):
                    last = mm(ps[0:1, 1 + s, :], c_act[:, k:k + 1], w[:, k, :], start=(k == 0), stop=(k == KC - 1))
                last.then_inc(freed[s], 1)
                for n in range(3 * s, min(3 * s + 3, KC)):
                    norm_sum(0, n)
            pe.drain().then_inc(s_mod, 1)
            pe.wait_ge(s_mrow, 1)
            for m in range(4 * MOD_FIRST):
                last = nc.tensor.transpose(ps[:, 6, m:m + 1], mod_row[:, m * P:(m + 1) * P], ident[0:1, 0:1])
            last.then_inc(s_mod, 1)

            pe.drain().then_inc(s_msum, 1)

            def mod_sum(src, at):
                for j in range(4):
                    last = mm(ps[:, 4, bass.ds(at + j, 1)], src[:, j * P:(j + 1) * P], ones[:, 0:1], start=True, stop=True)
                last.then_inc(s_msum, 1)

            def norm(r):
                for n in range(KC):
                    norm_sum(r, n)

            def ffn(r):
                def gate_up(s, have, n0):
                    pe.wait_ge(filled[s], have)
                    w = gu_view(s)
                    for j in range(2):
                        if not (isinstance(n0, int) and n0 == 0):
                            pe.wait_ge(s_hid, n0 + j - 1)
                        for g in range(2):
                            for k in range(KC):
                                if s == 0 and j == 0 and g == 0:
                                    pe.wait_ge(s_hn, 2 * KC * r + k + 1)
                                last = mm(ps[:, 2 * j + g, :], w[:, g, k, j * P:(j + 1) * P], hT[:, k, META:TOK],
                                          start=(k == 0), stop=(k == KC - 1))
                        last.then_inc(s_gu, 1)
                    pe.drain().then_inc(freed[s], 1)
                base = [u.take(s, 2, N_GU // 2)[0] for s in range(2)]
                if r == 0:
                    u.take(2, 1, N_GU)
                with pe.Fori(0, N_GU // 2) as i:
                    for s in range(2):
                        gate_up(s, base[s] + 32 + i * 32, (FC + 2) * r + 2 + i * 4 + 2 * s)
                        if r == 0:
                            pe.wait_ge(s_macc, i * 2 + (s + 1))
                            mod_sum(acc, i * 8 + 4 * s)
                gate_up(0, u.take(0, 2)[0] + 32, (FC + 2) * r + 2 + FC - 2)
                if r == 0:
                    pe.wait_ge(s_macc, N_GU)
                    mod_sum(acc, 4 * (N_GU - 1))
                    pe.wait_ge(s_mcp, 1)
                pe.wait_ge(s_hid, (FC + 2) * r + 2 + FC)
                for half in range(2):
                    bank = 4 if half == 0 else 0
                    for n, (f0, nf) in enumerate(DOWN_ITEMS):
                        s = down_slot(half, n)
                        pe.wait_ge(filled[s], u.take(s, 1)[0] + 16)
                        w = ring[s][:, 0:nf * 512].rearrange("p (f n) -> p f n", f=nf)
                        for f in range(nf):
                            for d in range(4):
                                last = mm(ps[:, bank + d, :], w[:, f, d * P:(d + 1) * P], aT[:, f0 + f, :],
                                          start=(f0 + f == 0), stop=(f0 + f == FC - 1))
                        pe.drain().then_inc(freed[s], 1)
                    pe.drain().then_inc(s_dn, 1)
                    if r == 0 and half == 0:
                        for s in MOD_LAST:
                            u.take(s, 1)
                if r == 0:
                    pe.wait_ge(s_d0, 1)
                    pe.wait_ge(s_macc, N_GU + len(MOD_LAST))
                    for n, src in enumerate(acc_last):
                        mod_sum(src, 4 * n)

            def qk_projection(s, have, i, fox, heads):
                w = ring[s][:, 0:KC * 384].rearrange("p (k w n) -> p k w n", k=KC, w=3)
                pe.wait_ge(filled[s], have + 48 + i * 48)
                for m in range(2):
                    if m == 1:
                        pe.wait_ge(s_o, heads)
                    for k in range(KC):
                        last = mm(ps[:, 7 - m, :], w[:, k, m, :], hT[:, k, META:TOK], start=(k == 0), stop=(k == KC - 1))
                    last.then_inc(s_qkv, 1)
                if fox:
                    pe.wait_ge(s_qc, i + 5)
                    pe.wait_ge(s_qsq, 2 * i + 1)
                    mm(ps[:, 7, :], const("head_ones"), buf1[:, 0:512], start=True, stop=True).then_inc(s_qss, 1)

            def pair(s, have, i, fox, after):
                w = ring[s][:, 0:KC * 384].rearrange("p (k w n) -> p k w n", k=KC, w=3)
                h0 = i * 2 + (8 if fox else 0)
                pr = i + (4 if fox else 0)
                if fox:
                    pe.wait_ge(s_qn, 2 * i + 2)
                else:
                    pe.wait_ge(s_qc, pr + 1)
                    pe.wait_ge(s_kvc, pr * 2 + 1)
                for hh in range(2):
                    h = h0 + hh
                    lo = hh * HD
                    if fox:
                        pe.wait_ge(s_fm, 2 * i + hh + 1)
                    for t in range(4):
                        n = P * (t + 1)
                        z = ps[:, [0, 0, 1, 2][t], (P if t == 1 else 0):(P if t == 1 else 0) + n]
                        last = mm(z, qT[lo:lo + HD, t * P:(t + 1) * P], kT[lo:lo + HD, 0:n], start=True, stop=not fox)
                        if fox:
                            mm(z, FL[lo:lo + HD, t * P:(t + 1) * P], FR[lo:lo + HD, 0:n], start=False, stop=True)
                            last = mm(z[:, t * P:n], ident, const("after"), start=False, stop=True, skip_group_check=True)
                    last.then_inc(s_z, 1)
                    if hh == 0:
                        for t in range(4):
                            for k in range(KC):
                                last = mm(ps[:, 7, t * P:(t + 1) * P], hT[:, k, META + t * P:META + (t + 1) * P], w[:, k, 2, :],
                                          start=(k == 0), stop=(k == KC - 1))
                        last.then_inc(s_qkv, 1)
                        pe.drain().then_inc(freed[s], 1)
                    elif after:
                        qk_projection(*after, h0 + 2)
                    pe.wait_ge(s_p, h + 1)
                    for (q, k), b in BLOCK_AT.items():
                        at = TILE_AT[q] + k * P
                        dst = ps[:, 3, b * P:(b + 1) * P] if b < 4 else \
                            ps[:, 4 + (b - 4) // 3, (b - 4) % 3 * P:(b - 4) % 3 * P + P]
                        last = nc.tensor.transpose(dst, buf2[:, at:at + P], ident)
                    last.then_inc(s_pt, 1)
                    if hh == 1 and after and after[3]:
                        pe.wait_ge(s_qsq, 2 * after[2] + 2)
                        pe.wait_ge(s_qstd, 2 * after[2] + 1)
                        mm(ps[:, 7, :], const("head_ones"), buf1[:, 512:1024], start=True, stop=True).then_inc(s_qss, 1)
                    pe.wait_ge(s_ptc, 2 * h + 2)
                    if hh == 0:
                        pe.wait_ge(s_kvc, pr * 2 + 2)
                    elif after:
                        pe.wait_ge(s_kvc, pr * 2 + 3)
                    pe.wait_ge(s_o, h + 1)
                    for q in range(4):
                        for k in range(q + 1):
                            last = mm(ps[0:HD, 6, q * P:(q + 1) * P], vt[:, k, lo:lo + HD], PT[:, BLOCK_AT[q, k], :],
                                      start=(k == 0), stop=(k == q))
                    last.then_inc(s_pv, 1)

            phase_left(pe, 2)
            ffn(0)
            phase_end(pe, 3)
            norm(1)
            phase_left(pe, 4)
            for k in range(KC):
                pe.wait_ge(s_hn, KC + k + 1)
                last = mm(ps[0:8, 5, :], wf[:, k, :], hT[:, k, META:TOK], start=(k == 0), stop=(k == KC - 1))
            last.then_inc(s_fp, 1)
            phase_left(pe, 5)
            have2, have3 = u.take(2, 3, 4)[0], u.take(3, 3, 4)[0]
            qk_projection(2, have2, 0, False, 1)
            with pe.Fori(0, 3) as i:
                pair(2, have2, i, False, (2, have2, i + 1, False))
            pair(2, have2, 3, False, (3, have3, 0, True))
            with pe.Fori(0, 3) as i:
                pair(3, have3, i, True, (3, have3, i + 1, True))
            pair(3, have3, 3, True, None)
            phase_end(pe, 6)
            wo = [ring[s][:, :].rearrange("p (f n) -> p f n", f=4) for s in (4, 5)]
            for n, s in enumerate((4, 5)):
                pe.wait_ge(filled[s], u.take(s, 1)[0] + 16)
            phase_left(pe, 7)
            for d in range(KC):
                for f in range(8):
                    last = mm(ps[:, d, :], wo[f // 4][:, f % 4, d * P:(d + 1) * P], oT[:, f, :], start=(f == 0), stop=(f == 7))
                last.then_inc(s_wo, 1)
                if d >= 2:
                    norm_sum(2, d - 2)
            for s in (4, 5):
                pe.drain().then_inc(freed[s], 1)
            norm_sum(2, KC - 2)
            norm_sum(2, KC - 1)
            phase_left(pe, 8)
            ffn(1)
            phase_end(pe, 9)
            norm(3)
            phase_left(pe, 10)
            item = -1
            for n, (it, c0, m, wide, _) in enumerate(UNITS):
                if it != item:
                    if item >= 0:
                        pe.drain().then_inc(freed[2 + item], 1)
                    item = it
                    pe.wait_ge(filled[2 + it], u.take(2 + it, 1)[0] + 16)
                if n >= 4:
                    pe.wait_ge(s_p2c[n % 2], (n - 4) // 2 + 1)
                b = 2 * (n % 4)
                for k in range(KC):
                    if n == 0:
                        pe.wait_ge(s_hn, KC * 3 + k + 1)
                    flags = dict(start=(k == 0), stop=(k == KC - 1))
                    if wide is None:
                        t = n - 4
                        last = mm(ps[0:m, b, :], hT[:, k, TILE0[t]:TILE0[t] + m], w2(it)[:, k, :], **flags)
                    elif wide:
                        for g in range(2):
                            last = mm(ps[0:m, b + g, 0:264], w2(it)[:, k, c0:c0 + m], hT[:, k, g * 264:(g + 1) * 264], **flags)
                    else:
                        last = mm(ps[0:m, b, :], w2(it)[:, k, c0:c0 + m], hT[:, k, META:TOK], **flags)
                last.then_inc(s_p2, 1)
            pe.drain().then_inc(freed[5], 1)
            phase_end(pe, 11)

            pe.wait_ge(filled[2], u.take(2, 3)[0] + 48)
            for p in range(2):
                for g in range(2):
                    last = mm(ps[:, 2 * p + g, 0:264], w_a2[:, p * P:(p + 1) * P], aL[0:16, g * 264:(g + 1) * 264],
                              start=True, stop=True)
            last.then_inc(s_la, 1)
            pe.wait_ge(s_lq, 1)
            for k in range(2):
                last = mm(ps[:, 4, :], ones, eb[:, k, :], start=(k == 0), stop=(k == 1))
            for g in range(2):
                last = mm(ps[:, 6 + g, 0:264], ones, tmp[:, 0, g * 264:(g + 1) * 264], start=True, stop=True)
            last.then_inc(s_lss, 1)
            pe.wait_ge(s_kd, 1)
            for t in range(5):
                for p in range(2):
                    last = nc.tensor.transpose(ps[0:TILEN[t], t // 2, (t % 2) * 256 + p * P:(t % 2) * 256 + (p + 1) * P],
                                               kd[:, p, TILE0[t]:TILE0[t] + TILEN[t]], ident)
            last.then_inc(s_kt, 1)
            pe.wait_ge(s_ktc, 1)
            for n in range(N_CHUNK):
                t, lo, rows = (0, 0, META) if n == 0 else (1 + (n - 1) // 2, (n - 1) % 2 * CHUNK, CHUNK)
                if n >= 4:
                    pe.wait_ge(s_st, n - 3)
                for p in range(2):
                    last = mm(ps[:, 4 + n % 4, p * 256:(p + 1) * 256], kdtok[lo:lo + rows, t, p * P:(p + 1) * P],
                              gv[lo:lo + rows, t, p * 256:(p + 1) * 256], start=True, stop=True)
                last.then_inc(s_U, 1)
            phase_end(pe, 12)
            def gla_scores(h):
                p, lo = h // 2, h % 2 * HD
                for b in range(NT):
                    last = mm(ps[:, 0, b * P:(b + 1) * P], km[lo:lo + HD, p, META + b * P:META + (b + 1) * P],
                              gq[lo:lo + HD, p, b * P:(b + 1) * P], start=True, stop=True)
                last.then_inc(s_at2, 1)
            gla_scores(0)
            for h in range(GH):
                p, lo = h // 2, h % 2 * HD
                out_bank = 1 + 2 * (h % 2)
                pe.wait_ge(s_atm, h + 1)
                if h >= 2:
                    pe.wait_ge(s_gf, h - 1)
                for b in range(NT):
                    mm(ps[:, out_bank, b * P:(b + 1) * P], gv[:, 1 + b, h * P:(h + 1) * P], attS[:, b, :], start=(b == 0), stop=True,
                       skip_group_check=True)
                for n in range(N_CHUNK):
                    last = mm(ps[:, out_bank, n * CHUNK:(n + 1) * CHUNK], states[lo:lo + HD, p, n + 1, :],
                              gq[lo:lo + HD, p, n * CHUNK:(n + 1) * CHUNK], start=False, stop=True, skip_group_check=True)
                last.then_inc(s_go, 1)
                if h + 1 < GH:
                    gla_scores(h + 1)
                pe.wait_ge(s_gsq, h + 1)
                mm(ps[:, 2, :], ones, osq, start=True, stop=True).then_inc(s_gss, 1)
            phase_end(pe, 13)

            NU = 0
            for h in range(GH):
                for kind in range(3):
                    b = 2 * (NU % 3)
                    if NU >= 3:
                        pe.wait_ge(s_mb, NU - 2)
                    for k in range(2 if kind < 2 else 1):
                        if kind == 0:
                            last = mm(ps[:, b, :], w_qb[:, k, h * 192:h * 192 + P], ql[:, k, :], start=(k == 0), stop=(k == 1))
                        elif kind == 1:
                            last = mm(ps[0:ROPE, b, :], w_qb[:, k, h * 192 + P:h * 192 + 192], ql[:, k, :], start=(k == 0), stop=(k == 1))
                        else:
                            for g in range(2):
                                last = mm(ps[:, b + g, 0:264], w_kvb[:, h * 256:h * 256 + P], kv[:, g * 264:(g + 1) * 264],
                                          start=True, stop=True)
                    last.then_inc(s_mz, 1)
                    NU += 1
            for t in range(5):
                if t >= 2:
                    pe.wait_ge(s_mtc, t - 1)
                mm(ps[0:TILEN[t], 6 + t % 2, :], kv[:, TILE0[t]:TILE0[t] + TILEN[t]],
                   w_kvb.rearrange("p (h n) -> p h n", h=GH)[:, :, P:2 * P], start=True, stop=True).then_inc(s_mt, 1)
            phase_end(pe, 14)

            def scores(un):
                h, t = un // NT, un % NT
                b = 2 * (un % 2)
                q0 = t * P
                for first, (lhs, rhs) in enumerate(((qn[:, h, q0:q0 + P], kn[:, h, :]), (qr[:, h, q0:q0 + P], kr[0:ROPE, :]))):
                    mm(ps[:, b, 512 - META:512], lhs, rhs[:, 0:META], start=(first == 0), stop=(first == 1))
                    last = mm(ps[:, b + 1, 0:P * (t + 1)], lhs, rhs[:, META:META + P * (t + 1)], start=(first == 0), stop=(first == 1))
                last.then_inc(s_mz, 1)
            scores(0)
            scores(1)
            for un in range(GH * NT):
                h, t = un // NT, un % NT
                pe.wait_ge(s_mp, un + 1)
                src = PB[un % 2]
                nc.tensor.transpose(ps[0:META, 5, 0:P], src[:, 0:META], ident)
                for b in range(t + 1):
                    last = nc.tensor.transpose(ps[:, 4, b * P:(b + 1) * P], src[:, META + b * P:META + (b + 1) * P], ident)
                last.then_inc(s_mt, 1)
                if un + 2 < GH * NT:
                    pe.wait_ge(s_me, un + 1)
                    scores(un + 2)
                pe.wait_ge(s_mtc, 5 + un + 1)
                if un >= 2:
                    pe.wait_ge(s_mo, un - 1)
                dst = ps[:, 6 + un % 2, 0:P]
                mm(dst, mv[0:META, 0, h * P:(h + 1) * P], mPT[0:META, 0, :], start=True, stop=False)
                for b in range(t + 1):
                    last = mm(dst, mv[:, 1 + b, h * P:(h + 1) * P], mPT[:, 1 + b, :], start=False, stop=(b == t))
                last.then_inc(s_mpv, 1)
            phase_end(pe, 15)
            u.take(0, 0), u.take(1, 0)
            pe.drain().then_inc(freed[2], 1)
            for n, s in enumerate((4, 5)):
                pe.wait_ge(filled[s], u.take(s, 1)[0] + 16)
            wo = [ring[s][:, :].rearrange("p (f n) -> p f n", f=4) for s in (4, 5)]
            for t in range(NT):
                b = 4 * (t % 2)
                if t >= 2:
                    pe.wait_ge(s_h2, t - 1)
                for k in range(KC):
                    last = nc.tensor.transpose(ps[:, b + k // 4, (k % 4) * P:(k % 4 + 1) * P],
                                               xT[:, k, META + t * P:META + (t + 1) * P], ident)
                last.then_inc(s_xr, 1)
                for g in range(2):
                    for f in range(8):
                        last = mm(ps[:, b + 2 + g, :], o2[:, f, t * P:(t + 1) * P], wo[f // 4][:, f % 4, g * 512:(g + 1) * 512],
                                  start=(f == 0), stop=(f == 7))
                last.then_inc(s_xr, 1)
            for s in (4, 5):
                pe.drain().then_inc(freed[s], 1)
            phase_end(pe, 16)
            for k in range(KC):
                if k == 0:
                    pe.wait_ge(s_un, NT)
                for t in range(NT):
                    last = nc.tensor.transpose(ps[:, k, t * P:(t + 1) * P], u2[:, t, k * P:(k + 1) * P], ident)
                last.then_inc(s_ut, 1)
            pe.wait_ge(s_utc, KC)
            pe.wait_ge(filled[3], u.take(3, 3)[0] + 48)
            for t in range(NT):
                for k in range(KC):
                    last = mm(ps[:, 0, t * 72:(t + 1) * 72], uT[:, k, t * P:(t + 1) * P], wr[:, k, :],
                              start=(k == 0), stop=(k == KC - 1))
            last.then_inc(s_lg, 1)
            for s in (0, 1, 3):
                pe.drain().then_inc(freed[s], 1)
            pe.wait_ge(s_M, 1)
            for t in [NT] + list(range(NT)):
                for q in range(min(t + 1, NT)):
                    last = mm(ps[:, 1 if t < NT else 5, t % NT * NE:(t % NT + 1) * NE], const("strict_t") if q == t else ones,
                              Mh[:, q, :], start=(q == 0), stop=(q == min(t, NT - 1)))
                if t in (NT, NT - 1):
                    last.then_inc(s_rk, 1)
            pe.wait_ge(s_be, 1)
            nc.tensor.transpose(ps[0:1, 4, 0:P], expert_col, ident).then_inc(s_tb, 1)
            pe.drain().then_inc(s_mg, 1)
            pe.drain().then_inc(s_mu, 1)
            pe.drain().then_inc(s_my, 1)
            pe.wait_ge(s_pos, 1)
            for w in range(2):
                for n in range(2 * NT):
                    last = mm(ps[0:CAP, 2 + w, 0:TAB], slot_hot[w][:, n, :], block_hot[:, n, :], start=(n == 0), stop=(n == 2 * NT - 1))
            last.then_inc(s_tb, 1)
            phase_end(pe, 17)
            phase_end(pe, 18)

            n_more = pe.value_load(pairs_ix[0:1, 1:2], min_val=1, max_val=MAX_PAIRS - 1)
            first = [u.take(s, 1)[0] for s in range(N_SLOT)]

            def turn_rows(j):
                for k in range(KC):
                    last = nc.tensor.transpose(ps[:, 4 + j, k * CAP:(k + 1) * CAP],
                                               xs[j].rearrange("p (m k) -> p k m", k=KC)[:, k, :], ident[0:CAP, 0:CAP])
                last.then_inc(s_xt, 1)

            def gate_up(j, n, i16, rows, hidden=None):
                pe.wait_ge(s_xtc, n)
                for g in range(2):
                    pe.wait_ge(filled[3 * j + g], i16 + (first[3 * j + g] + 16))
                w = [ring[3 * j + g][:, :].rearrange("p (k n) -> p k n", k=KC) for g in range(2)]
                for k in range(KC):
                    if k == KC - 1:
                        if rows is not None:
                            pe.wait_ge(s_gat[1 - j], rows)
                        if hidden is not None:
                            pe.wait_ge(s_ha, hidden)
                    for g in range(2):
                        last = mm(ps[g * CAP:(g + 1) * CAP, j, :], xsT[j][:, k, :], w[g][:, k, :], start=(k == 0), stop=(k == KC - 1))
                        if k == KC - 1:
                            last.then_inc((s_mg, s_mu)[g], 1)

            def turn_hidden(j, n):
                if n is not None:
                    pe.wait_ge(s_ha, n)
                for c in range(4):
                    last = nc.tensor.transpose(ps[:, 6 + j, c * CAP:(c + 1) * CAP], hrow[j][:, c * P:(c + 1) * P],
                                               ident[0:CAP, 0:CAP])
                last.then_inc(s_ta, 1)

            def down(j, n, i16):
                pe.wait_ge(filled[3 * j + 2], i16 + (first[3 * j + 2] + 16))
                pe.wait_ge(s_hd, n)
                w = ring[3 * j + 2][:, :].rearrange("p (f n) -> p f n", f=4)
                for c in range(4):
                    for g in range(2):
                        last = mm(ps[g * CAP:(g + 1) * CAP, 2 + j, :], hid[j][:, c, :], w[:, c, g * 512:(g + 1) * 512],
                                  start=(c == 0), stop=(c == 3))
                last.then_inc(s_my, 1)

            pe.wait_ge(s_gat[0], 16)
            pe.drain().then_inc(s_mg, 1)
            pe.drain().then_inc(s_mu, 1)
            pe.drain().then_inc(s_my, 1)
            turn_rows(0)
            gate_up(0, 1, 0, 16)
            turn_rows(1)
            with pe.Fori(0, n_more) as i:
                gate_up(1, i * 2 + 2, i * 16, i * 16 + 32, i * 2 + 1)
                turn_hidden(0, None)
                turn_rows(0)
                down(0, i * 2 + 1, i * 16)
                gate_up(0, i * 2 + 3, i * 16 + 16, i * 16 + 32, i * 2 + 2)
                turn_hidden(1, None)
                turn_rows(1)
                down(1, i * 2 + 2, i * 16)
            before = pe.snap(n_more * 2)
            before16 = pe.snap(n_more * 16)
            gate_up(1, before + 2, before16, None, before + 1)
            turn_hidden(0, None)
            down(0, before + 1, before16)
            pe.wait_ge(s_ha, before + 2)
            mm(ps[:, 7, 0:P], ident, ident, start=True, stop=True)
            turn_hidden(1, None)
            down(1, before + 2, before16)
            phase_end(pe, 19)
            phase_end(pe, 20)
            phase_end(pe, 21)
            phase_end(pe, 22)

        @block.scalar
        def _(act):
            av = nc.scalar.activation
            act.wait_ge(s_in, 64)
            av(c_exp, col("c"), ACT.Exp, scale=-1.0).then_inc(s_cexp, 1)
            phase_end(act, 1)

            def norm_std(r):
                t0, t1 = HALVES[r][0][0], TOK
                for k in range(KC):
                    if r == 2:
                        act.wait_ge(s_xu, k + 1)
                    if k >= 2:
                        act.wait_ge(s_ss, KC * r + k - 1)
                    av(tmp[:, k % 2, t0:t1], xT[:, k, t0:t1], ACT.Square).then_inc(s_sq, 1)
                act.wait_ge(s_ss, KC * (r + 1))
                for b, (h0, w) in enumerate(HALVES[r]):
                    last = av(rstd[:, h0:h0 + w], ps[:, b, 0:w], ACT.Sqrt, scale=1.0 / D, bias=eps_col[:, 0:1])
                last.then_inc(s_std, 1)

            def norm_scaled(r):
                t0, t1 = HALVES[r][0][0], TOK
                if r == 0:
                    act.wait_ge(s_scale, 1)
                for k in range(KC):
                    act.wait_ge(s_nx, KC * r + k + 1)
                    if r < 3:
                        av(hT[:, k, t0:t1], hT[:, k, t0:t1], ACT.Identity, scale=scale[r][:, k:k + 1],
                           bias=modT[:, 24 * r + k:24 * r + k + 1]).then_inc(s_hn, 1)
                    else:
                        av(hT[:, k, t0:t1], hT[:, k, t0:t1], ACT.Copy, scale=col("mix_norm_2", k)).then_inc(s_hn, 1)

            def ffn(r):
                def chunk(j, n):
                    act.wait_ge(s_gu, n + 1)
                    act.wait_ge(s_hid, n + 2 * r + 1)
                    av(eb[:, j, :], ps[:, 2 * j, :], ACT.Exp, scale=-1.0).then_inc(s_ge, 1)
                with act.Fori(0, FC // 2) as i:
                    for j in range(2):
                        chunk(j, FC * r + i * 2 + j)

            def norm(r):
                norm_std(r)
                norm_scaled(r)

            norm_std(0)
            act.wait_ge(s_mod, 1)
            av(mod_row.rearrange("p (b n) -> p b n", b=MOD_FIRST), ps[0:1, 1:1 + MOD_FIRST, :], ACT.Copy).then_inc(s_mrow, 1)
            norm_scaled(0)
            phase_end(act, 2)
            ffn(0)
            phase_end(act, 3)
            norm(1)
            phase_end(act, 4)
            act.wait_ge(s_f1, 1)
            av(fB, fA, ACT.Abs).then_inc(s_act, 1)
            act.wait_ge(s_act, 1)
            av(fB, fB, ACT.Exp, scale=-1.0).then_inc(s_act, 1)
            act.wait_ge(s_act, 2)
            av(fB, fB, ACT.Ln, bias=1.0).then_inc(s_f1, 1)
            phase_end(act, 5)

            def pair_in(i, fox):
                pr = i + (4 if fox else 0)
                act.wait_ge(s_qkv, pr * 3 + 1)
                av(qT, ps[:, 7, :], ACT.Copy, scale=1.0 if fox else HD ** -0.5).then_inc(s_qc, 1)
                if fox:
                    av(buf1[:, 0:512], ps[:, 7, :], ACT.Square).then_inc(s_qsq, 1)
                    act.wait_ge(s_kvc, pr * 2 + 1)
                    av(buf1[:, 512:1024], kT, ACT.Square).then_inc(s_qsq, 1)
                    qk_deviation(i, 0)

            def qk_deviation(i, m):
                act.wait_ge(s_qss, 2 * i + m + 1)
                av(buf1[:, m * 512:(m + 1) * 512], ps[:, 7, :], ACT.Sqrt, scale=1.0 / HD, bias=eps_col[:, 0:1])\
                    .then_inc(s_qstd, 1)

            def stick_pair(i, last_pair):
                for hh in range(2):
                    h = i * 2 + hh
                    act.wait_ge(s_z, h + 1)
                    av(buf1[:, 0:768].rearrange("p (b n) -> p b n", b=2), ps[:, 0:2, 0:384], ACT.Abs)
                    av(buf1[:, 768:TRI], ps[:, 2, :], ACT.Abs).then_inc(s_act, 1)
                    act.wait_ge(s_act, i * 4 + 3 + 2 * hh)
                    av(buf1, buf1, ACT.Exp, scale=-1.0).then_inc(s_act, 1)
                    act.wait_ge(s_act, i * 4 + 4 + 2 * hh)
                    av(buf1, buf1, ACT.Ln, bias=1.0).then_inc(s_sp, 1)
                    if hh == 1 and not last_pair:
                        pair_in(i + 1, False)
                    act.wait_ge(s_zz, h + 1)
                    av(buf2, buf1, ACT.Exp).then_inc(s_p, 1)
                    if hh == 1 and last_pair:
                        act.wait_ge(s_p, h + 1)
                        pair_in(0, True)
                    act.wait_ge(s_pt, h + 1)
                    av(PT[:, 4:10, :].rearrange("p (b m) q -> p b (m q)", b=2), ps[:, 4:6, 0:384], ACT.Copy).then_inc(s_ptc, 1)
                    if hh == 1 and last_pair:
                        qk_deviation(0, 1)

            def forget_pair(i, last_pair):
                for hh in range(2):
                    h = i * 2 + hh + 8
                    act.wait_ge(s_mx, i * 2 + hh + 1)
                    for t in range(4):
                        n = P * (t + 1)
                        z = ps[:, [0, 0, 1, 2][t], (P if t == 1 else 0):(P if t == 1 else 0) + n]
                        last = av(buf2[:, TILE_AT[t]:TILE_AT[t] + n], z, ACT.Exp, bias=fox_s[:, t:t + 1],
                                  accum_out=fox_s[:, 4 + t:5 + t])
                    last.then_inc(s_e, 1)
                    if hh == 1 and not last_pair:
                        pair_in(i + 1, True)
                    act.wait_ge(s_pt, h + 1)
                    av(PT[:, 4:10, :].rearrange("p (b m) q -> p b (m q)", b=2), ps[:, 4:6, 0:384], ACT.Copy).then_inc(s_ptc, 1)
                    if hh == 1 and not last_pair:
                        qk_deviation(i + 1, 1)
            pair_in(0, False)
            with act.Fori(0, 3) as i:
                stick_pair(i, False)
            stick_pair(3, True)
            with act.Fori(0, 3) as i:
                forget_pair(i, False)
            forget_pair(3, True)
            phase_end(act, 6)
            phase_left(act, 7)
            norm(2)
            phase_end(act, 8)
            ffn(1)
            phase_end(act, 9)
            norm(3)
            phase_end(act, 10)
            for n in range(1, len(UNITS), 2):
                act.wait_ge(s_p2, n + 1)
                av(unit_dst(n), unit_psum(n), ACT.Copy, scale=HD ** -0.5 if n == 1 else 1.0).then_inc(s_p2c[1], 1)
                if n in GATE_PAIRS:
                    h = GATE_PAIRS[n]
                    act.wait_ge(s_p2c[0], (n + 1) // 2)
                    act.wait_ge(s_p2c[1], n // 2)
                    av(gexp[:, h:h + 2, :], gr[:, h:h + 2, :], ACT.Exp, scale=-1.0).then_inc(s_gex, 1)
            phase_end(act, 11)
            av(eb[:, :, :], ql, ACT.Square)
            av(tmp[:, 0, :], kv, ACT.Square).then_inc(s_lq, 1)
            act.wait_ge(s_dt, 1)
            steps = [2 + 4 * 4]

            def link(ins):
                ins.then_inc(s_act, 1)
                steps[0] += 1
                act.wait_ge(s_act, steps[0])
            link(av(km, Sc, ACT.Abs))
            link(av(km, km, ACT.Exp, scale=-1.0))
            av(km, km, ACT.Ln, bias=1.0).then_inc(s_dsp, 1)
            act.wait_ge(s_lss, 1)
            av(tmp[:, 1, 0:SEQ], ps[:, 4, :], ACT.Sqrt, scale=1.0 / 256, bias=eps_col[:, 0:1])
            av(halves(tmp[:, 0, :]), ps[:, 6:8, 0:264], ACT.Sqrt, scale=1.0 / P, bias=eps_col[:, 0:1]).then_inc(s_lstd, 1)
            act.wait_ge(s_S, 1)
            av(km, Sc, ACT.Exp, scale=1.0 / 16).then_inc(s_dx, 1)
            av(glst[:, 0:18].rearrange("p (c n) -> p c n", c=2), Sc[:, :, META - 1::CHUNK], ACT.Exp, scale=-1.0 / 16).then_inc(s_dx, 1)
            av(eb[:, :, :], Sc[:, :, META:TOK], ACT.Exp, scale=-1.0 / 16).then_inc(s_dx, 1)
            act.wait_ge(s_S, 2)
            av(kd, kd, ACT.Exp, scale=1.0 / 16).then_inc(s_dx, 1)
            act.wait_ge(s_kt, 1)
            av(kdtok[:, 1:3, :], flat[:, 256:768].rearrange("p (t n) -> p t n", t=2), ACT.Copy)
            av(kdtok[:, 3:5, :], flat[:, 768:1280].rearrange("p (t n) -> p t n", t=2), ACT.Copy)
            av(kdtok[0:META, 0, :], ps[0:META, 0, 0:256], ACT.Copy).then_inc(s_ktc, 1)
            phase_end(act, 12)
            for h in range(GH):
                act.wait_ge(s_go, h + 1)
                av(osq, ps[:, 1 + 2 * (h % 2), :], ACT.Square).then_inc(s_gsq, 1)
                act.wait_ge(s_gss, h + 1)
                if h >= 1:
                    act.wait_ge(s_gf, h)
                av(orst, ps[:, 2, :], ACT.Sqrt, scale=1.0 / P, bias=eps_col[:, 0:1]).then_inc(s_gstd, 1)
            phase_end(act, 13)
            for t in range(5):
                act.wait_ge(s_mt, t + 1)
                av(mv[0:TILEN[t], t, :], ps[0:TILEN[t], 6 + t % 2, :], ACT.Copy).then_inc(s_mtc, 1)
            phase_end(act, 14)

            def mla_exp(un):
                n = META + P * (un % NT + 1)
                act.wait_ge(s_mb, 12 + un + 1)
                av(PB[un % 2][:, 0:n], mla_z(un), ACT.Exp, bias=glst[:, 20 + un % 2:21 + un % 2],
                   accum_out=glst[:, 22 + un % 2:23 + un % 2]).then_inc(s_me, 1)
            mla_exp(0)
            mla_exp(1)
            for un in range(GH * NT):
                t = un % NT
                act.wait_ge(s_mt, 5 + un + 1)
                av(mPT[0:META, 0, :], ps[0:META, 5, 0:P], ACT.Copy)
                av(mPT[:, 1:2 + t, :].rearrange("p b q -> p (b q)"), ps[:, 4, 0:P * (t + 1)], ACT.Copy).then_inc(s_mtc, 1)
                if un + 2 < GH * NT:
                    mla_exp(un + 2)
            phase_end(act, 15)
            for t in range(NT):
                b = 4 * (t % 2)
                act.wait_ge(s_xr, 2 * t + 1)
                av(h2[:, t, :].rearrange("p (b n) -> p b n", b=2), ps[:, b:b + 2, :], ACT.Copy).then_inc(s_xrc, 1)
                act.wait_ge(s_rn, t + 1)
                av(glst[:, 31:32], glst[:, 29:30], ACT.Sqrt).then_inc(s_rnq, 1)
            phase_end(act, 16)
            act.wait_ge(s_rx, 1)
            av(rx[:, 0:NT * NG], rx[:, 0:NT * NG], ACT.Exp)
            av(rx[:, NT * NG:NT * NG + NT], rx[:, NT * NG:NT * NG + NT], ACT.Exp).then_inc(s_rx, 1)
            phase_end(act, 17)
            act.drain().then_inc(s_ysf, 2)
            n_more = act.value_load(pairs_ix[0:1, 1:2], min_val=1, max_val=MAX_PAIRS - 1)
            phase_end(act, 18)

            def rows_in(j, n):
                act.wait_ge(s_xt, n)
                av(xsT[j].rearrange("p k s -> p (k s)"), ps[:, 4 + j, :], ACT.Copy).then_inc(s_xtc, 1)

            def gate_exp(j, n):
                act.wait_ge(s_mg, n + 2)
                av(sg[j], ps[0:CAP, j, :], ACT.Exp, scale=-1.0).then_inc(s_eg, 1)

            def rows_out(j, n):
                act.wait_ge(s_my, n + 2)
                act.wait_ge(s_ysf, n)
                for g in range(2):
                    last = av(ys[j][:, g * 512:(g + 1) * 512], ps[g * CAP:(g + 1) * CAP, 2 + j, :], ACT.Copy)
                last.then_inc(s_yc, 1)
            rows_in(0, 1)
            gate_exp(0, 1)
            rows_in(1, 2)
            with act.Fori(0, n_more) as i:
                gate_exp(1, i * 2 + 2)
                rows_in(0, i * 2 + 3)
                rows_out(0, i * 2 + 1)
                gate_exp(0, i * 2 + 3)
                rows_in(1, i * 2 + 4)
                rows_out(1, i * 2 + 2)
            before = act.snap(n_more * 2)
            gate_exp(1, before + 2)
            rows_out(0, before + 1)
            rows_out(1, before + 2)
            phase_end(act, 19)
            phase_end(act, 20)
            phase_end(act, 21)
            for t in range(NT):
                act.wait_ge(s_y2f, t + 1)
                av(sq_row, h2[:, t, :], ACT.Square, accum_out=glst[:, 32 + t:33 + t]).then_inc(s_fsq, 1)
                act.wait_ge(s_fsq, t + 1)
                av(glst[:, 36 + t:37 + t], glst[:, 32 + t:33 + t], ACT.Sqrt, scale=1.0 / D, bias=eps_col[:, 0:1]).then_inc(s_fst, 1)
            phase_end(act, 22)

        @block.vector
        def _(dve):
            v = nc.vector
            steps = [0]
            vec_sem = [s_vec]
            rn = [0]

            def link(ins):
                ins.then_inc(vec_sem[0], 1)
                steps[0] += 1
                dve.wait_ge(vec_sem[0], steps[0])

            def row_norm(t):
                link(v.tensor_tensor_reduce(out=sq_row, in0=h2[:, t, :], in1=h2[:, t, :], scale=1.0, scalar=0.0, op0=ALU.mult,
                                            op1=ALU.add, accum_out=glst[:, 28:29]))
                v.tensor_scalar(glst[:, 29:30], glst[:, 28:29], 1.0 / D, EPS, ALU.mult, ALU.add).then_inc(s_rn, 1)
                rn[0] += 1
                dve.wait_ge(s_rnq, rn[0])
                link(v.reciprocal(glst[:, 30:31], glst[:, 31:32]))

            v.memset(eps_col[:, :], EPS).then_inc(s_o, 1)
            for k in range(KC):
                dve.wait_ge(s_tr, k + 1)
                v.tensor_copy(xT[:, k, META:TOK], ps[:, k, :]).then_inc(s_trc, 1)
            dve.wait_ge(s_tr, KC + 1)
            v.tensor_copy(xT[:, :, 0:META], ps[:, 0, 0:KC * META].rearrange("p (k t) -> p k t", k=KC))
            dve.wait_ge(s_cexp, 1)
            link(v.tensor_scalar(c_act, c_exp, 1.0, None, ALU.add))
            link(v.reciprocal(c_exp, c_act))
            v.tensor_tensor(c_act, c_exp, col("c"), ALU.mult).then_inc(s_cact, 1)
            phase_end(dve, 1)

            def norm_scale(r):
                v.scalar_tensor_tensor(out=scale[r], in0=modT[:, 24 * r + 8:24 * r + 16], scalar=1.0,
                                       in1=col(("g_ffn1", "g_mix", "g_ffn2")[r]), op0=ALU.add, op1=ALU.mult).then_inc(s_scale, 1)

            def out_gate(r):
                v.tensor_scalar(gate[r], modT[:, 24 * r + 16:24 * r + 24], 1.0, 1.0 if r == 1 else 0.5, ALU.add, ALU.mult)

            def mod_item(s, have, dst):
                dve.wait_ge(filled[s], have)
                w = ring[s][:, :].rearrange("p (k n) -> p k n", k=KC)
                v.tensor_scalar(dst, w[:, 0, :], c_act[:, 0:1], None, ALU.mult).then_inc(s_mstep, 1)
                for k in range(1, KC):
                    yield k
                    last = v.scalar_tensor_tensor(out=dst, in0=w[:, k, :], scalar=c_act[:, k:k + 1], in1=dst,
                                                  op0=ALU.mult, op1=ALU.add)
                    last.then_inc(s_mstep if k < KC - 1 else s_macc, 1)
            v.tensor_scalar(gqs[:, :], col("g_q"), HD ** -0.5, None, ALU.mult)

            def norm(r):
                t0, t1 = HALVES[r][0][0], TOK
                if r in (0, 2):
                    v.tensor_copy(fox_s[:, 12:13], eps_col[:, 0:1]).then_inc(s_hid, 1)
                    v.tensor_copy(fox_s[:, 13:14], eps_col[:, 0:1]).then_inc(s_hid, 1)
                dve.wait_ge(s_std, r + 1)
                link(v.reciprocal(rstd[:, t0:t1], rstd[:, t0:t1]))
                for k in range(KC):
                    v.tensor_tensor(hT[:, k, t0:t1], xT[:, k, t0:t1], rstd[:, t0:t1], ALU.mult).then_inc(s_nx, 1)

            def ffn(r):
                at = steps[0]
                with dve.Fori(0, FC // 2) as i:
                    if r == 0:
                        dve.wait_ge(s_msum, i + 1)
                        for k in mod_item(2, i * 16 + 32, acc):
                            dve.wait_ge(s_mstep, i * (KC - 1) + k)
                        dve.wait_ge(s_macc, i + 1)
                        v.tensor_copy(fox_s[:, 14:15], eps_col[:, 0:1]).then_inc(freed[2], 1)
                    for j in range(2):
                        k = at + i * 6 + 3 * j
                        dve.wait_ge(s_ge, FC * r + i * 2 + j + 1)
                        v.tensor_scalar(eb[:, j, :], eb[:, j, :], 1.0, None, ALU.add).then_inc(s_vec, 1)
                        dve.wait_ge(s_vec, k + 1)
                        v.reciprocal(eb[:, j, :], eb[:, j, :]).then_inc(s_vec, 1)
                        dve.wait_ge(s_vec, k + 2)
                        v.tensor_tensor(eb[:, j, :], ps[:, 2 * j, :], eb[:, j, :], ALU.mult).then_inc(s_vec, 1)
                        dve.wait_ge(s_vec, k + 3)
                        v.tensor_tensor(aT[:, bass.ds(i * 2 + j, 1), :], ps[:, 2 * j + 1:2 * j + 2, :],
                                        eb[:, j:j + 1, :], ALU.mult).then_inc(s_hid, 1)
                steps[0] += 3 * FC
                if r == 0:
                    dve.wait_ge(s_msum, N_GU + 1)
                    link(v.tensor_tensor(modT[:, 16:60], ps[:, 4, 0:44], col("b_mod")[:, 16:60], ALU.add))
                    out_gate(0)
                    norm_scale(1)
                    out_gate(1)
                    dve.drain().then_inc(s_mcp, 1)
                    for n, s in enumerate(MOD_LAST):
                        have = (16 + 32 * (N_GU + 1) // 2, 16 + 32 * (N_GU // 2), 16 + 16 * N_GU)[n] + 16
                        for k in mod_item(s, have, acc_last[n]):
                            dve.wait_ge(s_mstep, (N_GU + n) * (KC - 1) + k)
                        dve.wait_ge(s_macc, N_GU + n + 1)
                        dve.drain().then_inc(freed[s], 1)
                for half in range(2):
                    dve.wait_ge(s_dn, 2 * r + half + 1)
                    for d in range(4):
                        k = 4 * half + d
                        v.scalar_tensor_tensor(out=xT[:, k, META:TOK], in0=ps[:, (4 if half == 0 else 0) + d, :],
                                               scalar=gate[2 * r][:, k:k + 1], in1=xT[:, k, META:TOK],
                                               op0=ALU.mult, op1=ALU.add)
                    if half == 0 and r == 0:
                        dve.drain().then_inc(s_d0, 1)
                if r == 0:
                    dve.wait_ge(s_msum, N_GU + len(MOD_LAST) + 1)
                    link(v.tensor_tensor(modT[:, 60:72], ps[:, 4, 0:12], col("b_mod")[:, 60:72], ALU.add))
                    norm_scale(2)
                    out_gate(2)

            norm(0)
            dve.wait_ge(s_mod, 2)
            link(v.tensor_tensor(modT[:, 0:16], ps[:, 6, 0:16], col("b_mod")[:, 0:16], ALU.add))
            norm_scale(0)
            phase_end(dve, 2)
            ffn(0)
            phase_end(dve, 3)
            norm(1)
            phase_end(dve, 4)
            dve.wait_ge(s_fp, 1)
            v.tensor_scalar(fA, ps[0:8, 5, :], bf[:, 0:1], -1.0, ALU.add, ALU.mult).then_inc(s_f1, 1)
            v.memset(FL, 0.0)
            v.memset(FR, 0.0).then_inc(s_fl, 1)
            dve.wait_ge(s_f1, 2)
            link(v.scalar_tensor_tensor(out=fA, in0=fA, scalar=0.0, in1=fB, op0=ALU.max, op1=ALU.add))
            link(v.memset(fB, 1.0))
            link(v.tensor_tensor_scan(Fc, fB, fA, 0.0, ALU.mult, ALU.add))
            for lo in (0, HD):
                v.memset(FL[lo + 32:lo + 40, :], 1.0)
                v.memset(FR[lo:lo + 8, :], 1.0)
            phase_end(dve, 5)

            def forget_rows(h, lo):
                v.tensor_scalar(FL[lo:lo + 8, :], Fc, ident[0:8, bass.ds(h, 1)], -1.0, ALU.mult, ALU.mult)
                v.tensor_scalar(FR[lo + 32:lo + 40, :], Fc, ident[0:8, bass.ds(h, 1)], None, ALU.mult).then_inc(s_fm, 1)

            def keys_in(pr):
                dve.wait_ge(s_qkv, pr * 3 + 2)
                v.tensor_copy(kT, ps[:, 6, :]).then_inc(s_kvc, 1)

            def values_in(pr):
                dve.wait_ge(s_qkv, pr * 3 + 3)
                v.tensor_copy(vt.rearrange("p t n -> p (t n)"), ps[:, 7, :]).then_inc(s_kvc, 1)

            def qk_rstd(i, m):
                b = buf1[:, m * 512:(m + 1) * 512]
                dve.wait_ge(s_qstd, 2 * i + m + 1)
                v.reciprocal(b, b).then_inc(s_qr, 1)

            def qk_norm(i, m):
                dst, g = ((qT, gqs[:, :]), (kT, col("g_k")))[m]
                dve.wait_ge(s_qr, 2 * i + m + 1)
                v.scalar_tensor_tensor(out=dst, in0=dst, scalar=g[:, bass.ds(i, 1)],
                                       in1=buf1[:, m * 512:(m + 1) * 512], op0=ALU.mult, op1=ALU.mult).then_inc(s_qn, 1)

            at = steps[0]

            def stick_pair(i, last_pair):
                for hh in range(2):
                    h = i * 2 + hh
                    k = at + i * 4 + 2 * hh
                    dve.wait_ge(s_sp, h + 1)
                    v.scalar_tensor_tensor(out=buf1[:, 0:768].rearrange("p (b n) -> p b n", b=2), in0=ps[:, 0:2, 0:384],
                                           scalar=0.0, in1=buf1[:, 0:768].rearrange("p (b n) -> p b n", b=2),
                                           op0=ALU.max, op1=ALU.add)
                    v.scalar_tensor_tensor(out=buf1[:, 768:TRI], in0=ps[:, 2, :], scalar=0.0, in1=buf1[:, 768:TRI],
                                           op0=ALU.max, op1=ALU.add).then_inc(s_vec, 1)
                    dve.wait_ge(s_vec, k + 1)
                    v.tensor_tensor_scan(buf2[:, ::-1], const("resets")[:, ::-1], buf1[:, ::-1], 0.0, ALU.mult, ALU.add)\
                        .then_inc(s_vec, 1)
                    dve.wait_ge(s_vec, k + 2)
                    v.tensor_tensor(buf1[:, 0:768].rearrange("p (b n) -> p b n", b=2), ps[:, 0:2, 0:384],
                                    buf2[:, 0:768].rearrange("p (b n) -> p b n", b=2), ALU.subtract)
                    v.tensor_tensor(buf1[:, 768:TRI], ps[:, 2, :], buf2[:, 768:TRI], ALU.subtract).then_inc(s_zz, 1)
                    if hh == 0:
                        values_in(i)
                    else:
                        keys_in(i + 1)
                    dve.wait_ge(s_pt, h + 1)
                    v.tensor_tensor(PT[:, 0:4, :], ps[:, 3, :].rearrange("p (b q) -> p b q", b=4),
                                    const("strict_t").unsqueeze(1).to_broadcast([P, 4, P]), ALU.mult).then_inc(s_ptc, 1)
                    if hh == 1 and last_pair:
                        for m in range(2):
                            qk_rstd(0, m)
                            qk_norm(0, m)
                    dve.wait_ge(s_pv, h + 1)
                    v.tensor_copy(oT[hh * HD:(hh + 1) * HD, bass.ds(i, 1), :], ps[0:HD, 6:7, :]).then_inc(s_o, 1)

            def forget_pair(i, last_pair):
                for hh in range(2):
                    h = i * 2 + hh
                    dve.wait_ge(s_z, h + 9)
                    for t in range(4):
                        n = P * (t + 1)
                        z = ps[:, [0, 0, 1, 2][t], (P if t == 1 else 0):(P if t == 1 else 0) + n]
                        last = v.tensor_reduce(fox_s[:, t:t + 1], z, AX_X, ALU.max, negate=True)
                    last.then_inc(s_mx, 1)
                    dve.wait_ge(s_e, h + 1)
                    v.reciprocal(fox_s[:, 8:12], fox_s[:, 4:8]).then_inc(s_vec, 1)
                    dve.wait_ge(s_vec, at + 16 + i * 2 + hh + 1)
                    for t in range(4):
                        n = P * (t + 1)
                        b = buf2[:, TILE_AT[t]:TILE_AT[t] + n]
                        last = v.tensor_scalar(b, b, fox_s[:, 8 + t:9 + t], None, ALU.mult)
                    last.then_inc(s_p, 1)
                    more = hh == 0 or not last_pair
                    if more:
                        forget_rows(h + 1, (1 - hh) * HD)
                    if hh == 0:
                        values_in(i + 4)
                    elif more:
                        keys_in(i + 5)
                        qk_rstd(i + 1, 0)
                    dve.wait_ge(s_pt, h + 9)
                    v.tensor_copy(PT[:, 0:4, :].rearrange("p b q -> p (b q)"), ps[:, 3, :]).then_inc(s_ptc, 1)
                    if hh == 1 and more:
                        qk_norm(i + 1, 0)
                        qk_rstd(i + 1, 1)
                        qk_norm(i + 1, 1)
                    dve.wait_ge(s_pv, h + 9)
                    v.tensor_copy(oT[hh * HD:(hh + 1) * HD, bass.ds(i + 4, 1), :], ps[0:HD, 6:7, :]).then_inc(s_o, 1)
            forget_rows(0, 0)
            keys_in(0)
            with dve.Fori(0, 3) as i:
                stick_pair(i, False)
            stick_pair(3, True)
            with dve.Fori(0, 3) as i:
                forget_pair(i, False)
            forget_pair(3, True)
            steps[0] += 24
            phase_end(dve, 6)
            for k in range(KC):
                dve.wait_ge(s_wo, k + 1)
                v.scalar_tensor_tensor(out=xT[:, k, META:TOK], in0=ps[:, k, :], scalar=gate[1][:, k:k + 1],
                                       in1=xT[:, k, META:TOK], op0=ALU.mult, op1=ALU.add).then_inc(s_xu, 1)
            phase_left(dve, 7)
            norm(2)
            phase_end(dve, 8)
            ffn(1)
            phase_end(dve, 9)
            norm(3)
            phase_end(dve, 10)
            for n in range(0, len(UNITS), 2):
                dve.wait_ge(s_p2, n + 1)
                if n == 0:
                    v.tensor_scalar(unit_dst(n), unit_psum(n), HD ** -0.5, None, ALU.mult).then_inc(s_p2c[0], 1)
                else:
                    v.tensor_copy(unit_dst(n), unit_psum(n)).then_inc(s_p2c[0], 1)
                if n - 1 in GATE_PAIRS:
                    h = GATE_PAIRS[n - 1]
                    dve.wait_ge(s_gex, h // 2 + 1)
                    link(v.tensor_scalar(gexp[:, h:h + 2, :], gexp[:, h:h + 2, :], 1.0, None, ALU.add))
                    link(v.reciprocal(gexp[:, h:h + 2, :], gexp[:, h:h + 2, :]))
                    v.tensor_tensor(gr[:, h:h + 2, :], gr[:, h:h + 2, :], gexp[:, h:h + 2, :], ALU.mult)
            phase_end(dve, 11)
            dve.wait_ge(s_la, 1)
            for p in range(2):
                last = v.tensor_scalar(halves(Sc[:, p, :]), ps[:, 2 * p:2 * p + 2, 0:264], col("gla_b_a_2", p), -1.0,
                                       ALU.add, ALU.mult)
            last.then_inc(s_dt, 1)
            v.tensor_copy(swap[0:32, :], kr[32:64, :])
            link(v.tensor_copy(swap[32:64, :], kr[0:32, :]))
            v.tensor_tensor(kr[0:ROPE, :], kr[0:ROPE, :], const("rope_cos")[0:ROPE, :], ALU.mult)
            link(v.tensor_tensor(swap[0:ROPE, :], swap[0:ROPE, :], const("rope_sin")[0:ROPE, :], ALU.mult))
            v.tensor_tensor(kr[0:ROPE, :], kr[0:ROPE, :], swap[0:ROPE, :], ALU.add)
            dve.wait_ge(s_dsp, 1)
            link(v.scalar_tensor_tensor(out=kd, in0=Sc, scalar=0.0, in1=km, op0=ALU.max, op1=ALU.add))
            for p in range(2):
                last = v.tensor_tensor_scan(Sc[:, p, :], const("chunk_resets"), kd[:, p, :], 0.0, ALU.mult, ALU.add)
            last.then_inc(s_S, 1)
            dve.wait_ge(s_S, 1)
            for p in range(2):
                v.tensor_scalar(kd[:, p, 0:META], Sc[:, p, 0:META], Sc[:, p, META - 1:META], None, ALU.subtract)
                ends = Sc[:, p, META - 1 + CHUNK::CHUNK].unsqueeze(2).to_broadcast([P, N_CHUNK, CHUNK])
                last = v.tensor_tensor(kd[:, p, META:].rearrange("p (n t) -> p n t", t=CHUNK),
                                       Sc[:, p, META:].rearrange("p (n t) -> p n t", t=CHUNK), ends, ALU.subtract)
            last.then_inc(s_S, 1)
            dve.wait_ge(s_dx, 1)
            v.tensor_tensor(km, km, gk, ALU.mult)
            dve.wait_ge(s_dx, 3)
            v.tensor_tensor(gq, gq, eb[:, :, :], ALU.mult)
            dve.wait_ge(s_dx, 4)
            v.tensor_tensor(kd, kd, gk, ALU.mult).then_inc(s_kd, 1)
            dve.wait_ge(s_lstd, 1)
            v.reciprocal(tmp[:, 1, 0:SEQ], tmp[:, 1, 0:SEQ])
            link(v.reciprocal(tmp[:, 0, :], tmp[:, 0, :]))
            for k in range(2):
                v.scalar_tensor_tensor(out=ql[:, k, :], in0=ql[:, k, :], scalar=col("mla_q_norm_2", k), in1=tmp[:, 1, 0:SEQ],
                                       op0=ALU.mult, op1=ALU.mult)
            v.scalar_tensor_tensor(out=kv, in0=kv, scalar=col("mla_kv_norm_2", 0), in1=tmp[:, 0, :],
                                   op0=ALU.mult, op1=ALU.mult)
            link(v.memset(states[:, :, 0, :], 0.0))
            for n in range(N_CHUNK):
                dve.wait_ge(s_U, n + 1)
                for p in range(2):
                    for g in range(2):
                        lo = g * HD
                        last = v.scalar_tensor_tensor(out=states[lo:lo + HD, p, n + 1, :], in0=states[lo:lo + HD, p, n, :],
                                                      scalar=glst[lo:lo + HD, 9 * p + n:9 * p + n + 1],
                                                      in1=ps[lo:lo + HD, 4 + n % 4, p * 256 + g * P:p * 256 + (g + 1) * P],
                                                      op0=ALU.mult, op1=ALU.add)
                last.then_inc(s_st, 1)
                dve.wait_ge(s_st, n + 1)
            phase_end(dve, 12)

            def gla_mask(h):
                dve.wait_ge(s_at2, h + 1)
                v.tensor_tensor(attS, ps[:, 0, :].rearrange("p (b c) -> p b c", b=4),
                                const("chunk_causal").unsqueeze(1).to_broadcast([P, 4, P]), ALU.mult).then_inc(s_atm, 1)
            gla_mask(0)
            for h in range(GH):
                if h + 1 < GH:
                    gla_mask(h + 1)
                dve.wait_ge(s_gstd, h + 1)
                link(v.reciprocal(orst, orst))
                link(v.tensor_tensor(sil, gr[:, h, :], orst, ALU.mult))
                v.scalar_tensor_tensor(out=o2[:, h, :], in0=ps[:, 1 + 2 * (h % 2), :], scalar=col("gla_out_norm_2", h), in1=sil,
                                       op0=ALU.mult, op1=ALU.mult).then_inc(s_gf, 1)
            phase_end(dve, 13)
            NU = 0
            for h in range(GH):
                for kind in range(3):
                    b = 2 * (NU % 3)
                    dve.wait_ge(s_mz, NU + 1)
                    if kind == 0:
                        v.tensor_scalar(qn[:, h, :], ps[:, b, :], MLA_SCALE, None, ALU.mult).then_inc(s_mb, 1)
                    elif kind == 1:
                        cos, sin = (const(n)[0:ROPE, META:TOK] for n in ("rope_cos", "rope_sin"))
                        v.tensor_scalar(swap[0:32, 0:SEQ], ps[32:64, b, :], MLA_SCALE, None, ALU.mult)
                        v.tensor_scalar(swap[32:64, 0:SEQ], ps[0:32, b, :], MLA_SCALE, None, ALU.mult)
                        link(v.scalar_tensor_tensor(out=qr[:, h, :], in0=ps[0:ROPE, b, :], scalar=MLA_SCALE, in1=cos,
                                                    op0=ALU.mult, op1=ALU.mult))
                        link(v.tensor_tensor(swap[0:ROPE, 0:SEQ], swap[0:ROPE, 0:SEQ], sin, ALU.mult))
                        v.tensor_tensor(qr[:, h, :], qr[:, h, :], swap[0:ROPE, 0:SEQ], ALU.add).then_inc(s_mb, 1)
                        dve.wait_ge(s_mb, NU + 1)
                    else:
                        v.tensor_copy(halves(kn[:, h, :]), ps[:, b:b + 2, 0:264]).then_inc(s_mb, 1)
                    NU += 1
            phase_end(dve, 14)

            def mla_max(un):
                t = un % NT
                dve.wait_ge(s_mz, NU + un + 1)
                z = ps[0:CHUNK, 2 * (un % 2) + 1, P * t + CHUNK:P * (t + 1)]
                link(v.tensor_scalar(z, z, -1e30, None, ALU.add))
                v.tensor_reduce(glst[:, 20 + un % 2:21 + un % 2], mla_z(un), AX_X, ALU.max, negate=True).then_inc(s_mb, 1)

            def mla_probs(un):
                dve.wait_ge(s_me, un + 1)
                link(v.reciprocal(glst[:, 24 + un % 2:25 + un % 2], glst[:, 22 + un % 2:23 + un % 2]))
                n = META + P * (un % NT + 1)
                v.tensor_scalar(PB[un % 2][:, 0:n], PB[un % 2][:, 0:n], glst[:, 24 + un % 2:25 + un % 2], None, ALU.mult).then_inc(s_mp, 1)
            mla_max(0)
            mla_max(1)
            mla_probs(0)
            for un in range(GH * NT):
                h, t = un // NT, un % NT
                if un + 1 < GH * NT:
                    mla_probs(un + 1)
                if un + 2 < GH * NT:
                    mla_max(un + 2)
                dve.wait_ge(s_mpv, un + 1)
                v.tensor_copy(o2[:, 4 + h, t * P:(t + 1) * P], ps[:, 6 + un % 2, 0:P]).then_inc(s_mo, 1)
            phase_end(dve, 15)
            for t in range(NT):
                b = 4 * (t % 2)
                dve.wait_ge(s_xrc, t + 1)
                dve.wait_ge(s_xr, 2 * t + 2)
                v.tensor_tensor(h2[:, t, :].rearrange("p (b n) -> p b n", b=2), ps[:, b + 2:b + 4, :],
                                h2[:, t, :].rearrange("p (b n) -> p b n", b=2), ALU.add).then_inc(s_h2, 1)
                dve.wait_ge(s_h2, t + 1)
                row_norm(t)
                if t == 0:
                    dve.wait_ge(s_row, 16)
                v.scalar_tensor_tensor(out=u2[:, t, :], in0=h2[:, t, :], scalar=glst[:, 30:31], in1=gain_row,
                                       op0=ALU.mult, op1=ALU.mult).then_inc(s_un, 1)
                dve.wait_ge(s_un, t + 1)
            phase_end(dve, 16)
            for k in range(KC):
                dve.wait_ge(s_ut, k + 1)
                v.tensor_copy(uT[:, k, :], ps[:, k, :]).then_inc(s_utc, 1)

            dve.wait_ge(s_lg, 1)
            link(v.tensor_tensor(lg, ps[:, 0, 0:NT * 72].rearrange("p (t n) -> p t n", t=NT),
                                 bias_row.unsqueeze(1).to_broadcast([P, NT, 72]), ALU.add))
            glog, elog = lg[:, :, 0:NG], lg[:, :, NG:72]
            iota8 = const("iota8").unsqueeze(1).to_broadcast([P, NT, 8])

            def wide(ap):
                return ap.unsqueeze(2).to_broadcast([P, NT, 8])

            def best(src, top, hot):
                link(v.tensor_reduce(top, src, AX_X, ALU.max))
                link(v.tensor_tensor(t8, src, wide(top), ALU.is_equal))
                link(v.tensor_scalar(t8, t8, -16.0, 16.0, ALU.mult, ALU.add))
                link(v.tensor_tensor(t8, t8, iota8, ALU.add))
                link(v.tensor_reduce(t1, t8, AX_X, ALU.min))
                link(v.tensor_tensor(hot, iota8, wide(t1), ALU.is_equal))
            best(glog, gtop, ghot)
            link(v.tensor_tensor(rx[:, 0:NT * NG].rearrange("p (t n) -> p t n", t=NT), glog, wide(gtop), ALU.subtract))
            link(v.tensor_tensor(pick, elog.rearrange("p t (g e) -> p t g e", g=NG),
                                 ghot.unsqueeze(3).to_broadcast([P, NT, NG, 8]), ALU.mult))
            link(v.tensor_reduce(el, pick.rearrange("p t g e -> p t e g"), AX_X, ALU.add))
            best(el, top1, hot1)
            link(v.scalar_tensor_tensor(out=el, in0=hot1, scalar=-1e30, in1=el, op0=ALU.mult, op1=ALU.add))
            best(el, top2, hot2)
            v.tensor_tensor(rx[:, NT * NG:NT * NG + NT], top2, top1, ALU.subtract).then_inc(s_rx, 1)
            for k, hot in enumerate((hot1, hot2)):
                link(v.tensor_tensor(Mk[k].rearrange("p t (g e) -> p t g e", g=NG), ghot.unsqueeze(3).to_broadcast([P, NT, NG, 8]),
                                     hot.unsqueeze(2).to_broadcast([P, NT, NG, 8]), ALU.mult))
            v.tensor_tensor(Mh, Mk[0], Mk[1], ALU.add).then_inc(s_M, 1)
            dve.wait_ge(s_rx, 2)
            link(v.tensor_reduce(gsum, rx[:, 0:NT * NG].rearrange("p (t n) -> p t n", t=NT), AX_X, ALU.add))
            e2 = rx[:, NT * NG:NT * NG + NT]
            link(v.scalar_tensor_tensor(out=gsum, in0=e2, scalar=1.0, in1=gsum, op0=ALU.add, op1=ALU.mult))
            link(v.reciprocal(gates[:, :, 0], gsum))
            v.tensor_tensor(gates[:, :, 1], gates[:, :, 0], e2, ALU.mult)
            v.memset(xs[0], 0.0)
            v.memset(xs[1], 0.0)
            dve.wait_ge(s_rk, 1)
            link(v.tensor_copy(cnt, ps[:, 5, 0:NE]))
            link(v.tensor_scalar(nblk, cnt, 0.0, None, ALU.is_gt))
            for m in range(1, SEQ // CAP):
                link(v.scalar_tensor_tensor(out=nblk, in0=cnt, scalar=float(CAP * m), in1=nblk, op0=ALU.is_gt, op1=ALU.add))
            link(v.tensor_tensor_scan(blk_end, ones[:, 0:NE], nblk, 0.0, ALU.mult, ALU.add))
            link(v.tensor_scalar(cnt, blk_end, const("block_no"), None, ALU.is_le))
            link(v.tensor_reduce(expert_col, cnt, AX_X, ALU.add))
            v.tensor_scalar(expert_col, expert_col, float(NE - 1), None, ALU.min).then_inc(s_be, 1)
            link(v.tensor_scalar(ge[0:1, 0, 0:TAB // 2], const("block_first")[0:1, 0:TAB // 2], 2.0 / CAP, 1.0, ALU.mult, ALU.add))
            link(v.tensor_scalar(ge[0:1, 0, 0:TAB // 2], ge[0:1, 0, 0:TAB // 2], blk_end[0:1, NE - 1:NE], None, ALU.is_le))
            link(v.tensor_reduce(t2[0:1, 0:1], ge[0:1, 0, 0:TAB // 2], AX_X, ALU.add))
            v.tensor_copy(pairs_ix[0:1, 0:1], t2[0:1, 0:1])
            v.tensor_scalar(pairs_ix[0:1, 1:2], t2[0:1, 0:1], -1.0, None, ALU.add).then_inc(s_bet, 1)
            dve.wait_ge(s_tb, 1)
            v.tensor_copy(expert_ix[:, :], ps[0:1, 4, 0:P]).then_inc(s_bet, 1)
            link(v.tensor_tensor(nblk, blk_end, nblk, ALU.subtract))
            dve.wait_ge(s_rk, 2)
            link(v.scalar_tensor_tensor(out=slot, in0=nblk.unsqueeze(1).to_broadcast([P, NT, NE]), scalar=float(CAP),
                                        in1=ps[:, 1, 0:NT * NE].rearrange("p (t e) -> p t e", t=NT), op0=ALU.mult, op1=ALU.add))
            for k in range(2):
                link(v.tensor_tensor(Mk[k], Mk[k], slot, ALU.mult))
                link(v.tensor_reduce(pos[:, :, k], Mk[k], AX_X, ALU.add))
            pos8 = pos.rearrange("p t k -> p (t k)")
            link(v.tensor_tensor(ge, pos8.unsqueeze(2).to_broadcast([P, 2 * NT, TAB + 1]),
                                 const("block_first").unsqueeze(1).to_broadcast([P, 2 * NT, TAB + 1]), ALU.is_ge))
            v.tensor_tensor(block_hot, ge[:, :, 0:TAB], ge[:, :, 1:TAB + 1], ALU.subtract)
            link(v.tensor_reduce(t2, ge, AX_X, ALU.add))
            link(v.tensor_scalar(t2, t2, -1.0, -float(CAP), ALU.add, ALU.mult))
            link(v.tensor_tensor(t2, pos8, t2, ALU.add))
            link(v.tensor_tensor(slot_hot[0], t2.unsqueeze(2).to_broadcast([P, 2 * NT, CAP]),
                                 const("iota_cap").unsqueeze(1).to_broadcast([P, 2 * NT, CAP]), ALU.is_equal))
            link(v.tensor_tensor(slot_hot[1], slot_hot[0], const("asg1").unsqueeze(2).to_broadcast([P, 2 * NT, CAP]), ALU.mult))
            v.tensor_tensor(slot_hot[0], slot_hot[0], const("tok1").unsqueeze(2).to_broadcast([P, 2 * NT, CAP]),
                            ALU.mult).then_inc(s_pos, 1)
            dve.wait_ge(s_tb, 2)
            for w, dst in enumerate((tok_ix, asg_ix)):
                tab = slot[0:CAP, :, :].rearrange("p t e -> p (t e)")[:, 0:TAB]
                link(v.tensor_scalar(tab, ps[0:CAP, 2 + w, 0:TAB], 0.0, FAR, ALU.is_equal, ALU.mult))
                link(v.scalar_tensor_tensor(out=dst[:, :], in0=ps[0:CAP, 2 + w, 0:TAB], scalar=-1.0, in1=tab,
                                            op0=ALU.add, op1=ALU.add))
            phase_end(dve, 17)
            n_more = dve.value_load(pairs_ix[0:1, 1:2], min_val=1, max_val=MAX_PAIRS - 1)
            phase_end(dve, 18)
            at = steps[0]

            def hidden(j, n, done):
                dve.wait_ge(s_eg, n)
                v.tensor_scalar(sg[j], sg[j], 1.0, None, ALU.add).then_inc(s_vec, 1)
                dve.wait_ge(s_vec, done + 1)
                v.reciprocal(sg[j], sg[j]).then_inc(s_vec, 1)
                dve.wait_ge(s_vec, done + 2)
                v.tensor_tensor(sg[j], ps[0:CAP, j, :], sg[j], ALU.mult).then_inc(s_vec, 1)
                dve.wait_ge(s_vec, done + 3)
                dve.wait_ge(s_mu, n + 2)
                v.tensor_tensor(hrow[j], ps[CAP:2 * CAP, j, :], sg[j], ALU.mult).then_inc(s_ha, 1)

            def hidden_in(j, n):
                dve.wait_ge(s_ta, n)
                v.tensor_copy(hid[j].rearrange("p c s -> p (c s)"), ps[:, 6 + j, 0:4 * CAP]).then_inc(s_hd, 1)
            hidden(0, 1, at)
            with dve.Fori(0, n_more) as i:
                hidden_in(0, i * 2 + 1)
                hidden(1, i * 2 + 2, i * 6 + (at + 3))
                hidden_in(1, i * 2 + 2)
                hidden(0, i * 2 + 3, i * 6 + (at + 6))
            before = dve.snap(n_more * 2)
            hidden_in(0, before + 1)
            hidden(1, before + 2, dve.snap(n_more * 6 + (at + 3)))
            hidden_in(1, before + 2)
            phase_end(dve, 19)
            phase_end(dve, 20)
            phase_end(dve, 21)
            steps[0] = 0
            vec_sem[0] = s_vec2

            def final_row(t):
                dve.wait_ge(s_fst, t + 1)
                link(v.reciprocal(glst[:, 40 + t:41 + t], glst[:, 36 + t:37 + t]))
                if t == 0:
                    dve.wait_ge(s_row, 32)
                v.scalar_tensor_tensor(out=h2[:, t, :], in0=h2[:, t, :], scalar=glst[:, 40 + t:41 + t], in1=gain_row,
                                       op0=ALU.mult, op1=ALU.mult).then_inc(s_fin, 1)
            for t in range(NT):
                dve.wait_ge(s_y2[t], 16)
                link(v.scalar_tensor_tensor(out=h2[:, t, :], in0=y2[t][:, 0, :], scalar=gates[:, t, 0:1], in1=h2[:, t, :],
                                            op0=ALU.mult, op1=ALU.add))
                v.scalar_tensor_tensor(out=h2[:, t, :], in0=y2[t][:, 1, :], scalar=gates[:, t, 1:2], in1=h2[:, t, :],
                                       op0=ALU.mult, op1=ALU.add).then_inc(s_y2f, 1)
                if t >= 1:
                    final_row(t - 1)
            final_row(NT - 1)
            phase_end(dve, 22)

        @block.gpsimd
        def _(pool):
            for n in range(1, 19):
                phase_end(pool, n)
            n_more = pool.value_load(pairs_ix[0:1, 1:2], min_val=2, max_val=MAX_PAIRS - 1)

            def settle(cell=0):
                return pool.tensor_tensor(spare[:, cell:cell + 1], spare[:, 2:3], spare[:, 2:3], ALU.add)

            def gather(j, b, copies):
                pool.tensor_copy(tcol[j][:, :], tok_ix[:, bass.ds(b, 1)]).then_inc(s_pix, 1)
                pool.wait_ge(s_pix, copies)
                settle()
                pool.indirect_dma_start(xs[j], None, u_dram, bass.IndirectOffsetOnAxis(tcol[j][:, :], 0),
                                        bounds_check=SEQ - 1, oob_is_err=False).then_inc(s_gat[j], 16)
            pool.memset(spare[:, :], 0.0).then_inc(s_pix, 1)
            pool.wait_ge(s_pix, 1)
            pool.wait_ge(s_ud, 16 * NT)
            gather(0, 0, 2)
            gather(1, 1, 3)
            def scatter(j, b, copies, n, earlier):
                if earlier is not None:
                    pool.wait_ge(s_scat[j], earlier)
                    settle(1).then_inc(s_ysf, 1)
                pool.tensor_copy(acol[j][:, :], asg_ix[:, bass.ds(b, 1)]).then_inc(s_pix, 1)
                pool.wait_ge(s_pix, copies)
                pool.wait_ge(s_yc, n)
                settle()
                pool.indirect_dma_start(y_dram, bass.IndirectOffsetOnAxis(acol[j][:, :], 0), ys[j], None,
                                        bounds_check=N_ASG - 1, oob_is_err=False).then_inc(s_scat[j], 16)

            for j in range(2):
                pool.wait_ge(s_xt, j + 1)
                gather(j, j + 2, j + 4)
            for j in range(2):
                pool.wait_ge(s_xt, j + 3)
                gather(j, j + 4, 2 * j + 6)
                scatter(j, j, 2 * j + 7, j + 1, None)
            with pool.Fori(1, n_more) as i:
                for j in range(2):
                    pool.wait_ge(s_xt, i * 2 + (j + 3))
                    gather(j, i * 2 + (j + 4), i * 4 + (2 * j + 6))
                    scatter(j, i * 2 + j, i * 4 + (2 * j + 7), i * 2 + (j + 1), i * 16)
            before = pool.snap(n_more * 2)
            for j in range(2):
                scatter(j, before + j, pool.snap(n_more * 4 + (j + 6)), pool.snap(n_more * 2 + (j + 1)), pool.snap(n_more * 16))
            for j in range(2):
                pool.wait_ge(s_gat[j], pool.snap(n_more * 16 + 32))
                pool.wait_ge(s_scat[j], pool.snap(n_more * 16 + 16))
            settle(3)
            for n in range(19, 23):
                phase_end(pool, n)


_INS = ["x", "w_mod", "w1_gate", "w1_up", "w1_down", "w_in", "b_f", "w_o", "w2_gate", "w2_up", "w2_down", "meta_tokens_2",
        "w_in_2", "gla_w_a2_2", "mla_w_qb_2", "mla_w_kvb_2", "w_out_2", "ffn_norm_2", "router_group_w_2", "router_expert_w_2",
        "expert_w_gate_2", "expert_w_up_2", "expert_w_down_2"]


def kernel(**inputs):
    import concourse.bacc as _bacc
    from concourse.bass_utils import run_bass_kernel_spmd as _run

    nc = _bacc.Bacc("TRN2", target_bir_lowering=False, num_devices=1)
    arrays = {name: np.ascontiguousarray(inputs[name]) for name in _INS}
    arrays["cols"] = np.ascontiguousarray(np.concatenate(
        [np.asarray(inputs[name]).reshape(-1, P) for name in COLS], axis=0).T)
    arrays["router_bias"] = np.concatenate([inputs["router_group_b_2"], inputs["router_expert_b_2"]], axis=1)
    arrays["final_norm_2"] = np.ascontiguousarray(inputs["final_norm_2"]).reshape(1, D)
    arrays["const"] = CONST_ARRAY
    args = {name: nc.dram_tensor(f"in_{name}", x.shape, mybir.dt.from_np(x.dtype), kind="ExternalInput").ap()
            for name, x in arrays.items()}
    out = nc.dram_tensor("out_0", (1, SEQ, D), F32, kind="ExternalOutput").ap()
    build(nc, args, out)
    r = _run(nc, [{f"in_{name}": x for name, x in arrays.items()}], core_ids=[0])
    return r.results[0]["out_0"]
```
